# Optimizing a Trainium2 kernel written in Bass

```python
import jax, jax.numpy as jnp
from jax import lax
import numpy as np

D_MODEL = 2048
BATCH = 1
SEQ = 256
DEPTH = 1

N_HEADS = 16
HEAD_DIM = 128
D_ATTN = N_HEADS * HEAD_DIM
MOBA_BLOCK = 256
MOBA_TOPK = 3
Q_CHUNK = 16
ROPE_THETA = 500000.0
ROT_DIM = HEAD_DIM // 4
D_RNN = 2048
N_RNN_BLOCKS = 16
RNN_BLOCK = D_RNN // N_RNN_BLOCKS
CONV_WIDTH = 4
LRU_C = 8.0
MEM_LEN = 256
MEM_HEADS = 4
MEM_HEAD_DIM = 128
D_MEM = MEM_HEADS * MEM_HEAD_DIM
D_FF = -(-8 * D_MODEL // (3 * 256)) * 256
IN_WIDTH = 2 * D_RNN + 3 * D_ATTN + 2 * D_MODEL
RMS_EPS = 1e-6
NEG_INF = -1e30

kernel_name = "hawk_moba_gated_hybrid"

def rmsnorm(x, g):
    xf = x.astype(jnp.float32)
    y = xf * lax.rsqrt(jnp.mean(xf * xf, axis=-1, keepdims=True) + RMS_EPS)
    return (y * g.astype(jnp.float32)).astype(x.dtype)

def partial_rope(x, positions):
    half = ROT_DIM // 2
    inv_freq = jnp.power(ROPE_THETA, -jnp.arange(half, dtype=jnp.float32) / half)
    ang = positions.astype(jnp.float32)[..., None] * inv_freq
    cos = jnp.cos(ang)[:, :, None, :]
    sin = jnp.sin(ang)[:, :, None, :]
    xf = x.astype(jnp.float32)
    x1 = xf[..., :half]
    x2 = xf[..., half:ROT_DIM]
    out = jnp.concatenate([x1 * cos - x2 * sin, x2 * cos + x1 * sin, xf[..., ROT_DIM:]], axis=-1)
    return out.astype(x.dtype)

def causal_depthwise_conv(x, w, b):
    y = lax.conv_general_dilated(
        x, w[:, None, :].astype(x.dtype), window_strides=(1,),
        padding=[(CONV_WIDTH - 1, 0)], dimension_numbers=("NWC", "WIO", "NWC"),
        feature_group_count=x.shape[-1])
    return y + b.astype(x.dtype)

def rg_lru(x, w_a, b_a, w_i, b_i, lam):
    B, S, _ = x.shape
    xb = x.reshape(B, S, N_RNN_BLOCKS, RNN_BLOCK)
    r = jax.nn.sigmoid(jnp.einsum('bsnk,nkj->bsnj', xb, w_a, preferred_element_type=jnp.float32)
                       .reshape(B, S, D_RNN) + b_a.astype(jnp.float32))
    i = jax.nn.sigmoid(jnp.einsum('bsnk,nkj->bsnj', xb, w_i, preferred_element_type=jnp.float32)
                       .reshape(B, S, D_RNN) + b_i.astype(jnp.float32))
    log_a = -LRU_C * r * jax.nn.softplus(-lam.astype(jnp.float32))
    a = jnp.exp(log_a)
    u = jnp.sqrt(-jnp.expm1(2.0 * log_a)) * (i * x.astype(jnp.float32))

    def combine(left, right):
        a1, b1 = left
        a2, b2 = right
        return a1 * a2, a2 * b1 + b2

    _, h = lax.associative_scan(combine, (a, u), axis=1)
    return h.astype(x.dtype)

def moba_attention(q, k, v):
    B, H, S, dh = q.shape
    nb = -(-S // MOBA_BLOCK)
    s_pad = nb * MOBA_BLOCK
    k_sel = min(MOBA_TOPK, nb)
    scale = dh ** -0.5
    pad = ((0, 0), (0, 0), (0, s_pad - S), (0, 0))
    kp = jnp.pad(k, pad)
    vp = jnp.pad(v, pad)
    k_blocks = kp.reshape(B, H, nb, MOBA_BLOCK, dh)
    v_blocks = vp.reshape(B, H, nb, MOBA_BLOCK, dh)
    k_mean = jnp.mean(k_blocks.astype(jnp.float32), axis=3)

    q_blk = jnp.arange(S) // MOBA_BLOCK
    gate = jnp.einsum('bhsd,bhnd->bhsn', q.astype(jnp.float32), k_mean)
    past = jnp.arange(nb)[None, :] < q_blk[:, None]
    gate = jnp.where(past, gate, -jnp.inf)
    _, sel_idx = lax.top_k(gate, k_sel)

    bi = jnp.arange(B)[:, None, None, None]
    hi = jnp.arange(H)[None, :, None, None]
    sel_width = k_sel * MOBA_BLOCK

    def chunk(c):
        start = c * Q_CHUNK
        qc = lax.dynamic_slice_in_dim(q, start, Q_CHUNK, axis=2)
        idx = lax.dynamic_slice_in_dim(sel_idx, start, Q_CHUNK, axis=2)
        pos = start + jnp.arange(Q_CHUNK)
        n_past = pos // MOBA_BLOCK
        valid = jnp.arange(k_sel)[None, :] < n_past[:, None]
        kg = k_blocks[bi, hi, idx]
        vg = v_blocks[bi, hi, idx]
        s_sel = jnp.einsum('bhqd,bhqnkd->bhqnk', qc, kg, preferred_element_type=jnp.float32) * scale
        s_sel = jnp.where(valid[None, None, :, :, None], s_sel, NEG_INF)
        own_start = (start // MOBA_BLOCK) * MOBA_BLOCK
        ko = lax.dynamic_slice_in_dim(kp, own_start, MOBA_BLOCK, axis=2)
        vo = lax.dynamic_slice_in_dim(vp, own_start, MOBA_BLOCK, axis=2)
        s_own = jnp.einsum('bhqd,bhkd->bhqk', qc, ko, preferred_element_type=jnp.float32) * scale
        causal = (own_start + jnp.arange(MOBA_BLOCK))[None, :] <= pos[:, None]
        s_own = jnp.where(causal[None, None], s_own, NEG_INF)
        s_all = jnp.concatenate([s_sel.reshape(B, H, Q_CHUNK, sel_width), s_own], axis=-1)
        p = jax.nn.softmax(s_all, axis=-1)
        p_sel = p[..., :sel_width].reshape(B, H, Q_CHUNK, k_sel, MOBA_BLOCK).astype(v.dtype)
        p_own = p[..., sel_width:].astype(v.dtype)
        o = (jnp.einsum('bhqnk,bhqnkd->bhqd', p_sel, vg, preferred_element_type=jnp.float32)
             + jnp.einsum('bhqk,bhkd->bhqd', p_own, vo, preferred_element_type=jnp.float32))
        return o.astype(q.dtype)

    out = lax.map(chunk, jnp.arange(S // Q_CHUNK))
    return out.transpose(1, 2, 0, 3, 4).reshape(B, H, S, dh)

def hybrid_mixer(h, positions, w_in, conv_w, conv_b, w_a, b_a, w_i, b_i, lam,
                 w_rnn_proj, w_attn_proj, w_mix_out):
    B, S, _ = h.shape
    proj = h @ w_in
    o0 = 0
    xr = proj[..., o0:o0 + D_RNN]; o0 += D_RNN
    yr = proj[..., o0:o0 + D_RNN]; o0 += D_RNN
    q = proj[..., o0:o0 + D_ATTN]; o0 += D_ATTN
    k = proj[..., o0:o0 + D_ATTN]; o0 += D_ATTN
    v = proj[..., o0:o0 + D_ATTN]; o0 += D_ATTN
    g_rnn = proj[..., o0:o0 + D_MODEL]; o0 += D_MODEL
    g_attn = proj[..., o0:o0 + D_MODEL]

    hr = rg_lru(causal_depthwise_conv(xr, conv_w, conv_b), w_a, b_a, w_i, b_i, lam)
    rnn_out = (jax.nn.gelu(yr) * hr) @ w_rnn_proj

    q = partial_rope(q.reshape(B, S, N_HEADS, HEAD_DIM), positions).transpose(0, 2, 1, 3)
    k = partial_rope(k.reshape(B, S, N_HEADS, HEAD_DIM), positions).transpose(0, 2, 1, 3)
    v = v.reshape(B, S, N_HEADS, HEAD_DIM).transpose(0, 2, 1, 3)
    o = moba_attention(q, k, v).transpose(0, 2, 1, 3).reshape(B, S, D_ATTN)
    attn_out = o @ w_attn_proj

    merged = jax.nn.sigmoid(g_rnn) * rnn_out + jax.nn.sigmoid(g_attn) * attn_out
    return merged @ w_mix_out

def memory_cross_attention(h, mem_n, w_q, w_kv, w_o):
    B, S, _ = h.shape
    M = mem_n.shape[1]
    q = (h @ w_q).reshape(B, S, MEM_HEADS, MEM_HEAD_DIM)
    kv = mem_n @ w_kv
    k = kv[..., :D_MEM].reshape(B, M, MEM_HEADS, MEM_HEAD_DIM)
    v = kv[..., D_MEM:].reshape(B, M, MEM_HEADS, MEM_HEAD_DIM)
    s = jnp.einsum('bshd,bmhd->bhsm', q, k, preferred_element_type=jnp.float32) * (MEM_HEAD_DIM ** -0.5)
    p = jax.nn.softmax(s, axis=-1).astype(v.dtype)
    o = jnp.einsum('bhsm,bmhd->bshd', p, v)
    return o.reshape(B, S, D_MEM) @ w_o

def swiglu(h, w_gate, w_up, w_down):
    return (jax.nn.silu(h @ w_gate) * (h @ w_up)) @ w_down

def setup_inputs(seed: int = 0) -> dict:
    key = jax.random.key(seed)
    ks = jax.random.split(key, 32)
    f32 = jnp.float32

    def nrm(k, shape, fan_in):
        return jax.random.normal(k, shape, f32) * (fan_in ** -0.5)

    def gain(k, shape):
        return 1.0 + 0.02 * jax.random.normal(k, shape, f32)

    def bias(k, shape):
        return 0.01 * jax.random.normal(k, shape, f32)

    L = DEPTH
    x = jax.random.normal(ks[0], (BATCH, SEQ, D_MODEL), f32)
    mem = jax.random.normal(ks[1], (BATCH, MEM_LEN, D_MODEL), f32)
    offset = jax.random.randint(ks[2], (BATCH, 1), 0, 1024, dtype=jnp.int32)
    positions = (offset + jnp.arange(SEQ, dtype=jnp.int32)[None, :]).astype(jnp.int32)
    a_init = jax.random.uniform(ks[3], (L, D_RNN), f32, 0.9, 0.999)
    lru_lambda = jnp.log(a_init) - jnp.log1p(-a_init)
    return {
        "x": x,
        "mem": mem,
        "positions": positions,
        "norm_mix_g": gain(ks[4], (L, D_MODEL)),
        "w_in": nrm(ks[5], (L, D_MODEL, IN_WIDTH), D_MODEL),
        "conv_w": nrm(ks[6], (L, CONV_WIDTH, D_RNN), CONV_WIDTH),
        "conv_b": bias(ks[7], (L, D_RNN)),
        "lru_w_a": nrm(ks[8], (L, N_RNN_BLOCKS, RNN_BLOCK, RNN_BLOCK), RNN_BLOCK),
        "lru_b_a": bias(ks[9], (L, D_RNN)),
        "lru_w_i": nrm(ks[10], (L, N_RNN_BLOCKS, RNN_BLOCK, RNN_BLOCK), RNN_BLOCK),
        "lru_b_i": bias(ks[11], (L, D_RNN)),
        "lru_lambda": lru_lambda,
        "w_rnn_proj": nrm(ks[12], (L, D_RNN, D_MODEL), D_RNN),
        "w_attn_proj": nrm(ks[13], (L, D_ATTN, D_MODEL), D_ATTN),
        "w_mix_out": nrm(ks[14], (L, D_MODEL, D_MODEL), D_MODEL),
        "norm_xq_g": gain(ks[15], (L, D_MODEL)),
        "norm_mem_g": gain(ks[16], (L, D_MODEL)),
        "w_xq": nrm(ks[17], (L, D_MODEL, D_MEM), D_MODEL),
        "w_xkv": nrm(ks[18], (L, D_MODEL, 2 * D_MEM), D_MODEL),
        "w_xo": nrm(ks[19], (L, D_MEM, D_MODEL), D_MEM),
        "norm_ffn_g": gain(ks[20], (L, D_MODEL)),
        "w_ffn_gate": nrm(ks[21], (L, D_MODEL, D_FF), D_MODEL),
        "w_ffn_up": nrm(ks[22], (L, D_MODEL, D_FF), D_MODEL),
        "w_ffn_down": nrm(ks[23], (L, D_FF, D_MODEL), D_FF),
        "norm_final_g": gain(ks[24], (D_MODEL,)),
    }

def reference(x, mem, positions, norm_mix_g, w_in, conv_w, conv_b, lru_w_a, lru_b_a,
              lru_w_i, lru_b_i, lru_lambda, w_rnn_proj, w_attn_proj, w_mix_out,
              norm_xq_g, norm_mem_g, w_xq, w_xkv, w_xo, norm_ffn_g, w_ffn_gate,
              w_ffn_up, w_ffn_down, norm_final_g):
    for l in range(DEPTH):
        h = rmsnorm(x, norm_mix_g[l])
        x = x + hybrid_mixer(h, positions, w_in[l], conv_w[l], conv_b[l], lru_w_a[l], lru_b_a[l],
                             lru_w_i[l], lru_b_i[l], lru_lambda[l], w_rnn_proj[l],
                             w_attn_proj[l], w_mix_out[l])
        h = rmsnorm(x, norm_xq_g[l])
        mem_n = rmsnorm(mem, norm_mem_g[l])
        x = x + memory_cross_attention(h, mem_n, w_xq[l], w_xkv[l], w_xo[l])
        h = rmsnorm(x, norm_ffn_g[l])
        x = x + swiglu(h, w_ffn_gate[l], w_ffn_up[l], w_ffn_down[l])
    return rmsnorm(x, norm_final_g)


_drawn_inputs = setup_inputs


def setup_inputs(seed=0):
    import zlib

    import numpy as np

    out = dict(_drawn_inputs(seed))
    spreads = {}
    factors = {'norm_mix_g': 7.397,
     'conv_b': 7.219,
     'lru_b_a': 8.0,
     'lru_b_i': 8.0,
     'norm_xq_g': 8.0,
     'norm_mem_g': 8.0,
     'norm_ffn_g': 16.387,
     'norm_final_g': 8.076}
    for name, (base, spread) in spreads.items():
        noise = np.random.default_rng([zlib.crc32(name.encode()), seed]).standard_normal(out[name].shape)
        drawn = base * np.exp(spread * noise) if base else spread * noise
        out[name] = __import__('jax').numpy.asarray(drawn.astype(out[name].dtype))
    for name, factor in factors.items():
        out[name] = (out[name] * factor).astype(out[name].dtype)
    return out
```

```python
import numpy as np
import concourse.bass as bass
from concourse import mybir
from contextlib import ExitStack

F32 = mybir.dt.float32
F32R = mybir.dt.float32r
I32 = mybir.dt.int32
ALU = mybir.AluOpType
ACT = mybir.ActivationFunctionType
AX = mybir.AxisListType.X

P = 128
SEQ, D, F, MEM = 256, 2048, 5632, 256
TT = SEQ // P
GW = 512
KG = D // GW
NB = GW // P
KT = D // P
R = 4
LEAD = 3
CK = 2
CG = KT // CK
EPS = 1e-6
ATT_SCALE = float(P) ** -0.5
FA, FB = 6, 5
ROT = 16
IN_COLS = {"xr": 0, "yr": D, "q": 2 * D, "k": 3 * D, "v": 4 * D, "g_rnn": 5 * D, "g_attn": 6 * D}
GELU_C = 0.7978845608028654
TWO_PI = 6.283185307179586
MAGIC = 12582912.0
PI_PARTS = [6.25, 0.03125, 0.0019340515136718750]
PI_PARTS.append(TWO_PI - sum(PI_PARTS))

STAGES = ["rnn_in", "rnn_out", "attn_in", "attn_out", "mix", "cross", "cross_out", "up_a", "down_a", "up_b", "down_b"]
_CH = [3 * KG * CG, KG * CG, 4 * KG * CG, KG * CG, KG * CG, 3 * CG, KG * 2, 2 * FA * CG, KG * FA * 2, 2 * FB * CG, KG * FB * 2]
_GR = [3 * KG, KG, 4 * KG, KG, KG, 3, KG, 2 * FA, KG, 2 * FB, KG]
CH0 = {s: sum(_CH[:i]) for i, s in enumerate(STAGES)}
GR0 = {s: sum(_GR[:i]) for i, s in enumerate(STAGES)}
CHUNKS = sum(_CH)
CW, CB, BA, BI, LAM = 0, 4, 5, 6, 7


def build(nc, t):
    ctx = ExitStack()
    with ctx:
        sems = {}

        def sem(name):
            if name not in sems:
                sems[name] = ctx.enter_context(nc.semaphore(name))
            return sems[name]

        K1 = 1024
        total = 207 * K1
        ctx.enter_context(nc.sbuf_tensor("arena", [P, total], mybir.dt.uint8))
        arena = nc.sbuf_base - total
        top = [0]

        def region(size):
            top[0] += size
            assert top[0] <= total
            return arena + top[0] - size

        def at(name, offset, shape, dt=F32):
            return nc.alloc_sbuf_tensor_at(name, [P] + shape, dt, offset=offset)

        def new(name, shape, dt=F32):
            size = 4 * int(np.prod(shape))
            return at(name, region((size + 31) // 32 * 32), shape, dt)

        raw = new("w_raw", [R, CK, GW])
        whi = new("w_hi", [R, CK, GW], F32R)
        wlo = new("w_lo", [R, CK, GW], F32R)
        xhi = new("x_hi", [KT, SEQ], F32R)
        xlo = new("x_lo", [KT, SEQ], F32R)
        U, V, G, S = region(32 * K1), region(32 * K1), region(16 * K1), region(16 * K1)
        vhi, vlo = at("v_hi", V, [KT, SEQ], F32R), at("v_lo", V + 16 * K1, [KT, SEQ], F32R)
        inner_hi = at("inner_hi", U, [FA * NB, SEQ], F32R)
        inner_lo = at("inner_lo", V, [FA * NB, SEQ], F32R)
        mhi, mlo = at("merged_hi", U, [KT, SEQ], F32R), at("merged_lo", U + 16 * K1, [KT, SEQ], F32R)
        rtok = at("rnn_tok", U, [TT, GW])
        conv = at("conv_T", U + 4 * K1, [NB, SEQ])
        rgate = at("r_gate", U + 8 * K1, [NB, SEQ])
        igate = at("i_gate", U + 12 * K1, [NB, SEQ])
        den = at("lru_den", U + 16 * K1, [NB, SEQ])
        yT = at("y_T", U + 20 * K1, [NB, SEQ])
        gelu = at("gelu_T", U + 24 * K1, [NB, SEQ])
        root = at("lru_root", U + 28 * K1, [NB, SEQ])
        ktok = at("k_tok", U, [TT, GW])
        qtok = at("q_tok", U + 4 * K1, [TT, GW])
        vtok = at("v_tok", U + 8 * K1, [TT, GW])
        kT = at("k_T", U + 12 * K1, [NB, SEQ])
        qT = at("q_T", U + 16 * K1, [NB, SEQ])
        prob = at("prob", U + 20 * K1, [NB, 3 * P])
        probT = at("prob_T", U + 26 * K1, [NB, 3 * P])
        cprob = at("cross_prob", U + 20 * K1, [TT, NB, MEM])
        gated = at("gated_rnn", G, [TT, D])
        xres = at("x_res", G, [TT, D])
        sig_attn = at("sig_attn", S, [TT, D])
        mem_tok = at("mem_tok", S, [TT, D])
        cprobT = at("cross_prob_T", S, [MEM // P, NB, SEQ])
        chi = at("cross_hi", S + 8 * K1, [NB, SEQ], F32R)
        clo = at("cross_lo", S + 12 * K1, [NB, SEQ], F32R)
        gate_tok = at("gate_tok", S, [TT, GW])
        silu = at("silu_tok", S + 4 * K1, [TT, GW])
        stage = [new("stage0", [TT, GW]), new("stage1", [TT, GW])]
        LW = region(8 * K1)
        lw = [at("lru_w0", LW, [2, NB, P]), at("lru_w1", LW + 4 * K1, [2, NB, P])]
        gain_final = at("gain_final", LW, [D])
        junk = new("junk", [TT, GW])
        xTp = new("conv_in_T", [NB, 4 + SEQ])
        consts = new("consts", [P + 2 * P + ROT])
        ident, mask, inv_freq = consts[:, 0:P], consts[:, P:3 * P], consts[:, 3 * P:3 * P + ROT]
        rows = at("param_rows", U, [2, P])
        params = new("params", [8, KT])
        gains = new("gains", [4, KT])
        neg_ba, half_bi, four_sp = new("neg_b_a", [KT]), new("half_b_i", [KT]), new("four_softplus", [KT])
        pj = [new("block_params0", [8, NB]), new("block_params1", [8, NB])]
        pos_i, pos_f = new("pos_i", [TT], I32), new("pos_f", [TT])
        rope = at("rope_tmp", U + 4 * K1, [6, TT, ROT])
        cos, sin = new("cos", [TT, NB, ROT]), new("sin", [TT, NB, ROT])
        rt = new("rope_products", [4, TT, NB, ROT])
        sp = new("softplus_tmp", [4, KT])
        pw = new("minus_half", [TT])
        ss = {n: new("ss_" + n, [TT, KG]) for n in ("x", "mem", "x1", "x2", "x3")}
        var = {n: new("var_" + n, [TT]) for n in ss}
        rstd = {n: new("rstd_" + n, [TT]) for n in ss}
        hrstd = {n: new("hrstd_" + n, [TT]) for n in ss}
        smax, nmax = new("smax", [TT, NB]), new("nmax", [TT, NB])
        psum_, rsum = new("prob_sum", [TT, NB]), new("prob_rsum", [TT, NB])

        gps = [ctx.enter_context(nc.psum_tensor(f"group{p}", [P, TT, GW], F32)) for p in range(2)]
        side = [ctx.enter_context(nc.psum_tensor(f"side{p}", [P, NB, SEQ], F32)) for p in range(2)]

        raw_full = [sem(f"raw_full{s}") for s in range(R)]
        hi_ready = [sem(f"hi_ready{s}") for s in range(R)]
        w_ready = [sem(f"w_ready{s}") for s in range(R)]
        w_used = [sem(f"w_used{s}") for s in range(R)]
        taken = [sem(f"taken{p}") for p in range(2)]

        START = 1

        def slot_of(n, i=0, per=0):
            return n % R, n // R + i * (per // R)

        def buf_of(g, i=0, per=0):
            return g % 2, g // 2 + i * (per // 2)

        def wait_product(engine, end, i=0, per=0):
            s, used = slot_of(end - 1, i, per)
            engine.wait_ge(w_used[s], START + used + 1)

        def wait_taken(engine, g, i=0, per=0):
            p, before = buf_of(g, i, per)
            engine.wait_ge(taken[p], START + before + 1)

        dram = t

        block = ctx.enter_context(nc.Block())

        @block.sync
        def _(sp_):
            sync = sp_
            for q in range(KG):
                sync.dma_start(xres[:, :, q * GW:(q + 1) * GW],
                               dram["x"][:, q * GW:(q + 1) * GW].rearrange("(t p) n -> p t n", p=P))\
                    .then_inc(sem(f"x_loaded{q}"), 16)

            def load(n, i, per, w, row, col):
                s, before = slot_of(n, i, per)
                sync.wait_ge(w_ready[s], START + before)
                sync.dma_start(raw[:, s], w[row:row + CK * P, bass.ds(col, GW)].rearrange("(k p) n -> p k n", p=P))\
                    .then_inc(raw_full[s], 16)

            def group(n, i, per, w, col, rows_=KT, row0=0):
                for c in range(rows_ // CK):
                    load(n + c, i, per, w, row0 + c * CK * P, col)

            w_in = dram["w_in"]
            with sync.Fori(0, KG // 2) as i:
                for h in range(2):
                    n = CH0["rnn_in"] + h * 3 * CG
                    j = 2 * i + h
                    sync.wait_ge(sem(f"lru_z{h}"), START + i)
                    for a, name in enumerate(("lru_w_a", "lru_w_i")):
                        sync.dma_start(lw[h][:, a], dram[name][bass.ds(j * NB, NB), :, :].rearrange("n k m -> k n m"))\
                            .then_inc(sem(f"lw_full{h}"), 16)
                    for m, name in enumerate(("xr", "yr", "g_rnn")):
                        group(n + m * CG, i, 6 * CG, w_in, IN_COLS[name] + j * GW)
            with sync.Fori(0, KG // 2) as i:
                for h in range(2):
                    group(CH0["rnn_out"] + h * CG, i, 2 * CG, dram["w_rnn_proj"], (2 * i + h) * GW)
            with sync.Fori(0, KG) as j:
                for m, name in enumerate(("k", "q", "v", "g_attn")):
                    group(CH0["attn_in"] + m * CG, j, 4 * CG, w_in, IN_COLS[name] + j * GW)
            for j in range(KG):
                group(CH0["attn_out"] + j * CG, 0, 0, dram["w_attn_proj"], j * GW)
            for j in range(KG):
                group(CH0["mix"] + j * CG, 0, 0, dram["w_mix_out"], j * GW)
                if j == 0:
                    sync.wait_ge(sem("merged"), KG)
                    sync.dma_start(xres[:, :, :], dram["x"].rearrange("(t p) n -> p t n", p=P)).then_inc(sem("xres_loaded"), 16)
                    sync.dma_start(mem_tok[:, :, :], dram["mem"].rearrange("(t p) n -> p t n", p=P)).then_inc(sem("mem_loaded"), 16)
                    sync.dma_start(gain_final[:, :], dram["norm_final_g"].partition_broadcast(P)).then_inc(sem("gain_final_loaded"), 16)
            group(CH0["cross"], 0, 0, dram["w_xkv"], 0)
            group(CH0["cross"] + CG, 0, 0, dram["w_xq"], 0)
            group(CH0["cross"] + 2 * CG, 0, 0, dram["w_xkv"], GW)
            for j in range(KG):
                group(CH0["cross_out"] + 2 * j, 0, 0, dram["w_xo"], j * GW, rows_=NB)
            for part, f0, groups in (("a", 0, FA), ("b", FA, FB)):
                with sync.Fori(0, groups) as j:
                    for m, name in enumerate(("w_ffn_gate", "w_ffn_up")):
                        group(CH0["up_" + part] + m * CG, j, 2 * CG, dram[name], (f0 + j) * GW)
                with sync.Fori(0, KG // 2) as i:
                    for h in range(2):
                        group(CH0["down_" + part] + h * groups * 2, i, groups * 4, dram["w_ffn_down"],
                              (2 * i + h) * GW, rows_=groups * NB, row0=f0 * GW)
            for h in range(TT):
                sync.wait_ge(sem("out_ready"), h + 1)
                sync.dma_start(dram["out"][h * P:(h + 1) * P, :], xres[:, h, :]).then_inc(sem("out_stored"), 16)
            sync.wait_ge(sem("out_stored"), 16 * TT)

        @block.gpsimd
        def _(pool):
            nc.gpsimd.memset(pw[:, :], -0.5).then_inc(sem("pw_set"), 1)
            pool.wait_ge(sem("pw_set"), 1)

            def root_of(name):
                pool.wait_ge(sem("var_" + name), 1)
                nc.gpsimd.tensor_tensor(rstd[name][:, :], var[name][:, :], pw[:, :], ALU.pow).then_inc(sem("rstd_" + name), 1)

            root_of("x")
            pool.wait_ge(sem("derived"), 1)
            with pool.Fori(0, KG // 2) as i:
                for h in range(2):
                    pool.wait_ge(sem(f"rnn_lo{h}"), START + i)
                    j4 = (2 * i + h) * NB
                    nc.gpsimd.tensor_copy(pj[h][:, 0:CB + 1, :], params[:, 0:CB + 1, bass.ds(j4, NB)])
                    for row, src in ((BA, neg_ba), (BI, half_bi), (LAM, four_sp)):
                        last = nc.gpsimd.tensor_copy(pj[h][:, row, :], src[:, bass.ds(j4, NB)])
                    last.then_inc(sem(f"pj_ready{h}"), 1)
            for name in ("x1", "mem", "x2", "x3"):
                root_of(name)

        @block.tensor
        def _(pe):
            for signal in (*w_used, *(sem(f"lru_z{h}") for h in range(2))):
                pe.sem_inc(signal, START)
            def gemm(n, g, i, per_n, per_g, xh, xl, tiles):
                p, before = buf_of(g, i, per_g)
                for c in range(tiles // CK):
                    yield c
                    if c == 0:
                        pe.wait_ge(taken[p], START + before)
                    s, used = slot_of(n + c, i, per_n)
                    pe.wait_ge(w_ready[s], START + used + 1)
                    for k in range(CK):
                        kt = c * CK + k
                        for tt in range(TT):
                            tok = slice(tt * P, (tt + 1) * P)
                            first, end = kt == 0, kt == tiles - 1
                            nc.tensor.matmul(gps[p][:, tt, :], xh[:, kt, tok], whi[:, s, k, :], start=first, stop=False)
                            nc.tensor.matmul(gps[p][:, tt, :], xh[:, kt, tok], wlo[:, s, k, :], start=False, stop=False)
                            last = nc.tensor.matmul(gps[p][:, tt, :], xl[:, kt, tok], whi[:, s, k, :], start=False, stop=end)
                    last.then_inc(w_used[s], 1)

            def transpose(src, dst, done):
                for k in range(NB):
                    for tt in range(TT):
                        last = nc.tensor.transpose(dst[:, k, tt * P:(tt + 1) * P], src[:, tt, k * P:(k + 1) * P], ident)
                last.then_inc(sem(done), 1)

            pe.wait_ge(sem("consts_loaded"), 16)
            pe.wait_ge(sem("rows_loaded"), 16 * 9)
            nc.tensor.transpose(side[1][:, 0, 0:P], rows[:, 0, :], ident)
            nc.tensor.transpose(side[1][:, 0, P:P + 4 * KT], rows[0:4 * KT, 1, :], consts[0:4 * KT, 0:4 * KT]).then_inc(sem("rows_T"), 1)
            for q in range(KG):
                pe.wait_ge(sem(f"x_loaded{q}"), 16)
                if q == 1:
                    pe.wait_ge(sem("params_ready"), 1)
                if q >= 2:
                    pe.wait_ge(sem("x_lo"), q - 1)
                transpose(xres[:, :, q * GW:(q + 1) * GW], side[q % 2], "x_T")
            pe.wait_ge(sem("x_lo"), KG)

            with pe.Fori(0, KG // 2) as i:
                for h in range(2):
                    j = 2 * i + h
                    n, g = CH0["rnn_in"] + h * 3 * CG, GR0["rnn_in"] + h * 3
                    for c in gemm(n, g, i, 6 * CG, 6, xhi, xlo, KT):
                        pass
                    for c in gemm(n + CG, g + 1, i, 6 * CG, 6, xhi, xlo, KT):
                        if c == 1:
                            wait_taken(pe, g, i, 6)
                            transpose(rtok, side[0], "xr_T")
                        if c == 5:
                            pe.wait_ge(sem(f"lw_full{h}"), 32 * (i + 1))
                            pe.wait_ge(sem("conv_done"), j + 1)
                            for a in range(2):
                                for b in range(NB):
                                    last = nc.tensor.matmul(side[a][:, b, :], lw[h][:, a, b, :], conv[:, b, :], start=True, stop=True)
                            last.then_inc(sem(f"lru_z{h}"), 1)
                    for c in gemm(n + 2 * CG, g + 2, i, 6 * CG, 6, xhi, xlo, KT):
                        if c == 1:
                            wait_taken(pe, g + 1, i, 6)
                            pe.wait_ge(sem("r_exp"), j + 1)
                            transpose(rtok, side[0], "yr_T")
            for h in range(2):
                pe.wait_ge(sem(f"rnn_lo{h}"), START + KG // 2)
            with pe.Fori(0, KG // 2) as i:
                for h in range(2):
                    for c in gemm(CH0["rnn_out"] + h * CG, GR0["rnn_out"] + h, i, 2 * CG, 2, vhi, vlo, KT):
                        pass
            with pe.Fori(0, KG) as j:
                n, g = CH0["attn_in"], GR0["attn_in"]
                for c in gemm(n, g, j, 4 * CG, 4, xhi, xlo, KT):
                    pass
                for c in gemm(n + CG, g + 1, j, 4 * CG, 4, xhi, xlo, KT):
                    if c == 2:
                        pe.wait_ge(sem("k_rot"), j + 1)
                        transpose(ktok, side[0], "k_T_ps")
                for c in gemm(n + 2 * CG, g + 2, j, 4 * CG, 4, xhi, xlo, KT):
                    if c == 2:
                        pe.wait_ge(sem("q_rot"), j + 1)
                        transpose(qtok, side[1], "q_T_ps")
                    if c == 4:
                        pe.wait_ge(sem("k_T"), j + 1)
                        pe.wait_ge(sem("q_T"), j + 1)
                        s0 = side[0][:, 0:2, :].rearrange("p a (b k) -> p (a b) k", b=2)
                        for b in range(NB):
                            nc.tensor.matmul(s0[:, b, :], qT[:, b, 0:P], kT[:, b, 0:P], start=True, stop=True)
                        for b in range(NB):
                            last = nc.tensor.matmul(side[1][:, b, :], qT[:, b, P:2 * P], kT[:, b, :], start=True, stop=True)
                        last.then_inc(sem("scores"), 1)
                for c in gemm(n + 3 * CG, g + 3, j, 4 * CG, 4, xhi, xlo, KT):
                    if c == 3:
                        pe.wait_ge(sem("prob"), j + 1)
                        pt1 = side[1][:, 0:2, :].rearrange("p a (b k) -> p (a b) k", b=2)
                        for b in range(NB):
                            nc.tensor.transpose(side[0][:, b, 0:P], prob[:, b, 0:P], ident)
                            nc.tensor.transpose(side[0][:, b, P:2 * P], prob[:, b, P:2 * P], ident)
                            last = nc.tensor.transpose(pt1[:, b, :], prob[:, b, 2 * P:3 * P], ident)
                        last.then_inc(sem("prob_T_ps"), 1)
                    if c == 5:
                        pe.wait_ge(sem("prob_T"), j + 1)
                        for b in range(NB):
                            v0, v1 = vtok[:, 0, b * P:(b + 1) * P], vtok[:, 1, b * P:(b + 1) * P]
                            nc.tensor.matmul(side[0][:, b, :], v0, probT[:, b, 0:2 * P], start=True, stop=False)
                            last = nc.tensor.matmul(side[0][:, b, P:2 * P], v1, probT[:, b, 2 * P:3 * P], start=False, stop=True)
                        last.then_inc(sem("attn_o"), 1)
            pe.wait_ge(sem("attn_lo"), KG)

            def merge_T(j):
                pe.wait_ge(sem("merged"), j + 1)
                transpose(stage[j % 2], side[j % 2], "merged_T")

            def res_T(name, g, j):
                wait_taken(pe, g)
                transpose(xres[:, :, j * GW:(j + 1) * GW], side[j % 2], name + "_T")

            for j in range(KG):
                for c in gemm(CH0["attn_out"] + j * CG, GR0["attn_out"] + j, 0, 0, 0, vhi, vlo, KT):
                    if c == 2 and j >= 1:
                        merge_T(j - 1)
            for j in range(KG):
                for c in gemm(CH0["mix"] + j * CG, GR0["mix"] + j, 0, 0, 0, mhi, mlo, KT):
                    if c == 2:
                        if j == 0:
                            merge_T(KG - 1)
                        else:
                            res_T("x1", GR0["mix"] + j - 1, j - 1)
                    if c == 6 and j == 0:
                        pe.wait_ge(sem("merged_lo"), KG)
                    if c == 5 and j >= 1:
                        pe.wait_ge(sem("mem_loaded"), 16)
                        pe.wait_ge(sem("x1_lo"), j)
                        transpose(mem_tok[:, :, (j - 1) * GW:j * GW], side[j % 2], "mem_T")
            n, g = CH0["cross"], GR0["cross"]
            pe.wait_ge(sem("mem_lo"), 1)
            for c in gemm(n, g, 0, 0, 0, vhi, vlo, KT):
                if c == 1:
                    transpose(mem_tok[:, :, (KG - 1) * GW:KG * GW], side[0], "mem_T")
                if c == 3:
                    res_T("x1", GR0["mix"] + KG - 1, KG - 1)
                if c == 6:
                    pe.wait_ge(sem("mem_lo"), KG)
            pe.wait_ge(sem("x1_lo"), KG)
            for c in gemm(n + CG, g + 1, 0, 0, 0, xhi, xlo, KT):
                if c == 2:
                    wait_taken(pe, g)
                    transpose(ktok, side[0], "ck_T_ps")
            for c in gemm(n + 2 * CG, g + 2, 0, 0, 0, vhi, vlo, KT):
                if c == 1:
                    wait_taken(pe, g + 1)
                    transpose(qtok, side[1], "cq_T_ps")
                if c == 2:
                    pe.wait_ge(sem("ck_T"), 1)
                    pe.wait_ge(sem("cq_T"), 1)
                    for tt in range(TT):
                        for b in range(NB):
                            last = nc.tensor.matmul(side[tt][:, b, :], qT[:, b, tt * P:(tt + 1) * P], kT[:, b, :], start=True, stop=True)
                    last.then_inc(sem("cscores"), 1)
                if c == 6:
                    pe.wait_ge(sem("cprob"), 1)
                    for m in range(MEM // P):
                        for b in range(NB):
                            for tt in range(TT):
                                last = nc.tensor.transpose(side[m][:, b, tt * P:(tt + 1) * P], cprob[:, tt, b, m * P:(m + 1) * P], ident)
                    last.then_inc(sem("cprob_T_ps"), 1)
            pe.wait_ge(sem("cprob_T"), 1)
            wait_taken(pe, g + 2)
            for b in range(NB):
                nc.tensor.matmul(side[0][:, b, :], vtok[:, 0, b * P:(b + 1) * P], cprobT[:, 0, b, :], start=True, stop=False)
                last = nc.tensor.matmul(side[0][:, b, :], vtok[:, 1, b * P:(b + 1) * P], cprobT[:, 1, b, :], start=False, stop=True)
            last.then_inc(sem("cross_o"), 1)
            pe.wait_ge(sem("cross_lo"), 1)
            for j in range(KG):
                for c in gemm(CH0["cross_out"] + 2 * j, GR0["cross_out"] + j, 0, 0, 0, chi, clo, NB):
                    if c == 1 and j >= 1:
                        res_T("x2", GR0["cross_out"] + j - 1, j - 1)

            def inner_T():
                transpose(stage[0], side[0], "inner_T")

            for part, groups in (("a", FA), ("b", FB)):
                n, g = CH0["up_" + part], GR0["up_" + part]

                def pair(j, tail):
                    for c in gemm(n, g, j, 2 * CG, 2, xhi, xlo, KT):
                        if c == 2:
                            tail()
                        if c == 4 and part == "a" and isinstance(j, int):
                            pe.wait_ge(sem("x2_lo"), KG)
                    for c in gemm(n + CG, g + 1, j, 2 * CG, 2, xhi, xlo, KT):
                        pass

                def tail_first():
                    if part == "a":
                        res_T("x2", GR0["cross_out"] + KG - 1, KG - 1)

                done = 0 if part == "a" else FA

                def tail_inner(j):
                    wait_taken(pe, g - 1, j, 2)
                    inner_T()

                if part == "a":
                    pe.wait_ge(sem("x2_lo"), 2)
                pair(0, tail_first)
                with pe.Fori(1, groups) as j:
                    pair(j, lambda: tail_inner(j))
                nd, gd = CH0["down_" + part], GR0["down_" + part]

                def down(i, h, first):
                    for c in gemm(nd + h * groups * 2, gd + h, i, groups * 4, 2, inner_hi, inner_lo, groups * NB):
                        if first and c == 2:
                            tail_inner(groups)
                        if first and c == 6:
                            pe.wait_ge(sem("inner_lo"), done + groups)
                down(0, 0, True)
                down(0, 1, False)
                for h in range(2):
                    down(1, h, False)

        @block.scalar
        def _(act):
            def splits(n, count, i=0, per=0):
                for c in range(count):
                    m = n + c + LEAD
                    if m < CHUNKS:
                        s, used = slot_of(m, i, per)
                        act.wait_ge(raw_full[s], 16 * (used + 1))
                        act.wait_ge(w_used[s], START + used)
                        nc.scalar.activation(whi[:, s], raw[:, s], ACT.Copy).then_inc(hi_ready[s], 1)
                    yield c

            def evac(g, end, i, per_g, per_n, dst, scale, func):
                p, _ = buf_of(g)
                wait_product(act, end, i, per_n)
                for tt in range(TT):
                    last = nc.scalar.activation(dst[tt], gps[p][:, tt, :], func, scale=scale[:, tt:tt + 1])
                last.then_inc(taken[p], 1)

            def toks(x):
                return [x[:, tt, :] for tt in range(TT)]

            def copy(dst, src, ready, value, done):
                act.wait_ge(sem(ready), value)
                nc.scalar.activation(dst, src, ACT.Copy).then_inc(sem(done), 1)

            def gained_hi(src, gain, dst_hi, j, ready, value, done):
                act.wait_ge(sem(ready), value)
                for b in range(NB):
                    kt = j * NB + b
                    last = nc.scalar.activation(dst_hi[:, kt, :], src[:, b, :], ACT.Copy, scale=gains[:, gain, kt:kt + 1])
                last.then_inc(sem(done), 1)

            squared = [0]

            def squares(src, name, j):
                if squared[0]:
                    act.wait_ge(sem("squared"), squared[0])
                for tt in range(TT):
                    last = nc.scalar.activation(junk[:, tt, :], src[:, tt, j * GW:(j + 1) * GW], ACT.Square, accum_out=ss[name][:, tt, j:j + 1])
                last.then_inc(sem("squared"), 1)
                squared[0] += 1

            act.dma_start(consts[:, :], dram["consts"]).then_inc(sem("consts_loaded"), 16)
            act.dma_start(rows[0:64, 0, :], dram["conv_w"].rearrange("w (b p) -> (w b) p", p=P)).then_inc(sem("rows_loaded"), 16)
            for r, name in ((CB, "conv_b"), (BA, "lru_b_a"), (BI, "lru_b_i"), (LAM, "lru_lambda")):
                act.dma_start(rows[r * KT:(r + 1) * KT, 0, :], dram[name].rearrange("(b p) -> b p", p=P)).then_inc(sem("rows_loaded"), 16)
            for r, name in enumerate(("norm_mix_g", "norm_xq_g", "norm_mem_g", "norm_ffn_g")):
                act.dma_start(rows[r * KT:(r + 1) * KT, 1, :], dram[name].rearrange("(b p) -> b p", p=P)).then_inc(sem("rows_loaded"), 16)
            act.dma_start(pos_i[:, :], dram["positions"].rearrange("(t p) -> p t", p=P), allow_slow_non_contiguous=True).then_inc(sem("pos_loaded"), 16)
            act.wait_ge(sem("angles"), 1)
            nc.scalar.activation(rope[:, 2], rope[:, 0], ACT.Sin)
            nc.scalar.activation(rope[:, 3], rope[:, 0], ACT.Sin, scale=0.5).then_inc(sem("sines"), 1)
            act.wait_ge(sem("params_ready"), 1)
            nc.scalar.activation(sp[:, 1, :], sp[:, 0, :], ACT.Exp).then_inc(sem("exp_lam"), 1)
            act.wait_ge(sem("gains_ready"), 1)
            for q in range(KG):
                gained_hi(side[q % 2], 0, xhi, q, "x_T", q + 1, "x_hi")
                squares(xres, "x", q)
            for s in range(LEAD):
                act.wait_ge(raw_full[s], 16)
                nc.scalar.activation(whi[:, s], raw[:, s], ACT.Copy).then_inc(hi_ready[s], 1)

            with act.Fori(0, KG // 2) as i:
                for h in range(2):
                    j = 2 * i + h
                    n, g = CH0["rnn_in"] + h * 3 * CG, GR0["rnn_in"] + h * 3
                    for c in splits(n, CG, i, 6 * CG):
                        pass
                    for c in splits(n + CG, CG, i, 6 * CG):
                        if c == 0:
                            act.wait_ge(sem("rstd_x"), 1)
                            evac(g, n + CG, i, 6, 6 * CG, toks(rtok), rstd["x"], ACT.Copy)
                        if c == 1:
                            copy(xTp[:, :, 4:], side[0][:, :, :], "xr_T", j + 1, "xr_T_sb")
                            act.wait_ge(sem("xr_T_sb"), j + 1)
                            act.wait_ge(sem(f"pj_ready{h}"), i + 1)
                            for b in range(NB):
                                last = nc.scalar.activation(conv[:, b, :], xTp[:, b, 4:], ACT.Identity, scale=pj[h][:, CW + 3, b:b + 1],
                                                            bias=pj[h][:, CB, b:b + 1])
                            last.then_inc(sem("conv_tap3"), 1)
                        if c == 5:
                            act.wait_ge(sem(f"lru_z{h}"), START + i + 1)
                            for b in range(NB):
                                last = nc.scalar.activation(rgate[:, b, :], side[0][:, b, :], ACT.Exp, scale=-1.0, bias=pj[h][:, BA, b:b + 1])
                            last.then_inc(sem("r_exp"), 1)
                            for b in range(NB):
                                last = nc.scalar.activation(igate[:, b, :], side[1][:, b, :], ACT.Tanh, scale=0.5, bias=pj[h][:, BI, b:b + 1])
                            last.then_inc(sem("i_tanh"), 1)
                    for c in splits(n + 2 * CG, CG, i, 6 * CG):
                        if c == 0:
                            evac(g + 1, n + 2 * CG, i, 6, 6 * CG, toks(rtok), rstd["x"], ACT.Copy)
                            act.wait_ge(sem("r_gate"), j + 1)
                            for b in range(NB):
                                last = nc.scalar.activation(rgate[:, b, :], rgate[:, b, :], ACT.Tanh, scale=pj[h][:, LAM, b:b + 1])
                            last.then_inc(sem("s_tanh"), 1)
                        if c == 1:
                            copy(yT[:, :, :], side[0][:, :, :], "yr_T", j + 1, "y_T")
                        if c == 2:
                            act.wait_ge(sem("s_tanh"), j + 1)
                            nc.scalar.activation(root[:, :, :], rgate[:, :, :], ACT.Sqrt).then_inc(sem("root"), 1)
                        if c == 4:
                            act.wait_ge(sem("gelu_arg"), j + 1)
                            nc.scalar.activation(gelu[:, :, :], gelu[:, :, :], ACT.Tanh).then_inc(sem("gelu_tanh"), 1)
                    act.wait_ge(sem("rnn_val"), j + 1)
                    nc.scalar.activation(vhi[:, bass.ds(j * NB, NB), :], yT[:, :, :], ACT.Copy, scale=0.5).then_inc(sem("rnn_hi"), 1)
                    evac(g + 2, n + 3 * CG, i, 6, 6 * CG, [gated[:, tt, bass.ds(j * GW, GW)] for tt in range(TT)], hrstd["x"], ACT.Tanh)
            with act.Fori(0, KG // 2) as i:
                for h in range(2):
                    for c in splits(CH0["rnn_out"] + h * CG, CG, i, 2 * CG):
                        pass
            with act.Fori(0, KG) as j:
                n, g = CH0["attn_in"], GR0["attn_in"]
                for c in splits(n, CG, j, 4 * CG):
                    pass
                for c in splits(n + CG, CG, j, 4 * CG):
                    if c == 0:
                        evac(g, n + CG, j, 4, 4 * CG, toks(ktok), rstd["x"], ACT.Copy)
                    if c == 2:
                        copy(kT[:, :, :], side[0][:, :, :], "k_T_ps", j + 1, "k_T")
                for c in splits(n + 2 * CG, CG, j, 4 * CG):
                    if c == 0:
                        evac(g + 1, n + 2 * CG, j, 4, 4 * CG, toks(qtok), rstd["x"], ACT.Copy)
                    if c == 2:
                        copy(qT[:, :, :], side[1][:, :, :], "q_T_ps", j + 1, "q_T")
                for c in splits(n + 3 * CG, CG, j, 4 * CG):
                    if c == 0:
                        act.wait_ge(sem("neg_max"), j + 1)
                        for b in range(NB):
                            for tt, cols in ((0, slice(0, P)), (1, slice(P, 3 * P))):
                                last = nc.scalar.activation(prob[:, b, cols], prob[:, b, cols], ACT.Exp, scale=ATT_SCALE,
                                                            bias=nmax[:, tt, b:b + 1], accum_out=psum_[:, tt, b:b + 1])
                        last.then_inc(sem("prob_exp"), 1)
                        evac(g + 2, n + 3 * CG, j, 4, 4 * CG, toks(vtok), rstd["x"], ACT.Copy)
                    if c == 3:
                        act.wait_ge(sem("prob_T_ps"), j + 1)
                        nc.scalar.activation(probT[:, :, 0:2 * P], side[0][:, :, :], ACT.Copy)
                        nc.scalar.activation(probT[:, :, 2 * P:3 * P], side[1][:, 0:2, :].rearrange("p a (b k) -> p (a b) k", b=2),
                                             ACT.Copy).then_inc(sem("prob_T"), 1)
                    if c == 5:
                        act.wait_ge(sem("attn_o"), j + 1)
                        nc.scalar.activation(vhi[:, bass.ds(j * NB, NB), :], side[0][:, :, :], ACT.Copy).then_inc(sem("attn_hi"), 1)
                evac(g + 3, n + 4 * CG, j, 4, 4 * CG, [sig_attn[:, tt, bass.ds(j * GW, GW)] for tt in range(TT)], hrstd["x"], ACT.Tanh)

            def merge_hi(j):
                act.wait_ge(sem("merged_T"), j + 1)
                nc.scalar.activation(mhi[:, j * NB:(j + 1) * NB, :], side[j % 2][:, :, :], ACT.Copy, scale=0.5).then_inc(sem("merged_hi"), 1)

            for j in range(KG):
                for c in splits(CH0["attn_out"] + j * CG, CG):
                    if c == 2 and j >= 1:
                        merge_hi(j - 1)
            for j in range(KG):
                for c in splits(CH0["mix"] + j * CG, CG):
                    if c == 2:
                        if j == 0:
                            merge_hi(KG - 1)
                        else:
                            gained_hi(side[(j - 1) % 2], 1, xhi, j - 1, "x1_T", j, "x1_hi")
                            squares(xres, "x1", j - 1)
                    if c == 5 and j >= 1:
                        gained_hi(side[j % 2], 2, vhi, j - 1, "mem_T", j, "mem_hi")
                        squares(mem_tok, "mem", j - 1)
            n, g = CH0["cross"], GR0["cross"]
            for c in splits(n, CG):
                if c == 1:
                    gained_hi(side[0], 2, vhi, KG - 1, "mem_T", KG, "mem_hi")
                    squares(mem_tok, "mem", KG - 1)
                if c == 3:
                    gained_hi(side[1], 1, xhi, KG - 1, "x1_T", KG, "x1_hi")
                    squares(xres, "x1", KG - 1)
            for c in splits(n + CG, CG):
                if c == 0:
                    act.wait_ge(sem("rstd_mem"), 1)
                    evac(g, n + CG, 0, 0, 0, toks(ktok), rstd["mem"], ACT.Copy)
                if c == 2:
                    copy(kT[:, :, :], side[0][:, :, :], "ck_T_ps", 1, "ck_T")
            for c in splits(n + 2 * CG, CG):
                if c == 0:
                    act.wait_ge(sem("rstd_x1"), 1)
                    evac(g + 1, n + 2 * CG, 0, 0, 0, toks(qtok), rstd["x1"], ACT.Copy)
                if c == 1:
                    copy(qT[:, :, :], side[1][:, :, :], "cq_T_ps", 1, "cq_T")
                if c == 4:
                    act.wait_ge(sem("cneg_max"), 1)
                    for tt in range(TT):
                        for b in range(NB):
                            last = nc.scalar.activation(cprob[:, tt, b, :], cprob[:, tt, b, :], ACT.Exp, scale=ATT_SCALE,
                                                        bias=nmax[:, tt, b:b + 1], accum_out=psum_[:, tt, b:b + 1])
                    last.then_inc(sem("cprob_exp"), 1)
            act.wait_ge(sem("cprob_T_ps"), 1)
            nc.scalar.activation(cprobT[:, 0], side[0][:, :, :], ACT.Copy)
            nc.scalar.activation(cprobT[:, 1], side[1][:, :, :], ACT.Copy).then_inc(sem("cprob_T"), 1)
            evac(g + 2, n + 3 * CG, 0, 0, 0, toks(vtok), rstd["mem"], ACT.Copy)
            act.wait_ge(sem("cross_o"), 1)
            nc.scalar.activation(chi[:, :, :], side[0][:, :, :], ACT.Copy).then_inc(sem("cross_hi"), 1)
            for j in range(KG):
                for c in splits(CH0["cross_out"] + 2 * j, 2):
                    if c == 1 and j >= 1:
                        gained_hi(side[(j - 1) % 2], 3, xhi, j - 1, "x2_T", j, "x2_hi")
                        squares(xres, "x2", j - 1)
            for part, groups in (("a", FA), ("b", FB)):
                n, g = CH0["up_" + part], GR0["up_" + part]
                done = 0 if part == "a" else FA

                def inner_split(j):
                    act.wait_ge(sem("inner_T"), done + j)
                    nc.scalar.activation(inner_hi[:, bass.ds((j - 1) * NB, NB), :], side[0][:, :, :], ACT.Copy).then_inc(sem("inner_hi"), 1)

                def pair(j, tail):
                    for c in splits(n, CG, j, 2 * CG):
                        if c == 2:
                            tail()
                    for c in splits(n + CG, CG, j, 2 * CG):
                        if c == 0:
                            act.wait_ge(sem("rstd_x2"), 1)
                            p, _ = buf_of(g)
                            wait_product(act, n + CG, j, 2 * CG)
                            for tt in range(TT):
                                nc.scalar.activation(silu[:, tt, :], gps[p][:, tt, :], ACT.Tanh, scale=hrstd["x2"][:, tt:tt + 1])
                            for tt in range(TT):
                                last = nc.scalar.activation(gate_tok[:, tt, :], gps[p][:, tt, :], ACT.Copy, scale=hrstd["x2"][:, tt:tt + 1])
                            last.then_inc(taken[p], 1)

                def tail_first():
                    if part == "a":
                        gained_hi(side[1], 3, xhi, KG - 1, "x2_T", KG, "x2_hi")
                        squares(xres, "x2", KG - 1)
                pair(0, tail_first)
                with act.Fori(1, groups) as j:
                    pair(j, lambda: inner_split(j))
                nd = CH0["down_" + part]
                for q in range(KG):
                    for c in splits(nd + q * groups * 2, groups * 2):
                        if c == 2 and q == 0:
                            inner_split(groups)
                        if c == 1 and q >= 1 and part == "b":
                            wait_taken(act, GR0["down_b"] + q - 1)
                            squares(xres, "x3", q - 1)
            wait_taken(act, GR0["down_b"] + KG - 1)
            squares(xres, "x3", KG - 1)

        @block.vector
        def _(dve):
            V_ = nc.vector
            for signal in (*w_ready, *taken, *(sem(f"rnn_lo{h}") for h in range(2))):
                dve.sem_inc(signal, START)

            def splits(n, count, i=0, per=0):
                for c in range(count):
                    m = n + c + LEAD
                    if m < CHUNKS:
                        s, used = slot_of(m, i, per)
                        dve.wait_ge(hi_ready[s], used + 1)
                        V_.tensor_tensor(wlo[:, s], raw[:, s], whi[:, s].bitcast(F32), ALU.subtract).then_inc(w_ready[s], 1)
                    yield c

            chain = [0]

            def then(inst):
                chain[0] += 1
                inst.then_inc(sem("vector_chain"), 1)
                dve.wait_ge(sem("vector_chain"), chain[0])

            def gained_lo(src, gain, hi, lo, j, name):
                dve.wait_ge(sem(name + "_hi"), j + 1)
                for b in range(NB):
                    kt = j * NB + b
                    last = V_.scalar_tensor_tensor(lo[:, kt, :], src[:, b, :], gains[:, gain, kt:kt + 1], hi[:, kt, :].bitcast(F32), ALU.mult, ALU.subtract)
                last.then_inc(sem(name + "_lo"), 1)

            def variance(name):
                dve.wait_ge(sem("squared"), KG * ORDER[name])
                then(V_.tensor_reduce(var[name][:, :], ss[name][:, :, :], AX, ALU.add))
                V_.tensor_scalar(var[name][:, :], var[name][:, :], 1.0 / D, EPS, ALU.mult, ALU.add).then_inc(sem("var_" + name), 1)

            ORDER = {"x": 1, "mem": 3, "x1": 3, "x2": 4, "x3": 5}

            def half(name):
                dve.wait_ge(sem("rstd_" + name), 1)
                then(V_.tensor_scalar(hrstd[name][:, :], rstd[name][:, :], 0.5, None, ALU.mult))

            V_.memset(xTp[:, :, :], 0.0).then_inc(sem("conv_pad"), 1)
            dve.wait_ge(sem("pos_loaded"), 16)
            dve.wait_ge(sem("consts_loaded"), 16)
            then(V_.tensor_copy(pos_f[:, :], pos_i[:, :]))
            for tt in range(TT):
                last = V_.tensor_scalar(rope[:, 0, tt, :], inv_freq, pos_f[:, tt:tt + 1], None, ALU.mult)
            then(last)
            then(V_.tensor_scalar(rope[:, 1], rope[:, 0], 1.0 / TWO_PI, MAGIC, ALU.mult, ALU.add))
            then(V_.tensor_scalar(rope[:, 1], rope[:, 1], MAGIC, None, ALU.subtract))
            for part in PI_PARTS:
                then(V_.scalar_tensor_tensor(rope[:, 0], rope[:, 1], -part, rope[:, 0], ALU.mult, ALU.add))
            V_.tensor_scalar(rope[:, 0], rope[:, 0], 3.1415925, -3.1415925, ALU.min, ALU.max).then_inc(sem("angles"), 1)
            dve.wait_ge(sem("rows_T"), 1)
            V_.tensor_copy(params[:, :, :], side[1][:, 0, 0:P].rearrange("p (r b) -> p r b", r=8))
            V_.tensor_copy(gains[:, :, :], side[1][:, 0, P:P + 4 * KT].rearrange("p (r b) -> p r b", r=4)).then_inc(sem("gains_ready"), 1)
            dve.wait_ge(sem("gains_ready"), 1)
            then(V_.tensor_scalar(sp[:, 1, :], params[:, LAM, :], -1.0, None, ALU.mult))
            V_.tensor_tensor(sp[:, 0, :], params[:, LAM, :], sp[:, 1, :], ALU.min).then_inc(sem("neg_abs_lam"), 1)
            dve.wait_ge(sem("neg_abs_lam"), 1)
            V_.tensor_scalar(sp[:, 2, :], sp[:, 1, :], 0.0, None, ALU.max).then_inc(sem("params_ready"), 1)
            dve.wait_ge(sem("exp_lam"), 1)
            e, w, w2, acc = sp[:, 1, :], sp[:, 0, :], sp[:, 3, :], four_sp[:, :]
            then(V_.tensor_scalar(w, e, 2.0, None, ALU.add))
            then(V_.reciprocal(w2, w))
            then(V_.tensor_tensor(w, e, w2, ALU.mult))
            then(V_.tensor_tensor(w2, w, w, ALU.mult))
            then(V_.tensor_scalar(acc, w2, 1.0 / 17, 1.0 / 15, ALU.mult, ALU.add))
            for k in (13, 11, 9, 7, 5, 3, 1):
                then(V_.tensor_tensor(acc, acc, w2, ALU.mult))
                then(V_.tensor_scalar(acc, acc, 1.0 / k, None, ALU.add))
            then(V_.tensor_tensor(acc, acc, w, ALU.mult))
            then(V_.scalar_tensor_tensor(acc, acc, 2.0, sp[:, 2, :], ALU.mult, ALU.add))
            then(V_.tensor_scalar(acc, acc, 4.0, None, ALU.mult))
            V_.tensor_scalar(neg_ba[:, :], params[:, BA, :], -1.0, None, ALU.mult)
            V_.tensor_scalar(half_bi[:, :], params[:, BI, :], 0.5, None, ALU.mult).then_inc(sem("derived"), 1)
            for q in range(KG):
                gained_lo(side[q % 2], 0, xhi, xlo, q, "x")
            for s in range(LEAD):
                dve.wait_ge(hi_ready[s], 1)
                V_.tensor_tensor(wlo[:, s], raw[:, s], whi[:, s].bitcast(F32), ALU.subtract).then_inc(w_ready[s], 1)
            variance("x")
            dve.wait_ge(sem("sines"), 1)
            then(V_.tensor_tensor(rope[:, 4], rope[:, 3], rope[:, 3], ALU.mult))
            for b in range(NB):
                V_.tensor_copy(sin[:, :, b, :], rope[:, 2])
                last = V_.tensor_scalar(cos[:, :, b, :], rope[:, 4], -2.0, 1.0, ALU.mult, ALU.add)
            then(last)
            half("x")

            with dve.Fori(0, KG // 2) as i:
                for h in range(2):
                    j = 2 * i + h
                    n = CH0["rnn_in"] + h * 3 * CG
                    for c in splits(n, CG, i, 6 * CG):
                        pass
                    for c in splits(n + CG, CG, i, 6 * CG):
                        if c == 2:
                            dve.wait_ge(sem("conv_tap3"), j + 1)
                            for tap in (2, 1, 0):
                                if tap < 2:
                                    dve.wait_ge(sem(f"conv_tap{tap + 1}"), j + 1)
                                for b in range(NB):
                                    last = V_.scalar_tensor_tensor(conv[:, b, :], xTp[:, b, 1 + tap:1 + tap + SEQ], pj[h][:, CW + tap, b:b + 1],
                                                                   conv[:, b, :], ALU.mult, ALU.add)
                                last.then_inc(sem(f"conv_tap{tap}" if tap else "conv_done"), 1)
                        if c == 6:
                            dve.wait_ge(sem("r_exp"), j + 1)
                            V_.tensor_scalar(den[:, :, :], rgate[:, :, :], 1.0, None, ALU.add).then_inc(sem("r_den"), 1)
                            dve.wait_ge(sem("r_den"), j + 1)
                            V_.reciprocal(rgate[:, :, :], den[:, :, :]).then_inc(sem("r_gate"), 1)
                        if c == 7:
                            dve.wait_ge(sem("i_tanh"), j + 1)
                            dve.wait_ge(sem("conv_done"), j + 1)
                            V_.scalar_tensor_tensor(igate[:, :, :], igate[:, :, :], 1.0, conv[:, :, :], ALU.add, ALU.mult).then_inc(sem("ix"), 1)
                    for c in splits(n + 2 * CG, CG, i, 6 * CG):
                        if c == 1:
                            dve.wait_ge(sem("s_tanh"), j + 1)
                            V_.tensor_scalar(den[:, :, :], rgate[:, :, :], 1.0, None, ALU.add).then_inc(sem("s_den"), 1)
                            dve.wait_ge(sem("s_den"), j + 1)
                            V_.reciprocal(den[:, :, :], den[:, :, :]).then_inc(sem("s_rden"), 1)
                        if c == 2:
                            dve.wait_ge(sem("s_rden"), j + 1)
                            dve.wait_ge(sem("ix"), j + 1)
                            V_.tensor_tensor(igate[:, :, :], igate[:, :, :], den[:, :, :], ALU.mult).then_inc(sem("ixd"), 1)
                            dve.wait_ge(sem("y_T"), j + 1)
                            V_.tensor_tensor(gelu[:, :, :], yT[:, :, :], yT[:, :, :], ALU.mult).then_inc(sem("y2"), 1)
                            dve.wait_ge(sem("y2"), j + 1)
                            V_.tensor_scalar(gelu[:, :, :], gelu[:, :, :], GELU_C * 0.044715, GELU_C, ALU.mult, ALU.add).then_inc(sem("y2c"), 1)
                        if c == 3:
                            dve.wait_ge(sem("y2c"), j + 1)
                            V_.tensor_tensor(gelu[:, :, :], gelu[:, :, :], yT[:, :, :], ALU.mult).then_inc(sem("gelu_arg"), 1)
                            dve.wait_ge(sem("root"), j + 1)
                            V_.tensor_scalar(rgate[:, :, :], rgate[:, :, :], -1.0, 1.0, ALU.mult, ALU.add).then_inc(sem("one_minus_s"), 1)
                            dve.wait_ge(sem("one_minus_s"), j + 1)
                            V_.tensor_tensor(rgate[:, :, :], rgate[:, :, :], den[:, :, :], ALU.mult).then_inc(sem("a"), 1)
                        if c == 4:
                            dve.wait_ge(sem("ixd"), j + 1)
                            V_.tensor_tensor(igate[:, :, :], igate[:, :, :], root[:, :, :], ALU.mult).then_inc(sem("u"), 1)
                            dve.wait_ge(sem("u"), j + 1)
                            dve.wait_ge(sem("a"), j + 1)
                            for b in range(NB):
                                last = V_.tensor_tensor_scan(conv[:, b, :], rgate[:, b, :], igate[:, b, :], 0.0, ALU.mult, ALU.add)
                            last.then_inc(sem("scanned"), 1)
                        if c == 5:
                            dve.wait_ge(sem("gelu_tanh"), j + 1)
                            V_.scalar_tensor_tensor(yT[:, :, :], gelu[:, :, :], 1.0, yT[:, :, :], ALU.add, ALU.mult).then_inc(sem("gelu2"), 1)
                            dve.wait_ge(sem("gelu2"), j + 1)
                            dve.wait_ge(sem("scanned"), j + 1)
                            V_.tensor_tensor(yT[:, :, :], yT[:, :, :], conv[:, :, :], ALU.mult).then_inc(sem("rnn_val"), 1)
                    dve.wait_ge(sem("rnn_hi"), j + 1)
                    last = V_.scalar_tensor_tensor(vlo[:, bass.ds(j * NB, NB), :], yT[:, :, :], 0.5, vhi[:, bass.ds(j * NB, NB), :].bitcast(F32),
                                                   ALU.mult, ALU.subtract)
                    last.then_inc(sem(f"rnn_lo{h}"), 1)
            with dve.Fori(0, KG // 2) as i:
                for h in range(2):
                    j = 2 * i + h
                    for c in splits(CH0["rnn_out"] + h * CG, CG, i, 2 * CG):
                        pass
                    p, _ = buf_of(GR0["rnn_out"] + h)
                    wait_product(dve, CH0["rnn_out"] + (h + 1) * CG, i, 2 * CG)
                    for g in range(GR0["attn_in"] - KG - 2, GR0["attn_in"] - KG):
                        wait_taken(dve, g)
                    cols = bass.ds(j * GW, GW)
                    last = V_.scalar_tensor_tensor(gated[:, :, cols], gated[:, :, cols], 1.0, gps[p][:, :, :], ALU.add, ALU.mult)
                    last.then_inc(taken[p], 1)

            def rotate(x, what, j):
                v = x[:, :, :].rearrange("p t (b d) -> p t b d", d=P)
                x1, x2 = v[:, :, :, 0:ROT], v[:, :, :, ROT:2 * ROT]
                wait_taken(dve, GR0["attn_in"] + (0 if what == "k" else 1), j, 4)
                V_.tensor_tensor(rt[:, 0], x1, cos[:, :, :, :], ALU.mult)
                V_.tensor_tensor(rt[:, 1], x2, sin[:, :, :, :], ALU.mult)
                V_.tensor_tensor(rt[:, 2], x2, cos[:, :, :, :], ALU.mult)
                V_.tensor_tensor(rt[:, 3], x1, sin[:, :, :, :], ALU.mult).then_inc(sem(what + "_rot_products"), 1)
                dve.wait_ge(sem(what + "_rot_products"), j + 1)
                V_.tensor_tensor(x1, rt[:, 0], rt[:, 1], ALU.subtract)
                V_.tensor_tensor(x2, rt[:, 2], rt[:, 3], ALU.add).then_inc(sem(what + "_rot"), 1)

            with dve.Fori(0, KG) as j:
                n = CH0["attn_in"]
                for c in splits(n, CG, j, 4 * CG):
                    pass
                for c in splits(n + CG, CG, j, 4 * CG):
                    if c == 0:
                        rotate(ktok, "k", j)
                for c in splits(n + 2 * CG, CG, j, 4 * CG):
                    if c == 0:
                        rotate(qtok, "q", j)
                    if c == 4:
                        dve.wait_ge(sem("scores"), j + 1)
                        s0 = side[0][:, 0:2, :].rearrange("p a (b k) -> p (a b) k", b=2)
                        V_.tensor_tensor(prob[:, :, 0:P], s0, mask[:, P:2 * P].unsqueeze(1).to_broadcast([P, NB, P]), ALU.add)
                        V_.tensor_tensor(prob[:, :, P:3 * P], side[1][:, :, :], mask.unsqueeze(1).to_broadcast([P, NB, 2 * P]), ALU.add)\
                            .then_inc(sem("masked"), 1)
                    if c == 6:
                        dve.wait_ge(sem("masked"), j + 1)
                        V_.tensor_reduce(smax[:, 0, :], prob[:, :, 0:P], AX, ALU.max)
                        V_.tensor_reduce(smax[:, 1, :], prob[:, :, P:3 * P], AX, ALU.max).then_inc(sem("smax"), 1)
                        dve.wait_ge(sem("smax"), j + 1)
                        V_.tensor_scalar(nmax[:, :, :], smax[:, :, :], -ATT_SCALE, None, ALU.mult).then_inc(sem("neg_max"), 1)
                for c in splits(n + 3 * CG, CG, j, 4 * CG):
                    if c == 1:
                        dve.wait_ge(sem("prob_exp"), j + 1)
                        V_.reciprocal(rsum[:, :, :], psum_[:, :, :]).then_inc(sem("rsum"), 1)
                        dve.wait_ge(sem("rsum"), j + 1)
                        V_.tensor_tensor(prob[:, :, 0:P], prob[:, :, 0:P], rsum[:, 0, :].unsqueeze(2).to_broadcast([P, NB, P]), ALU.mult)
                        V_.tensor_tensor(prob[:, :, P:3 * P], prob[:, :, P:3 * P], rsum[:, 1, :].unsqueeze(2).to_broadcast([P, NB, 2 * P]), ALU.mult)\
                            .then_inc(sem("prob"), 1)
                dve.wait_ge(sem("attn_hi"), j + 1)
                V_.tensor_tensor(vlo[:, bass.ds(j * NB, NB), :], side[0][:, :, :], vhi[:, bass.ds(j * NB, NB), :].bitcast(F32), ALU.subtract)\
                    .then_inc(sem("attn_lo"), 1)

            def merge(j):
                p, before = buf_of(GR0["attn_out"] + j)
                cols = slice(j * GW, (j + 1) * GW)
                wait_product(dve, CH0["attn_out"] + (j + 1) * CG)
                wait_taken(dve, GR0["attn_out"] - 1)
                V_.scalar_tensor_tensor(stage[j % 2][:, :, :], sig_attn[:, :, cols], 1.0, gps[p][:, :, :], ALU.add, ALU.mult).then_inc(taken[p], 1)
                dve.wait_ge(taken[p], START + before + 1)
                V_.tensor_tensor(stage[j % 2][:, :, :], stage[j % 2][:, :, :], gated[:, :, cols], ALU.add).then_inc(sem("merged"), 1)

            def merge_lo(j):
                kts = slice(j * NB, (j + 1) * NB)
                dve.wait_ge(sem("merged_hi"), j + 1)
                V_.scalar_tensor_tensor(mlo[:, kts, :], side[j % 2][:, :, :], 0.5, mhi[:, kts, :].bitcast(F32), ALU.mult, ALU.subtract)\
                    .then_inc(sem("merged_lo"), 1)

            def add_group(g, end, j):
                p, _ = buf_of(g)
                cols = slice(j * GW, (j + 1) * GW)
                wait_product(dve, end)
                V_.tensor_tensor(xres[:, :, cols], xres[:, :, cols], gps[p][:, :, :], ALU.add).then_inc(taken[p], 1)

            for j in range(KG):
                for c in splits(CH0["attn_out"] + j * CG, CG):
                    if c == 3 and j >= 1:
                        merge_lo(j - 1)
                merge(j)
            for j in range(KG):
                for c in splits(CH0["mix"] + j * CG, CG):
                    if c == 3:
                        if j == 0:
                            merge_lo(KG - 1)
                        else:
                            gained_lo(side[(j - 1) % 2], 1, xhi, xlo, j - 1, "x1")
                    if c == 6 and j >= 1:
                        gained_lo(side[j % 2], 2, vhi, vlo, j - 1, "mem")
                if j == 0:
                    dve.wait_ge(sem("xres_loaded"), 16)
                add_group(GR0["mix"] + j, CH0["mix"] + (j + 1) * CG, j)
            n, g = CH0["cross"], GR0["cross"]
            for c in splits(n, CG):
                if c == 2:
                    gained_lo(side[0], 2, vhi, vlo, KG - 1, "mem")
                if c == 4:
                    gained_lo(side[1], 1, xhi, xlo, KG - 1, "x1")
                if c == 5:
                    variance("x1")
                    variance("mem")
            for c in splits(n + CG, CG):
                pass
            for c in splits(n + 2 * CG, CG):
                if c == 2:
                    dve.wait_ge(sem("cscores"), 1)
                    for tt in range(TT):
                        V_.tensor_copy(cprob[:, tt], side[tt][:, :, :]).then_inc(sem("cscores_sb"), 1)
                if c == 3:
                    dve.wait_ge(sem("cscores_sb"), TT)
                    then(V_.tensor_reduce(smax[:, :, :].rearrange("p t b -> p (t b)"), cprob[:, :, :, :].rearrange("p t b k -> p (t b) k"), AX, ALU.max))
                    V_.tensor_scalar(nmax[:, :, :], smax[:, :, :], -ATT_SCALE, None, ALU.mult).then_inc(sem("cneg_max"), 1)
                if c == 6:
                    dve.wait_ge(sem("cprob_exp"), 1)
                    then(V_.reciprocal(rsum[:, :, :], psum_[:, :, :]))
                    for tt in range(TT):
                        last = V_.tensor_tensor(cprob[:, tt], cprob[:, tt], rsum[:, tt, :].unsqueeze(2).to_broadcast([P, NB, MEM]), ALU.mult)
                    last.then_inc(sem("cprob"), 1)
            dve.wait_ge(sem("cross_hi"), 1)
            V_.tensor_tensor(clo[:, :, :], side[0][:, :, :], chi[:, :, :].bitcast(F32), ALU.subtract).then_inc(sem("cross_lo"), 1)
            for j in range(KG):
                for c in splits(CH0["cross_out"] + 2 * j, 2):
                    if c == 1 and j >= 1:
                        gained_lo(side[(j - 1) % 2], 3, xhi, xlo, j - 1, "x2")
                add_group(GR0["cross_out"] + j, CH0["cross_out"] + 2 * (j + 1), j)
            for part, groups in (("a", FA), ("b", FB)):
                n, g = CH0["up_" + part], GR0["up_" + part]
                done = 0 if part == "a" else FA

                def inner_rest(j):
                    kts = bass.ds((j - 1) * NB, NB)
                    dve.wait_ge(sem("inner_hi"), done + j)
                    V_.tensor_tensor(inner_lo[:, kts, :], side[0][:, :, :], inner_hi[:, kts, :].bitcast(F32), ALU.subtract)\
                        .then_inc(sem("inner_lo"), 1)

                def pair(j, tail):
                    for c in splits(n, CG, j, 2 * CG):
                        if c == 3:
                            tail()
                    for c in splits(n + CG, CG, j, 2 * CG):
                        if c == 2:
                            wait_taken(dve, g, j, 2)
                            V_.scalar_tensor_tensor(silu[:, :, :], silu[:, :, :], 1.0, gate_tok[:, :, :], ALU.add, ALU.mult).then_inc(sem("silu"), 1)
                    p, _ = buf_of(g + 1)
                    wait_product(dve, n + 2 * CG, j, 2 * CG)
                    dve.wait_ge(sem("silu"), done + j + 1)
                    for tt in range(TT):
                        last = V_.scalar_tensor_tensor(stage[0][:, tt, :], gps[p][:, tt, :], rstd["x2"][:, tt:tt + 1], silu[:, tt, :], ALU.mult, ALU.mult)
                    last.then_inc(taken[p], 1)

                def tail_first():
                    if part == "a":
                        gained_lo(side[1], 3, xhi, xlo, KG - 1, "x2")
                        variance("x2")
                        half("x2")
                pair(0, tail_first)
                with dve.Fori(1, groups) as j:
                    pair(j, lambda: inner_rest(j))
                nd, gd = CH0["down_" + part], GR0["down_" + part]
                for q in range(KG):
                    for c in splits(nd + q * groups * 2, groups * 2):
                        if c == 3 and q == 0:
                            inner_rest(groups)
                    add_group(gd + q, nd + (q + 1) * groups * 2, q)
            variance("x3")
            dve.wait_ge(sem("gain_final_loaded"), 16)
            for tt in range(TT):
                then(V_.tensor_tensor(xres[:, tt, :], xres[:, tt, :], gain_final[:, :], ALU.mult))
            dve.wait_ge(sem("rstd_x3"), 1)
            for tt in range(TT):
                V_.tensor_scalar(xres[:, tt, :], xres[:, tt, :], rstd["x3"][:, tt:tt + 1], None, ALU.mult).then_inc(sem("out_ready"), 1)


NAMES = ["x", "mem", "positions", "norm_mix_g", "w_in", "conv_w", "conv_b", "lru_w_a", "lru_b_a", "lru_w_i", "lru_b_i",
         "lru_lambda", "w_rnn_proj", "w_attn_proj", "w_mix_out", "norm_xq_g", "norm_mem_g", "w_xq", "w_xkv", "w_xo",
         "norm_ffn_g", "w_ffn_gate", "w_ffn_up", "w_ffn_down", "norm_final_g"]


def constants():
    c = np.zeros((P, 3 * P + ROT), np.float32)
    c[:, 0:P] = np.eye(P)
    c[:, 2 * P:3 * P] = np.where(np.arange(P)[None, :] > np.arange(P)[:, None], -1e30, 0.0)
    c[:, 3 * P:] = np.power(np.float32(500000.0), -np.arange(ROT, dtype=np.float32) / np.float32(ROT))
    return c


def kernel(**inputs):
    import concourse.bacc as bacc
    from concourse.bass_utils import run_bass_kernel_spmd

    nc = bacc.Bacc("TRN2", target_bir_lowering=False, num_devices=1)
    arrays, tensors = {}, {}
    for name in NAMES:
        a = np.ascontiguousarray(inputs[name])
        if a.shape[0] == 1:
            a = a.reshape(a.shape[1:])
        arrays["in_" + name] = a
    arrays["in_consts"] = constants()
    for name, a in arrays.items():
        tensors[name[3:]] = nc.dram_tensor(name, a.shape, mybir.dt.from_np(a.dtype), kind="ExternalInput").ap()
    tensors["out"] = nc.dram_tensor("out", (SEQ, D), F32, kind="ExternalOutput").ap()
    build(nc, tensors)
    result = run_bass_kernel_spmd(nc, [arrays], core_ids=[0])
    return result.results[0]["out"].reshape(1, SEQ, D)
```

```python
import numpy as np
import concourse.bass as bass
from concourse import mybir
from contextlib import ExitStack

F32 = mybir.dt.float32
F32R = mybir.dt.float32r
I32 = mybir.dt.int32
ALU = mybir.AluOpType
ACT = mybir.ActivationFunctionType
AX = mybir.AxisListType.X

P = 128
SEQ, D, F, MEM = 256, 2048, 5632, 256
TT = SEQ // P
GW = 512
KG = D // GW
NB = GW // P
KT = D // P
R = 4
LEAD = 3
CK = 2
CG = KT // CK
EPS = 1e-6
ATT_SCALE = float(P) ** -0.5
FA, FB = 6, 5
ROT = 16
IN_COLS = {"xr": 0, "yr": D, "q": 2 * D, "k": 3 * D, "v": 4 * D, "g_rnn": 5 * D, "g_attn": 6 * D}
GELU_C = 0.7978845608028654
TWO_PI = 6.283185307179586
MAGIC = 12582912.0
PI_PARTS = [6.25, 0.03125, 0.0019340515136718750]
PI_PARTS.append(TWO_PI - sum(PI_PARTS))

STAGES = ["rnn_in", "rnn_out", "attn_in", "attn_out", "mix", "cross", "cross_out", "up_a", "down_a", "up_b", "down_b"]
_CH = [3 * KG * CG, KG * CG, 4 * KG * CG, KG * CG, KG * CG, 3 * CG, KG * 2, 2 * FA * CG, KG * FA * 2, 2 * FB * CG, KG * FB * 2]
_GR = [3 * KG, KG, 4 * KG, KG, KG, 3, KG, 2 * FA, KG, 2 * FB, KG]
CH0 = {s: sum(_CH[:i]) for i, s in enumerate(STAGES)}
GR0 = {s: sum(_GR[:i]) for i, s in enumerate(STAGES)}
CHUNKS = sum(_CH)
CW, CB, BA, BI, LAM = 0, 4, 5, 6, 7


def build(nc, t):
    ctx = ExitStack()
    with ctx:
        sems = {}

        def sem(name):
            if name not in sems:
                sems[name] = ctx.enter_context(nc.semaphore(name))
            return sems[name]

        K1 = 1024
        total = 207 * K1
        ctx.enter_context(nc.sbuf_tensor("arena", [P, total], mybir.dt.uint8))
        arena = nc.sbuf_base - total
        top = [0]

        def region(size):
            top[0] += size
            assert top[0] <= total
            return arena + top[0] - size

        def at(name, offset, shape, dt=F32):
            return nc.alloc_sbuf_tensor_at(name, [P] + shape, dt, offset=offset)

        def new(name, shape, dt=F32):
            size = 4 * int(np.prod(shape))
            return at(name, region((size + 31) // 32 * 32), shape, dt)

        raw = new("w_raw", [R, CK, GW])
        whi = new("w_hi", [R, CK, GW], F32R)
        wlo = new("w_lo", [R, CK, GW], F32R)
        xhi = new("x_hi", [KT, SEQ], F32R)
        xlo = new("x_lo", [KT, SEQ], F32R)
        U, V, G, S = region(32 * K1), region(32 * K1), region(16 * K1), region(16 * K1)
        vhi, vlo = at("v_hi", V, [KT, SEQ], F32R), at("v_lo", V + 16 * K1, [KT, SEQ], F32R)
        inner_hi = at("inner_hi", U, [FA * NB, SEQ], F32R)
        inner_lo = at("inner_lo", V, [FA * NB, SEQ], F32R)
        mhi, mlo = at("merged_hi", U, [KT, SEQ], F32R), at("merged_lo", U + 16 * K1, [KT, SEQ], F32R)
        rtok = at("rnn_tok", U, [TT, GW])
        conv = at("conv_T", U + 4 * K1, [NB, SEQ])
        ysq = at("y_squared", U, [NB, SEQ])
        rgate = at("r_gate", U + 8 * K1, [NB, SEQ])
        igate = at("i_gate", U + 12 * K1, [NB, SEQ])
        den = at("lru_den", U + 16 * K1, [NB, SEQ])
        yT = at("y_T", U + 20 * K1, [NB, SEQ])
        gelu = at("gelu_T", U + 24 * K1, [NB, SEQ])
        root = at("lru_root", U + 28 * K1, [NB, SEQ])
        ktok = at("k_tok", U, [TT, GW])
        qtok = at("q_tok", U + 4 * K1, [TT, GW])
        vtok = at("v_tok", U + 8 * K1, [TT, GW])
        kT = at("k_T", U + 12 * K1, [NB, SEQ])
        qT = at("q_T", U + 16 * K1, [NB, SEQ])
        prob = at("prob", U + 20 * K1, [NB, 3 * P])
        probT = at("prob_T", U + 26 * K1, [NB, 3 * P])
        cprob = at("cross_prob", U + 20 * K1, [TT, NB, MEM])
        gated = at("gated_rnn", G, [TT, D])
        xres = at("x_res", G, [TT, D])
        sig_attn = at("sig_attn", S, [TT, D])
        cprobT = at("cross_prob_T", S, [MEM // P, NB, SEQ])
        chi = at("cross_hi", S + 8 * K1, [NB, SEQ], F32R)
        clo = at("cross_lo", S + 12 * K1, [NB, SEQ], F32R)
        gate_tok = at("gate_tok", S, [TT, GW])
        silu = at("silu_tok", S + 4 * K1, [TT, GW])
        stage = [new("stage0", [TT, GW]), new("stage1", [TT, GW])]
        LW = region(8 * K1)
        lw = [at("lru_w0", LW, [2, NB, P]), at("lru_w1", LW + 4 * K1, [2, NB, P])]
        gain_final = at("gain_final", LW, [D])
        square_out = {"x": at("x_squares0", V, [D]), "mem": at("mem_squares0", U, [D])}
        square_out2 = {"x": at("x_squares1", V + 8 * K1, [D]), "mem": at("mem_squares1", U + 16 * K1, [D])}
        PAD = region(4 * NB * (4 + SEQ))
        xTp = at("conv_in_T", PAD, [NB, 4 + SEQ])
        junk = at("junk", PAD, [TT, GW])
        consts = new("consts", [P + 2 * P + ROT])
        ident, mask, inv_freq = consts[:, 0:P], consts[:, P:3 * P], consts[:, 3 * P:3 * P + ROT]
        xT_in = at("x_T_in", U + 16 * K1, [KT, SEQ])
        mem_sq = at("mem_for_squares", S, [TT, D])
        memT_in = at("mem_T_in", S, [KT, MEM])
        table = new("params", [12, KT])
        params, gains = table[:, 0:8], table[:, 8:12]
        neg_ba, half_bi, four_sp = new("neg_b_a", [KT]), new("half_b_i", [KT]), new("four_softplus", [KT])
        pj = [new("block_params0", [8, NB]), new("block_params1", [8, NB])]
        pos_i, pos_f = new("pos_i", [TT], I32), new("pos_f", [TT])
        rope = new("rope_tmp", [5, TT, ROT])
        cos, sin = new("cos", [TT, NB, ROT]), new("sin", [TT, NB, ROT])
        rt = new("rope_products", [4, TT, NB, ROT])
        sp = new("softplus_tmp", [4, KT])
        pw = new("minus_half", [TT])
        ss = {n: new("ss_" + n, [TT, KG]) for n in ("x1", "x2", "x3")}
        ss.update({n: new("ss_" + n, [TT]) for n in ("x", "mem")})
        var = {n: new("var_" + n, [TT]) for n in ss}
        rstd = {n: new("rstd_" + n, [TT]) for n in ss}
        hrstd = {n: new("hrstd_" + n, [TT]) for n in ss}
        smax, nmax = new("smax", [TT, NB]), new("nmax", [TT, NB])
        psum_, rsum = new("prob_sum", [TT, NB]), new("prob_rsum", [TT, NB])

        gps = [ctx.enter_context(nc.psum_tensor(f"group{p}", [P, TT, GW], F32)) for p in range(2)]
        side = [ctx.enter_context(nc.psum_tensor(f"side{p}", [P, NB, SEQ], F32)) for p in range(2)]

        raw_full = [sem(f"raw_full{s}") for s in range(R)]
        hi_ready = [sem(f"hi_ready{s}") for s in range(R)]
        w_ready = [sem(f"w_ready{s}") for s in range(R)]
        w_used = [sem(f"w_used{s}") for s in range(R)]
        taken = [sem(f"taken{p}") for p in range(2)]

        START = 1

        def slot_of(n, i=0, per=0):
            return n % R, n // R + i * (per // R)

        def buf_of(g, i=0, per=0):
            return g % 2, g // 2 + i * (per // 2)

        def wait_product(engine, end, i=0, per=0):
            s, used = slot_of(end - 1, i, per)
            engine.wait_ge(w_used[s], START + used + 1)

        def wait_taken(engine, g, i=0, per=0):
            p, before = buf_of(g, i, per)
            engine.wait_ge(taken[p], START + before + 1)

        dram = t

        block = ctx.enter_context(nc.Block())

        @block.sync
        def _(sp_):
            sync = sp_
            def load(n, i, per, w, row, col):
                s, before = slot_of(n, i, per)
                sync.wait_ge(w_ready[s], START + before)
                sync.dma_start(raw[:, s], w[row:row + CK * P, bass.ds(col, GW)].rearrange("(k p) n -> p k n", p=P))\
                    .then_inc(raw_full[s], 16)

            def group(n, i, per, w, col, rows_=KT, row0=0):
                for c in range(rows_ // CK):
                    load(n + c, i, per, w, row0 + c * CK * P, col)

            w_in = dram["w_in"]
            with sync.Fori(0, KG // 2) as i:
                for h in range(2):
                    n = CH0["rnn_in"] + h * 3 * CG
                    j = 2 * i + h
                    sync.wait_ge(sem(f"lru_z{h}"), START + i)
                    for a, name in enumerate(("lru_w_a", "lru_w_i")):
                        sync.dma_start(lw[h][:, a], dram[name][bass.ds(j * NB, NB), :, :].rearrange("n k m -> k n m"))\
                            .then_inc(sem(f"lw_full{h}"), 16)
                    for m, name in enumerate(("xr", "yr", "g_rnn")):
                        group(n + m * CG, i, 6 * CG, w_in, IN_COLS[name] + j * GW)
            with sync.Fori(0, KG // 2) as i:
                for h in range(2):
                    group(CH0["rnn_out"] + h * CG, i, 2 * CG, dram["w_rnn_proj"], (2 * i + h) * GW)
            with sync.Fori(0, KG) as j:
                for m, name in enumerate(("k", "q", "v", "g_attn")):
                    group(CH0["attn_in"] + m * CG, j, 4 * CG, w_in, IN_COLS[name] + j * GW)
            for j in range(KG):
                group(CH0["attn_out"] + j * CG, 0, 0, dram["w_attn_proj"], j * GW)
            for j in range(KG):
                group(CH0["mix"] + j * CG, 0, 0, dram["w_mix_out"], j * GW)
            group(CH0["cross"], 0, 0, dram["w_xkv"], 0)
            group(CH0["cross"] + CG, 0, 0, dram["w_xq"], 0)
            group(CH0["cross"] + 2 * CG, 0, 0, dram["w_xkv"], GW)
            for j in range(KG):
                group(CH0["cross_out"] + 2 * j, 0, 0, dram["w_xo"], j * GW, rows_=NB)
            for part, f0, groups in (("a", 0, FA), ("b", FA, FB)):
                with sync.Fori(0, groups) as j:
                    for m, name in enumerate(("w_ffn_gate", "w_ffn_up")):
                        group(CH0["up_" + part] + m * CG, j, 2 * CG, dram[name], (f0 + j) * GW)
                with sync.Fori(0, KG // 2) as i:
                    for h in range(2):
                        group(CH0["down_" + part] + h * groups * 2, i, groups * 4, dram["w_ffn_down"],
                              (2 * i + h) * GW, rows_=groups * NB, row0=f0 * GW)
            for h in range(TT):
                for part, cols in enumerate((slice(0, D // 2), slice(D // 2, D))):
                    sync.wait_ge(sem("out_ready"), 2 * h + part + 1)
                    sync.dma_start(dram["out"][h * P:(h + 1) * P, cols], xres[:, h, cols]).then_inc(sem("out_stored"), 16)
            sync.wait_ge(sem("out_stored"), 16 * 2 * TT)

        @block.gpsimd
        def _(pool):
            nc.gpsimd.memset(pw[:, :], -0.5).then_inc(sem("pw_set"), 1)
            pool.wait_ge(sem("pw_set"), 1)

            def root_of(name):
                pool.wait_ge(sem("var_" + name), 1)
                nc.gpsimd.tensor_tensor(rstd[name][:, :], var[name][:, :], pw[:, :], ALU.pow).then_inc(sem("rstd_" + name), 1)

            pool.dma_start(consts[:, :], dram["consts"]).then_inc(sem("consts_loaded"), 16)
            pool.dma_start(xres[:, :, :], dram["x"].rearrange("(t p) n -> p t n", p=P)).then_inc(sem("x_loaded"), 16)
            pool.dma_start(mem_sq[:, :, :], dram["mem"].rearrange("(t p) n -> p t n", p=P)).then_inc(sem("mem_loaded"), 16)
            root_of("x")
            pool.wait_ge(sem("derived"), 1)
            with pool.Fori(0, KG // 2) as i:
                for h in range(2):
                    pool.wait_ge(sem(f"rnn_lo{h}"), START + i)
                    j4 = (2 * i + h) * NB
                    nc.gpsimd.tensor_copy(pj[h][:, 0:CB + 1, :], params[:, 0:CB + 1, bass.ds(j4, NB)])
                    for row, src in ((BA, neg_ba), (BI, half_bi), (LAM, four_sp)):
                        last = nc.gpsimd.tensor_copy(pj[h][:, row, :], src[:, bass.ds(j4, NB)])
                    last.then_inc(sem(f"pj_ready{h}"), 1)
            root_of("mem")
            pool.wait_ge(sem("merged"), KG)
            pool.dma_start(xres[:, :, :], dram["x"].rearrange("(t p) n -> p t n", p=P)).then_inc(sem("xres_loaded"), 16)
            pool.dma_start(memT_in[:, :, :], dram["mem_T"]).then_inc(sem("memT_loaded"), 16)
            pool.dma_start(gain_final[:, :], dram["norm_final_g"].partition_broadcast(P)).then_inc(sem("gain_final_loaded"), 16)
            for name in ("x1", "x2", "x3"):
                root_of(name)

        @block.tensor
        def _(pe):
            for signal in (*w_used, *(sem(f"lru_z{h}") for h in range(2))):
                pe.sem_inc(signal, START)
            def gemm(n, g, i, per_n, per_g, xh, xl, tiles):
                p, before = buf_of(g, i, per_g)
                for c in range(tiles // CK):
                    yield c
                    if c == 0:
                        pe.wait_ge(taken[p], START + before)
                    s, used = slot_of(n + c, i, per_n)
                    pe.wait_ge(w_ready[s], START + used + 1)
                    for k in range(CK):
                        kt = c * CK + k
                        for tt in range(TT):
                            tok = slice(tt * P, (tt + 1) * P)
                            first, end = kt == 0, kt == tiles - 1
                            nc.tensor.matmul(gps[p][:, tt, :], xh[:, kt, tok], whi[:, s, k, :], start=first, stop=False)
                            nc.tensor.matmul(gps[p][:, tt, :], xh[:, kt, tok], wlo[:, s, k, :], start=False, stop=False)
                            last = nc.tensor.matmul(gps[p][:, tt, :], xl[:, kt, tok], whi[:, s, k, :], start=False, stop=end)
                    last.then_inc(w_used[s], 1)

            def transpose(src, dst, done):
                for k in range(NB):
                    for tt in range(TT):
                        last = nc.tensor.transpose(dst[:, k, tt * P:(tt + 1) * P], src[:, tt, k * P:(k + 1) * P], ident)
                last.then_inc(sem(done), 1)

            pe.wait_ge(sem("consts_loaded"), 16)
            with pe.Fori(0, KG // 2) as i:
                for h in range(2):
                    j = 2 * i + h
                    n, g = CH0["rnn_in"] + h * 3 * CG, GR0["rnn_in"] + h * 3
                    for c in gemm(n, g, i, 6 * CG, 6, xhi, xlo, KT):
                        if h == 0 and c % 2 == 0:
                            pe.wait_ge(sem("x_lo"), c // 2 + 1)
                    for c in gemm(n + CG, g + 1, i, 6 * CG, 6, xhi, xlo, KT):
                        if c == 1:
                            wait_taken(pe, g, i, 6)
                            transpose(rtok, side[0], "xr_T")
                        if c == 4:
                            pe.wait_ge(sem(f"lw_full{h}"), 32 * (i + 1))
                            pe.wait_ge(sem("conv_done"), j + 1)
                            for a in range(2):
                                for b in range(NB):
                                    last = nc.tensor.matmul(side[a][:, b, :], lw[h][:, a, b, :], conv[:, b, :], start=True, stop=True)
                            last.then_inc(sem(f"lru_z{h}"), 1)
                    for c in gemm(n + 2 * CG, g + 2, i, 6 * CG, 6, xhi, xlo, KT):
                        if c == 1:
                            wait_taken(pe, g + 1, i, 6)
                            pe.wait_ge(sem("r_exp"), j + 1)
                            transpose(rtok, side[0], "yr_T")
            with pe.Fori(0, KG // 2) as i:
                for h in range(2):
                    for c in gemm(CH0["rnn_out"] + h * CG, GR0["rnn_out"] + h, i, 2 * CG, 2, vhi, vlo, KT):
                        if c == 0 and h == 0:
                            pe.wait_ge(sem("rnn_lo0"), START + KG // 2)
                            pe.wait_ge(sem("rnn_lo1"), START + KG // 2 - 1)
                        if c == 6 and h == 0:
                            pe.wait_ge(sem("rnn_lo1"), START + KG // 2)
            with pe.Fori(0, KG) as j:
                n, g = CH0["attn_in"], GR0["attn_in"]
                for c in gemm(n, g, j, 4 * CG, 4, xhi, xlo, KT):
                    pass
                for c in gemm(n + CG, g + 1, j, 4 * CG, 4, xhi, xlo, KT):
                    if c == 2:
                        pe.wait_ge(sem("k_rot"), j + 1)
                        transpose(ktok, side[0], "k_T_ps")
                for c in gemm(n + 2 * CG, g + 2, j, 4 * CG, 4, xhi, xlo, KT):
                    if c == 2:
                        pe.wait_ge(sem("q_rot"), j + 1)
                        transpose(qtok, side[1], "q_T_ps")
                    if c == 3:
                        pe.wait_ge(sem("k_T"), j + 1)
                        pe.wait_ge(sem("q_T"), j + 1)
                        s0 = side[0][:, 0:2, :].rearrange("p a (b k) -> p (a b) k", b=2)
                        for b in range(NB):
                            nc.tensor.matmul(s0[:, b, :], qT[:, b, 0:P], kT[:, b, 0:P], start=True, stop=True)
                        for b in range(NB):
                            last = nc.tensor.matmul(side[1][:, b, :], qT[:, b, P:2 * P], kT[:, b, :], start=True, stop=True)
                        last.then_inc(sem("scores"), 1)
                for c in gemm(n + 3 * CG, g + 3, j, 4 * CG, 4, xhi, xlo, KT):
                    if c == 2:
                        pe.wait_ge(sem("prob"), j + 1)
                        pt1 = side[1][:, 0:2, :].rearrange("p a (b k) -> p (a b) k", b=2)
                        for b in range(NB):
                            nc.tensor.transpose(side[0][:, b, 0:P], prob[:, b, 0:P], ident)
                            nc.tensor.transpose(side[0][:, b, P:2 * P], prob[:, b, P:2 * P], ident)
                            last = nc.tensor.transpose(pt1[:, b, :], prob[:, b, 2 * P:3 * P], ident)
                        last.then_inc(sem("prob_T_ps"), 1)
                    if c == 4:
                        pe.wait_ge(sem("prob_T"), j + 1)
                        wait_taken(pe, g + 2, j, 4)
                        for b in range(NB):
                            v0, v1 = vtok[:, 0, b * P:(b + 1) * P], vtok[:, 1, b * P:(b + 1) * P]
                            nc.tensor.matmul(side[0][:, b, :], v0, probT[:, b, 0:2 * P], start=True, stop=False)
                            last = nc.tensor.matmul(side[0][:, b, P:2 * P], v1, probT[:, b, 2 * P:3 * P], start=False, stop=True)
                        last.then_inc(sem("attn_o"), 1)
            def merge_T(j):
                pe.wait_ge(sem("merged"), j + 1)
                transpose(stage[j % 2], side[j % 2], "merged_T")

            def res_T(name, g, j):
                wait_taken(pe, g)
                transpose(xres[:, :, j * GW:(j + 1) * GW], side[j % 2], name + "_T")

            for j in range(KG):
                for c in gemm(CH0["attn_out"] + j * CG, GR0["attn_out"] + j, 0, 0, 0, vhi, vlo, KT):
                    if j == 0 and c in (0, 6):
                        pe.wait_ge(sem("attn_lo"), KG - 1 if c == 0 else KG)
                    if c == 2 and j >= 1:
                        merge_T(j - 1)
            for j in range(KG):
                for c in gemm(CH0["mix"] + j * CG, GR0["mix"] + j, 0, 0, 0, mhi, mlo, KT):
                    if c == 2:
                        if j == 0:
                            merge_T(KG - 1)
                        else:
                            res_T("x1", GR0["mix"] + j - 1, j - 1)
                    if c == 6 and j == 0:
                        pe.wait_ge(sem("merged_lo"), KG)
            n, g = CH0["cross"], GR0["cross"]
            pe.wait_ge(sem("mem_lo"), KG)
            for c in gemm(n, g, 0, 0, 0, vhi, vlo, KT):
                if c == 2:
                    res_T("x1", GR0["mix"] + KG - 1, KG - 1)
            pe.wait_ge(sem("x1_lo"), KG)
            for c in gemm(n + CG, g + 1, 0, 0, 0, xhi, xlo, KT):
                if c == 2:
                    wait_taken(pe, g)
                    transpose(ktok, side[0], "ck_T_ps")
            for c in gemm(n + 2 * CG, g + 2, 0, 0, 0, vhi, vlo, KT):
                if c == 1:
                    wait_taken(pe, g + 1)
                    transpose(qtok, side[1], "cq_T_ps")
                if c == 2:
                    pe.wait_ge(sem("ck_T"), 1)
                    pe.wait_ge(sem("cq_T"), 1)
                    for tt in range(TT):
                        for b in range(NB):
                            last = nc.tensor.matmul(side[tt][:, b, :], qT[:, b, tt * P:(tt + 1) * P], kT[:, b, :], start=True, stop=True)
                    last.then_inc(sem("cscores"), 1)
                if c == 7:
                    pe.wait_ge(sem("cprob"), TT)
                    for m in range(MEM // P):
                        for b in range(NB):
                            for tt in range(TT):
                                last = nc.tensor.transpose(side[m][:, b, tt * P:(tt + 1) * P], cprob[:, tt, b, m * P:(m + 1) * P], ident)
                    last.then_inc(sem("cprob_T_ps"), 1)
            pe.wait_ge(sem("cprob_T"), 1)
            wait_taken(pe, g + 2)
            for b in range(NB):
                nc.tensor.matmul(side[0][:, b, :], vtok[:, 0, b * P:(b + 1) * P], cprobT[:, 0, b, :], start=True, stop=False)
                last = nc.tensor.matmul(side[0][:, b, :], vtok[:, 1, b * P:(b + 1) * P], cprobT[:, 1, b, :], start=False, stop=True)
            last.then_inc(sem("cross_o"), 1)
            pe.wait_ge(sem("cross_lo"), 1)
            for j in range(KG):
                for c in gemm(CH0["cross_out"] + 2 * j, GR0["cross_out"] + j, 0, 0, 0, chi, clo, NB):
                    if c == 1 and j >= 1:
                        res_T("x2", GR0["cross_out"] + j - 1, j - 1)

            def inner_T():
                transpose(stage[0], side[0], "inner_T")

            for part, groups in (("a", FA), ("b", FB)):
                n, g = CH0["up_" + part], GR0["up_" + part]

                def pair(j, tail):
                    for c in gemm(n, g, j, 2 * CG, 2, xhi, xlo, KT):
                        if c == 2:
                            tail()
                        if c == 4 and part == "a" and isinstance(j, int):
                            pe.wait_ge(sem("x2_lo"), KG)
                    for c in gemm(n + CG, g + 1, j, 2 * CG, 2, xhi, xlo, KT):
                        pass

                def tail_first():
                    if part == "a":
                        res_T("x2", GR0["cross_out"] + KG - 1, KG - 1)

                done = 0 if part == "a" else FA

                def tail_inner(j):
                    wait_taken(pe, g - 1, j, 2)
                    inner_T()

                if part == "a":
                    pe.wait_ge(sem("x2_lo"), 2)
                pair(0, tail_first)
                with pe.Fori(1, groups) as j:
                    pair(j, lambda: tail_inner(j))
                nd, gd = CH0["down_" + part], GR0["down_" + part]

                def down(i, h, first):
                    for c in gemm(nd + h * groups * 2, gd + h, i, groups * 4, 2, inner_hi, inner_lo, groups * NB):
                        if first and c == 2:
                            tail_inner(groups)
                        if first and c == 6:
                            pe.wait_ge(sem("inner_lo"), done + groups)
                down(0, 0, True)
                down(0, 1, False)
                for h in range(2):
                    down(1, h, False)

        @block.scalar
        def _(act):
            def splits(n, count, i=0, per=0):
                for c in range(count):
                    m = n + c + LEAD
                    if m < CHUNKS:
                        s, used = slot_of(m, i, per)
                        act.wait_ge(raw_full[s], 16 * (used + 1))
                        act.wait_ge(w_used[s], START + used)
                        nc.scalar.activation(whi[:, s], raw[:, s], ACT.Copy).then_inc(hi_ready[s], 1)
                    yield c

            def evac(g, end, i, per_g, per_n, dst, scale, func):
                p, _ = buf_of(g)
                wait_product(act, end, i, per_n)
                for tt in range(TT):
                    last = nc.scalar.activation(dst[tt], gps[p][:, tt, :], func, scale=scale[:, tt:tt + 1])
                last.then_inc(taken[p], 1)

            def toks(x):
                return [x[:, tt, :] for tt in range(TT)]

            def copy(dst, src, ready, value, done):
                act.wait_ge(sem(ready), value)
                nc.scalar.activation(dst, src, ACT.Copy).then_inc(sem(done), 1)

            def gained_hi(src, gain, dst_hi, j, ready, value, done):
                act.wait_ge(sem(ready), value)
                for b in range(NB):
                    kt = j * NB + b
                    last = nc.scalar.activation(dst_hi[:, kt, :], src[:, b, :], ACT.Copy, scale=gains[:, gain, kt:kt + 1])
                last.then_inc(sem(done), 1)

            squared = [0]

            def squares(src, name, j):
                if squared[0]:
                    act.wait_ge(sem("squared"), squared[0])
                for tt in range(TT):
                    last = nc.scalar.activation(junk[:, tt, :], src[:, tt, j * GW:(j + 1) * GW], ACT.Square, accum_out=ss[name][:, tt, j:j + 1])
                last.then_inc(sem("squared"), 1)
                squared[0] += 1

            act.dma_start(table[:, :, :], dram["params"]).then_inc(sem("params_loaded"), 16)
            for q in range(KG):
                act.dma_start(xT_in[:, q * NB:(q + 1) * NB, :], dram["x_T"][:, q * NB:(q + 1) * NB, :]).then_inc(sem(f"xT_loaded{q}"), 16)
            act.dma_start(pos_i[:, :], dram["positions"].rearrange("(t p) -> p t", p=P), allow_slow_non_contiguous=True)\
                .then_inc(sem("pos_loaded"), 16)
            act.wait_ge(sem("params_loaded"), 16)
            gained_hi(xT_in[:, 0:NB, :], 0, xhi, 0, "xT_loaded0", 16, "x_hi")
            for s in range(LEAD):
                act.wait_ge(raw_full[s], 16)
                nc.scalar.activation(whi[:, s], raw[:, s], ACT.Copy).then_inc(hi_ready[s], 1)
            for q in range(1, KG):
                gained_hi(xT_in[:, q * NB:(q + 1) * NB, :], 0, xhi, q, f"xT_loaded{q}", 16, "x_hi")
            act.wait_ge(sem("neg_abs_lam"), 1)
            nc.scalar.activation(sp[:, 1, :], sp[:, 0, :], ACT.Exp).then_inc(sem("exp_lam"), 1)
            act.wait_ge(sem("x_loaded"), 16)
            nc.scalar.activation(square_out["x"][:, :], xres[:, 0, :], ACT.Square, accum_out=ss["x"][:, 0:1]).then_inc(sem("x_square0"), 1)

            with act.Fori(0, KG // 2) as i:
                for h in range(2):
                    j = 2 * i + h
                    n, g = CH0["rnn_in"] + h * 3 * CG, GR0["rnn_in"] + h * 3
                    for c in splits(n, CG, i, 6 * CG):
                        pass
                    for c in splits(n + CG, CG, i, 6 * CG):
                        if c == 0:
                            act.wait_ge(sem("rstd_x"), 1)
                            evac(g, n + CG, i, 6, 6 * CG, toks(rtok), rstd["x"], ACT.Copy)
                        if c == 1:
                            copy(xTp[:, :, 4:], side[0][:, :, :], "xr_T", j + 1, "xr_T_sb")
                            act.wait_ge(sem("xr_T_sb"), j + 1)
                            act.wait_ge(sem(f"pj_ready{h}"), i + 1)
                            for b in range(NB):
                                last = nc.scalar.activation(conv[:, b, :], xTp[:, b, 4:], ACT.Identity, scale=pj[h][:, CW + 3, b:b + 1],
                                                            bias=pj[h][:, CB, b:b + 1])
                            last.then_inc(sem("conv_tap3"), 1)
                        if c == 4:
                            act.wait_ge(sem(f"lru_z{h}"), START + i + 1)
                            for b in range(NB):
                                last = nc.scalar.activation(rgate[:, b, :], side[0][:, b, :], ACT.Exp, scale=-1.0, bias=pj[h][:, BA, b:b + 1])
                            last.then_inc(sem("r_exp"), 1)
                            for b in range(NB):
                                last = nc.scalar.activation(igate[:, b, :], side[1][:, b, :], ACT.Tanh, scale=0.5, bias=pj[h][:, BI, b:b + 1])
                            last.then_inc(sem("i_tanh"), 1)
                        if c == 6:
                            act.wait_ge(sem("r_gate"), j + 1)
                            for b in range(NB):
                                last = nc.scalar.activation(rgate[:, b, :], rgate[:, b, :], ACT.Tanh, scale=pj[h][:, LAM, b:b + 1])
                            last.then_inc(sem("s_tanh"), 1)
                        if c == 7:
                            act.wait_ge(sem("s_tanh"), j + 1)
                            nc.scalar.activation(root[:, :, :], rgate[:, :, :], ACT.Sqrt).then_inc(sem("root"), 1)
                    for c in splits(n + 2 * CG, CG, i, 6 * CG):
                        if c == 0:
                            evac(g + 1, n + 2 * CG, i, 6, 6 * CG, toks(rtok), rstd["x"], ACT.Copy)
                        if c == 1:
                            copy(yT[:, :, :], side[0][:, :, :], "yr_T", j + 1, "y_T")
                            nc.scalar.activation(ysq[:, :, :], side[0][:, :, :], ACT.Square).then_inc(sem("y2"), 1)
                        if c == 3:
                            act.wait_ge(sem("gelu_arg"), j + 1)
                            nc.scalar.activation(gelu[:, :, :], gelu[:, :, :], ACT.Tanh, scale=GELU_C * 0.044715).then_inc(sem("gelu_tanh"), 1)
                        if c == 6:
                            act.wait_ge(sem("rnn_val"), j + 1)
                            nc.scalar.activation(vhi[:, bass.ds(j * NB, NB), :], yT[:, :, :], ACT.Copy, scale=0.5).then_inc(sem("rnn_hi"), 1)
                    evac(g + 2, n + 3 * CG, i, 6, 6 * CG, [gated[:, tt, bass.ds(j * GW, GW)] for tt in range(TT)], hrstd["x"], ACT.Tanh)
            act.wait_ge(sem("mem_loaded"), 16)
            nc.scalar.activation(square_out["mem"][:, :], mem_sq[:, 0, :], ACT.Square, accum_out=ss["mem"][:, 0:1]).then_inc(sem("mem_square0"), 1)
            with act.Fori(0, KG // 2) as i:
                for h in range(2):
                    for c in splits(CH0["rnn_out"] + h * CG, CG, i, 2 * CG):
                        pass
            act.wait_ge(sem("angles"), 1)
            nc.scalar.activation(rope[:, 2], rope[:, 0], ACT.Sin)
            nc.scalar.activation(rope[:, 3], rope[:, 0], ACT.Sin, scale=0.5).then_inc(sem("sines"), 1)
            with act.Fori(0, KG) as j:
                n, g = CH0["attn_in"], GR0["attn_in"]
                for c in splits(n, CG, j, 4 * CG):
                    pass
                for c in splits(n + CG, CG, j, 4 * CG):
                    if c == 0:
                        evac(g, n + CG, j, 4, 4 * CG, toks(ktok), rstd["x"], ACT.Copy)
                    if c == 2:
                        copy(kT[:, :, :], side[0][:, :, :], "k_T_ps", j + 1, "k_T")
                for c in splits(n + 2 * CG, CG, j, 4 * CG):
                    if c == 0:
                        evac(g + 1, n + 2 * CG, j, 4, 4 * CG, toks(qtok), rstd["x"], ACT.Copy)
                    if c == 2:
                        copy(qT[:, :, :], side[1][:, :, :], "q_T_ps", j + 1, "q_T")
                    if c in (6, 7):
                        act.wait_ge(sem("neg_max"), j + 1)
                        for b in range(2 * (c - 6), 2 * (c - 6) + 2):
                            for tt, cols in ((0, slice(0, P)), (1, slice(P, 3 * P))):
                                last = nc.scalar.activation(prob[:, b, cols], prob[:, b, cols], ACT.Exp, scale=ATT_SCALE,
                                                            bias=nmax[:, tt, b:b + 1], accum_out=psum_[:, tt, b:b + 1])
                        if c == 7:
                            last.then_inc(sem("prob_exp"), 1)
                for c in splits(n + 3 * CG, CG, j, 4 * CG):
                    if c == 0:
                        evac(g + 2, n + 3 * CG, j, 4, 4 * CG, toks(vtok), rstd["x"], ACT.Copy)
                    if c == 2:
                        act.wait_ge(sem("prob_T_ps"), j + 1)
                        nc.scalar.activation(probT[:, :, 0:2 * P], side[0][:, :, :], ACT.Copy)
                        nc.scalar.activation(probT[:, :, 2 * P:3 * P], side[1][:, 0:2, :].rearrange("p a (b k) -> p (a b) k", b=2),
                                             ACT.Copy).then_inc(sem("prob_T"), 1)
                    if c == 4:
                        act.wait_ge(sem("attn_o"), j + 1)
                        nc.scalar.activation(vhi[:, bass.ds(j * NB, NB), :], side[0][:, :, :], ACT.Copy).then_inc(sem("attn_hi"), 1)
                evac(g + 3, n + 4 * CG, j, 4, 4 * CG, [sig_attn[:, tt, bass.ds(j * GW, GW)] for tt in range(TT)], hrstd["x"], ACT.Tanh)

            def merge_hi(j):
                act.wait_ge(sem("merged_T"), j + 1)
                nc.scalar.activation(mhi[:, j * NB:(j + 1) * NB, :], side[j % 2][:, :, :], ACT.Copy, scale=0.5).then_inc(sem("merged_hi"), 1)

            for j in range(KG):
                for c in splits(CH0["attn_out"] + j * CG, CG):
                    if c == 2 and j >= 1:
                        merge_hi(j - 1)
            for j in range(KG):
                for c in splits(CH0["mix"] + j * CG, CG):
                    if c == 2:
                        if j == 0:
                            merge_hi(KG - 1)
                        else:
                            gained_hi(side[(j - 1) % 2], 1, xhi, j - 1, "x1_T", j, "x1_hi")
                            squares(xres, "x1", j - 1)
                    if c == 6:
                        gained_hi(memT_in[:, j * NB:(j + 1) * NB, :], 2, vhi, j, "memT_loaded", 16, "mem_hi")
            n, g = CH0["cross"], GR0["cross"]
            for c in splits(n, CG):
                if c == 2:
                    gained_hi(side[1], 1, xhi, KG - 1, "x1_T", KG, "x1_hi")
                    squares(xres, "x1", KG - 1)
            for c in splits(n + CG, CG):
                if c == 0:
                    act.wait_ge(sem("rstd_mem"), 1)
                    evac(g, n + CG, 0, 0, 0, toks(ktok), rstd["mem"], ACT.Copy)
                if c == 2:
                    copy(kT[:, :, :], side[0][:, :, :], "ck_T_ps", 1, "ck_T")
            for c in splits(n + 2 * CG, CG):
                if c == 0:
                    act.wait_ge(sem("rstd_x1"), 1)
                    evac(g + 1, n + 2 * CG, 0, 0, 0, toks(qtok), rstd["x1"], ACT.Copy)
                if c == 1:
                    copy(qT[:, :, :], side[1][:, :, :], "cq_T_ps", 1, "cq_T")
                if c in (3, 4):
                    tt = c - 3
                    act.wait_ge(sem("cneg_max"), tt + 1)
                    for b in range(NB):
                        last = nc.scalar.activation(cprob[:, tt, b, :], side[tt][:, b, :], ACT.Exp, scale=ATT_SCALE,
                                                    bias=nmax[:, tt, b:b + 1], accum_out=psum_[:, tt, b:b + 1])
                    last.then_inc(sem("cprob_exp"), 1)
            act.wait_ge(sem("cprob_T_ps"), 1)
            nc.scalar.activation(cprobT[:, 0], side[0][:, :, :], ACT.Copy)
            nc.scalar.activation(cprobT[:, 1], side[1][:, :, :], ACT.Copy).then_inc(sem("cprob_T"), 1)
            evac(g + 2, n + 3 * CG, 0, 0, 0, toks(vtok), rstd["mem"], ACT.Copy)
            act.wait_ge(sem("cross_o"), 1)
            nc.scalar.activation(chi[:, :, :], side[0][:, :, :], ACT.Copy).then_inc(sem("cross_hi"), 1)
            for j in range(KG):
                for c in splits(CH0["cross_out"] + 2 * j, 2):
                    if c == 1 and j >= 1:
                        gained_hi(side[(j - 1) % 2], 3, xhi, j - 1, "x2_T", j, "x2_hi")
                        squares(xres, "x2", j - 1)
            for part, groups in (("a", FA), ("b", FB)):
                n, g = CH0["up_" + part], GR0["up_" + part]
                done = 0 if part == "a" else FA

                def inner_split(j):
                    act.wait_ge(sem("inner_T"), done + j)
                    nc.scalar.activation(inner_hi[:, bass.ds((j - 1) * NB, NB), :], side[0][:, :, :], ACT.Copy).then_inc(sem("inner_hi"), 1)

                def pair(j, tail):
                    for c in splits(n, CG, j, 2 * CG):
                        if c == 2:
                            tail()
                    for c in splits(n + CG, CG, j, 2 * CG):
                        if c == 0:
                            act.wait_ge(sem("rstd_x2"), 1)
                            p, _ = buf_of(g)
                            wait_product(act, n + CG, j, 2 * CG)
                            for tt in range(TT):
                                nc.scalar.activation(silu[:, tt, :], gps[p][:, tt, :], ACT.Tanh, scale=hrstd["x2"][:, tt:tt + 1])
                            for tt in range(TT):
                                last = nc.scalar.activation(gate_tok[:, tt, :], gps[p][:, tt, :], ACT.Copy, scale=hrstd["x2"][:, tt:tt + 1])
                            last.then_inc(taken[p], 1)

                def tail_first():
                    if part == "a":
                        gained_hi(side[1], 3, xhi, KG - 1, "x2_T", KG, "x2_hi")
                        squares(xres, "x2", KG - 1)
                pair(0, tail_first)
                with act.Fori(1, groups) as j:
                    pair(j, lambda: inner_split(j))
                nd = CH0["down_" + part]
                for q in range(KG):
                    for c in splits(nd + q * groups * 2, groups * 2):
                        if c == 2 and q == 0:
                            inner_split(groups)
                        if c == 1 and q >= 1 and part == "b":
                            wait_taken(act, GR0["down_b"] + q - 1)
                            squares(xres, "x3", q - 1)
            wait_taken(act, GR0["down_b"] + KG - 1)
            squares(xres, "x3", KG - 1)

        @block.vector
        def _(dve):
            V_ = nc.vector
            for signal in (*w_ready, *taken, *(sem(f"rnn_lo{h}") for h in range(2))):
                dve.sem_inc(signal, START)

            def splits(n, count, i=0, per=0):
                for c in range(count):
                    m = n + c + LEAD
                    if m < CHUNKS:
                        s, used = slot_of(m, i, per)
                        dve.wait_ge(hi_ready[s], used + 1)
                        V_.tensor_tensor(wlo[:, s], raw[:, s], whi[:, s].bitcast(F32), ALU.subtract).then_inc(w_ready[s], 1)
                    yield c

            chain = [0]

            def then(inst):
                chain[0] += 1
                inst.then_inc(sem("vector_chain"), 1)
                dve.wait_ge(sem("vector_chain"), chain[0])

            def gained_lo(src, gain, hi, lo, j, name):
                dve.wait_ge(sem(name + "_hi"), j + 1)
                for b in range(NB):
                    kt = j * NB + b
                    last = V_.scalar_tensor_tensor(lo[:, kt, :], src[:, b, :], gains[:, gain, kt:kt + 1], hi[:, kt, :].bitcast(F32), ALU.mult, ALU.subtract)
                last.then_inc(sem(name + "_lo"), 1)

            def variance(name):
                if name in ORDER:
                    dve.wait_ge(sem("squared"), KG * ORDER[name])
                    then(V_.tensor_reduce(var[name][:, :], ss[name][:, :, :], AX, ALU.add))
                    total = var[name]
                else:
                    dve.wait_ge(sem(name + "_square0"), 1)
                    total = ss[name]
                V_.tensor_scalar(var[name][:, :], total[:, :], 1.0 / D, EPS, ALU.mult, ALU.add).then_inc(sem("var_" + name), 1)

            ORDER = {"x1": 1, "x2": 2, "x3": 3}

            def square_tile(name, src):
                then(V_.tensor_tensor_reduce(out=square_out2[name][:, :], in0=src, in1=src, scale=1.0, scalar=0.0, op0=ALU.mult, op1=ALU.add,
                                             accum_out=ss[name][:, 1:2]))

            def half(name):
                dve.wait_ge(sem("rstd_" + name), 1)
                then(V_.tensor_scalar(hrstd[name][:, :], rstd[name][:, :], 0.5, None, ALU.mult))

            def lo_prologue():
                dve.wait_ge(sem("params_loaded"), 16)
                gained_lo(xT_in[:, 0:NB, :], 0, xhi, xlo, 0, "x")
                for s in range(LEAD):
                    dve.wait_ge(hi_ready[s], 1)
                    V_.tensor_tensor(wlo[:, s], raw[:, s], whi[:, s].bitcast(F32), ALU.subtract).then_inc(w_ready[s], 1)
                for q in range(1, KG):
                    gained_lo(xT_in[:, q * NB:(q + 1) * NB, :], 0, xhi, xlo, q, "x")

            V_.memset(xTp[:, :, :], 0.0).then_inc(sem("conv_pad"), 1)
            lo_prologue()
            then(V_.tensor_scalar(sp[:, 1, :], params[:, LAM, :], -1.0, None, ALU.mult))
            V_.tensor_tensor(sp[:, 0, :], params[:, LAM, :], sp[:, 1, :], ALU.min)
            V_.tensor_scalar(sp[:, 2, :], sp[:, 1, :], 0.0, None, ALU.max).then_inc(sem("neg_abs_lam"), 1)
            dve.wait_ge(sem("exp_lam"), 1)
            e, w, w2, acc = sp[:, 1, :], sp[:, 0, :], sp[:, 3, :], four_sp[:, :]
            then(V_.tensor_scalar(w, e, 2.0, None, ALU.add))
            then(V_.reciprocal(w2, w))
            then(V_.tensor_tensor(w, e, w2, ALU.mult))
            then(V_.tensor_tensor(w2, w, w, ALU.mult))
            then(V_.tensor_scalar(acc, w2, 1.0 / 17, 1.0 / 15, ALU.mult, ALU.add))
            for k in (13, 11, 9, 7, 5, 3, 1):
                then(V_.tensor_tensor(acc, acc, w2, ALU.mult))
                then(V_.tensor_scalar(acc, acc, 1.0 / k, None, ALU.add))
            then(V_.tensor_tensor(acc, acc, w, ALU.mult))
            then(V_.scalar_tensor_tensor(acc, acc, 2.0, sp[:, 2, :], ALU.mult, ALU.add))
            then(V_.tensor_scalar(acc, acc, 4.0, None, ALU.mult))
            V_.tensor_scalar(neg_ba[:, :], params[:, BA, :], -1.0, None, ALU.mult)
            V_.tensor_scalar(half_bi[:, :], params[:, BI, :], 0.5, None, ALU.mult).then_inc(sem("derived"), 1)
            dve.wait_ge(sem("x_loaded"), 16)
            square_tile("x", xres[:, 1, :])
            variance("x")
            half("x")

            with dve.Fori(0, KG // 2) as i:
                for h in range(2):
                    j = 2 * i + h
                    n = CH0["rnn_in"] + h * 3 * CG
                    for c in splits(n, CG, i, 6 * CG):
                        pass
                    for c in splits(n + CG, CG, i, 6 * CG):
                        if c == 2:
                            dve.wait_ge(sem("conv_tap3"), j + 1)
                            for tap in (2, 1, 0):
                                if tap < 2:
                                    dve.wait_ge(sem(f"conv_tap{tap + 1}"), j + 1)
                                for b in range(NB):
                                    last = V_.scalar_tensor_tensor(conv[:, b, :], xTp[:, b, 1 + tap:1 + tap + SEQ], pj[h][:, CW + tap, b:b + 1],
                                                                   conv[:, b, :], ALU.mult, ALU.add)
                                last.then_inc(sem(f"conv_tap{tap}" if tap else "conv_done"), 1)
                        if c == 4:
                            dve.wait_ge(sem("r_exp"), j + 1)
                            V_.tensor_scalar(rgate[:, :, :], rgate[:, :, :], 1.0, None, ALU.add).then_inc(sem("r_den"), 1)
                            dve.wait_ge(sem("r_den"), j + 1)
                            V_.reciprocal(rgate[:, :, :], rgate[:, :, :]).then_inc(sem("r_gate"), 1)
                        if c == 5:
                            dve.wait_ge(sem("i_tanh"), j + 1)
                            dve.wait_ge(sem("conv_done"), j + 1)
                            V_.scalar_tensor_tensor(igate[:, :, :], igate[:, :, :], 1.0, conv[:, :, :], ALU.add, ALU.mult).then_inc(sem("ix"), 1)
                    for c in splits(n + 2 * CG, CG, i, 6 * CG):
                        if c == 0:
                            dve.wait_ge(sem("s_tanh"), j + 1)
                            V_.tensor_scalar(den[:, :, :], rgate[:, :, :], 1.0, None, ALU.add).then_inc(sem("s_den"), 1)
                            dve.wait_ge(sem("s_den"), j + 1)
                            V_.reciprocal(den[:, :, :], den[:, :, :]).then_inc(sem("s_rden"), 1)
                        if c == 1:
                            dve.wait_ge(sem("s_rden"), j + 1)
                            dve.wait_ge(sem("ix"), j + 1)
                            V_.tensor_tensor(igate[:, :, :], igate[:, :, :], den[:, :, :], ALU.mult).then_inc(sem("ixd"), 1)
                            dve.wait_ge(sem("root"), j + 1)
                            V_.tensor_scalar(rgate[:, :, :], den[:, :, :], 2.0, -1.0, ALU.mult, ALU.add).then_inc(sem("a"), 1)
                        if c == 2:
                            dve.wait_ge(sem("y_T"), j + 1)
                            dve.wait_ge(sem("y2"), j + 1)
                            V_.scalar_tensor_tensor(gelu[:, :, :], ysq[:, :, :], 1.0 / 0.044715, yT[:, :, :], ALU.add, ALU.mult).then_inc(sem("gelu_arg"), 1)
                        if c == 3:
                            dve.wait_ge(sem("ixd"), j + 1)
                            V_.tensor_tensor(igate[:, :, :], igate[:, :, :], root[:, :, :], ALU.mult).then_inc(sem("u"), 1)
                            dve.wait_ge(sem("u"), j + 1)
                            dve.wait_ge(sem("a"), j + 1)
                            for b in range(NB):
                                last = V_.tensor_tensor_scan(conv[:, b, :], rgate[:, b, :], igate[:, b, :], 0.0, ALU.mult, ALU.add)
                            last.then_inc(sem("scanned"), 1)
                        if c == 5:
                            dve.wait_ge(sem("gelu_tanh"), j + 1)
                            V_.scalar_tensor_tensor(yT[:, :, :], gelu[:, :, :], 1.0, yT[:, :, :], ALU.add, ALU.mult).then_inc(sem("gelu2"), 1)
                            dve.wait_ge(sem("gelu2"), j + 1)
                            dve.wait_ge(sem("scanned"), j + 1)
                            V_.tensor_tensor(yT[:, :, :], yT[:, :, :], conv[:, :, :], ALU.mult).then_inc(sem("rnn_val"), 1)
                        if c == 6:
                            dve.wait_ge(sem("rnn_hi"), j + 1)
                            V_.scalar_tensor_tensor(vlo[:, bass.ds(j * NB, NB), :], yT[:, :, :], 0.5, vhi[:, bass.ds(j * NB, NB), :].bitcast(F32),
                                                    ALU.mult, ALU.subtract).then_inc(sem(f"rnn_lo{h}"), 1)
            dve.wait_ge(sem("mem_loaded"), 16)
            dve.wait_ge(sem("rnn_lo1"), START + KG // 2)
            square_tile("mem", mem_sq[:, 1, :])
            variance("mem")
            dve.wait_ge(sem("pos_loaded"), 16)
            dve.wait_ge(sem("consts_loaded"), 16)
            then(V_.tensor_copy(pos_f[:, :], pos_i[:, :]))
            for tt in range(TT):
                last = V_.tensor_scalar(rope[:, 0, tt, :], inv_freq, pos_f[:, tt:tt + 1], None, ALU.mult)
            then(last)
            then(V_.tensor_scalar(rope[:, 1], rope[:, 0], 1.0 / TWO_PI, MAGIC, ALU.mult, ALU.add))
            then(V_.tensor_scalar(rope[:, 1], rope[:, 1], MAGIC, None, ALU.subtract))
            for part in PI_PARTS:
                then(V_.scalar_tensor_tensor(rope[:, 0], rope[:, 1], -part, rope[:, 0], ALU.mult, ALU.add))
            V_.tensor_scalar(rope[:, 0], rope[:, 0], 3.1415925, -3.1415925, ALU.min, ALU.max).then_inc(sem("angles"), 1)
            with dve.Fori(0, KG // 2) as i:
                for h in range(2):
                    j = 2 * i + h
                    for c in splits(CH0["rnn_out"] + h * CG, CG, i, 2 * CG):
                        pass
                    p, _ = buf_of(GR0["rnn_out"] + h)
                    wait_product(dve, CH0["rnn_out"] + (h + 1) * CG, i, 2 * CG)
                    for g in range(GR0["attn_in"] - KG - 2, GR0["attn_in"] - KG):
                        wait_taken(dve, g)
                    cols = bass.ds(j * GW, GW)
                    last = V_.scalar_tensor_tensor(gated[:, :, cols], gated[:, :, cols], 1.0, gps[p][:, :, :], ALU.add, ALU.mult)
                    last.then_inc(taken[p], 1)
            dve.wait_ge(sem("sines"), 1)
            then(V_.tensor_tensor(rope[:, 4], rope[:, 3], rope[:, 3], ALU.mult))
            for b in range(NB):
                V_.tensor_copy(sin[:, :, b, :], rope[:, 2])
                last = V_.tensor_scalar(cos[:, :, b, :], rope[:, 4], -2.0, 1.0, ALU.mult, ALU.add)
            then(last)

            def rotate(x, what, j):
                v = x[:, :, :].rearrange("p t (b d) -> p t b d", d=P)
                x1, x2 = v[:, :, :, 0:ROT], v[:, :, :, ROT:2 * ROT]
                wait_taken(dve, GR0["attn_in"] + (0 if what == "k" else 1), j, 4)
                V_.tensor_tensor(rt[:, 0], x1, cos[:, :, :, :], ALU.mult)
                V_.tensor_tensor(rt[:, 1], x2, sin[:, :, :, :], ALU.mult)
                V_.tensor_tensor(rt[:, 2], x2, cos[:, :, :, :], ALU.mult)
                V_.tensor_tensor(rt[:, 3], x1, sin[:, :, :, :], ALU.mult).then_inc(sem(what + "_rot_products"), 1)
                dve.wait_ge(sem(what + "_rot_products"), j + 1)
                V_.tensor_tensor(x1, rt[:, 0], rt[:, 1], ALU.subtract)
                V_.tensor_tensor(x2, rt[:, 2], rt[:, 3], ALU.add).then_inc(sem(what + "_rot"), 1)

            with dve.Fori(0, KG) as j:
                n = CH0["attn_in"]
                for c in splits(n, CG, j, 4 * CG):
                    pass
                for c in splits(n + CG, CG, j, 4 * CG):
                    if c == 0:
                        rotate(ktok, "k", j)
                for c in splits(n + 2 * CG, CG, j, 4 * CG):
                    if c == 0:
                        rotate(qtok, "q", j)
                    if c == 3:
                        dve.wait_ge(sem("scores"), j + 1)
                        s0 = side[0][:, 0:2, :].rearrange("p a (b k) -> p (a b) k", b=2)
                        V_.tensor_tensor(prob[:, :, 0:P], s0, mask[:, P:2 * P].unsqueeze(1).to_broadcast([P, NB, P]), ALU.add)
                        V_.tensor_tensor(prob[:, :, P:3 * P], side[1][:, :, :], mask.unsqueeze(1).to_broadcast([P, NB, 2 * P]), ALU.add)\
                            .then_inc(sem("masked"), 1)
                    if c == 5:
                        dve.wait_ge(sem("masked"), j + 1)
                        V_.tensor_reduce(smax[:, 0, :], prob[:, :, 0:P], AX, ALU.max)
                        V_.tensor_reduce(smax[:, 1, :], prob[:, :, P:3 * P], AX, ALU.max).then_inc(sem("smax"), 1)
                        dve.wait_ge(sem("smax"), j + 1)
                        V_.tensor_scalar(nmax[:, :, :], smax[:, :, :], -ATT_SCALE, None, ALU.mult).then_inc(sem("neg_max"), 1)
                for c in splits(n + 3 * CG, CG, j, 4 * CG):
                    if c == 0:
                        dve.wait_ge(sem("prob_exp"), j + 1)
                        V_.reciprocal(rsum[:, :, :], psum_[:, :, :]).then_inc(sem("rsum"), 1)
                        dve.wait_ge(sem("rsum"), j + 1)
                        V_.tensor_tensor(prob[:, :, 0:P], prob[:, :, 0:P], rsum[:, 0, :].unsqueeze(2).to_broadcast([P, NB, P]), ALU.mult)
                        V_.tensor_tensor(prob[:, :, P:3 * P], prob[:, :, P:3 * P], rsum[:, 1, :].unsqueeze(2).to_broadcast([P, NB, 2 * P]), ALU.mult)\
                            .then_inc(sem("prob"), 1)
                    if c == 5:
                        dve.wait_ge(sem("attn_hi"), j + 1)
                        V_.tensor_tensor(vlo[:, bass.ds(j * NB, NB), :], side[0][:, :, :], vhi[:, bass.ds(j * NB, NB), :].bitcast(F32), ALU.subtract)\
                            .then_inc(sem("attn_lo"), 1)

            def merge(j):
                p, before = buf_of(GR0["attn_out"] + j)
                cols = slice(j * GW, (j + 1) * GW)
                wait_product(dve, CH0["attn_out"] + (j + 1) * CG)
                wait_taken(dve, GR0["attn_out"] - 1)
                V_.scalar_tensor_tensor(stage[j % 2][:, :, :], sig_attn[:, :, cols], 1.0, gps[p][:, :, :], ALU.add, ALU.mult).then_inc(taken[p], 1)
                dve.wait_ge(taken[p], START + before + 1)
                V_.tensor_tensor(stage[j % 2][:, :, :], stage[j % 2][:, :, :], gated[:, :, cols], ALU.add).then_inc(sem("merged"), 1)

            def merge_lo(j):
                kts = slice(j * NB, (j + 1) * NB)
                dve.wait_ge(sem("merged_hi"), j + 1)
                V_.scalar_tensor_tensor(mlo[:, kts, :], side[j % 2][:, :, :], 0.5, mhi[:, kts, :].bitcast(F32), ALU.mult, ALU.subtract)\
                    .then_inc(sem("merged_lo"), 1)

            def add_group(g, end, j):
                p, _ = buf_of(g)
                cols = slice(j * GW, (j + 1) * GW)
                wait_product(dve, end)
                V_.tensor_tensor(xres[:, :, cols], xres[:, :, cols], gps[p][:, :, :], ALU.add).then_inc(taken[p], 1)

            for j in range(KG):
                for c in splits(CH0["attn_out"] + j * CG, CG):
                    if c == 3 and j >= 1:
                        merge_lo(j - 1)
                merge(j)
            for j in range(KG):
                for c in splits(CH0["mix"] + j * CG, CG):
                    if c == 3:
                        if j == 0:
                            merge_lo(KG - 1)
                        else:
                            gained_lo(side[(j - 1) % 2], 1, xhi, xlo, j - 1, "x1")
                    if c == 7:
                        gained_lo(memT_in[:, j * NB:(j + 1) * NB, :], 2, vhi, vlo, j, "mem")
                if j == 0:
                    dve.wait_ge(sem("xres_loaded"), 16)
                add_group(GR0["mix"] + j, CH0["mix"] + (j + 1) * CG, j)
            n, g = CH0["cross"], GR0["cross"]
            for c in splits(n, CG):
                if c == 3:
                    gained_lo(side[1], 1, xhi, xlo, KG - 1, "x1")
                if c == 4:
                    variance("x1")
            for c in splits(n + CG, CG):
                pass
            for c in splits(n + 2 * CG, CG):
                if c == 2:
                    dve.wait_ge(sem("cscores"), 1)
                    for tt in range(TT):
                        then(V_.tensor_reduce(smax[:, tt, :], side[tt][:, :, :], AX, ALU.max))
                        V_.tensor_scalar(nmax[:, tt, :], smax[:, tt, :], -ATT_SCALE, None, ALU.mult).then_inc(sem("cneg_max"), 1)
                if c in (4, 5):
                    tt = c - 4
                    dve.wait_ge(sem("cprob_exp"), tt + 1)
                    then(V_.reciprocal(rsum[:, tt, :], psum_[:, tt, :]))
                    V_.tensor_tensor(cprob[:, tt], cprob[:, tt], rsum[:, tt, :].unsqueeze(2).to_broadcast([P, NB, MEM]), ALU.mult)\
                        .then_inc(sem("cprob"), 1)
            dve.wait_ge(sem("cross_hi"), 1)
            V_.tensor_tensor(clo[:, :, :], side[0][:, :, :], chi[:, :, :].bitcast(F32), ALU.subtract).then_inc(sem("cross_lo"), 1)
            for j in range(KG):
                for c in splits(CH0["cross_out"] + 2 * j, 2):
                    if c == 1 and j >= 1:
                        gained_lo(side[(j - 1) % 2], 3, xhi, xlo, j - 1, "x2")
                add_group(GR0["cross_out"] + j, CH0["cross_out"] + 2 * (j + 1), j)
            for part, groups in (("a", FA), ("b", FB)):
                n, g = CH0["up_" + part], GR0["up_" + part]
                done = 0 if part == "a" else FA

                def inner_rest(j):
                    kts = bass.ds((j - 1) * NB, NB)
                    dve.wait_ge(sem("inner_hi"), done + j)
                    V_.tensor_tensor(inner_lo[:, kts, :], side[0][:, :, :], inner_hi[:, kts, :].bitcast(F32), ALU.subtract)\
                        .then_inc(sem("inner_lo"), 1)

                def pair(j, tail):
                    for c in splits(n, CG, j, 2 * CG):
                        if c == 3:
                            tail()
                    for c in splits(n + CG, CG, j, 2 * CG):
                        if c == 2:
                            wait_taken(dve, g, j, 2)
                            V_.scalar_tensor_tensor(silu[:, :, :], silu[:, :, :], 1.0, gate_tok[:, :, :], ALU.add, ALU.mult).then_inc(sem("silu"), 1)
                    p, _ = buf_of(g + 1)
                    wait_product(dve, n + 2 * CG, j, 2 * CG)
                    dve.wait_ge(sem("silu"), done + j + 1)
                    for tt in range(TT):
                        last = V_.scalar_tensor_tensor(stage[0][:, tt, :], gps[p][:, tt, :], rstd["x2"][:, tt:tt + 1], silu[:, tt, :], ALU.mult, ALU.mult)
                    last.then_inc(taken[p], 1)

                def tail_first():
                    if part == "a":
                        gained_lo(side[1], 3, xhi, xlo, KG - 1, "x2")
                        variance("x2")
                        half("x2")
                pair(0, tail_first)
                with dve.Fori(1, groups) as j:
                    pair(j, lambda: inner_rest(j))
                nd, gd = CH0["down_" + part], GR0["down_" + part]
                for q in range(KG):
                    for c in splits(nd + q * groups * 2, groups * 2):
                        if c == 3 and q == 0:
                            inner_rest(groups)
                        if c == 4 and q >= 1 and part == "b":
                            dve.wait_ge(sem("gain_final_loaded"), 16)
                            dve.wait_ge(sem("squared"), 2 * KG + q)
                            V_.tensor_tensor(xres[:, :, (q - 1) * GW:q * GW], xres[:, :, (q - 1) * GW:q * GW],
                                             gain_final[:, (q - 1) * GW:q * GW].unsqueeze(1).to_broadcast([P, TT, GW]), ALU.mult)\
                                .then_inc(sem("gained"), 1)
                    add_group(gd + q, nd + (q + 1) * groups * 2, q)
            variance("x3")
            last_group = slice((KG - 1) * GW, D)
            dve.wait_ge(sem("gained"), KG - 1)
            dve.wait_ge(sem("rstd_x3"), 1)
            for tt in range(TT):
                r = rstd["x3"][:, tt:tt + 1]
                V_.tensor_scalar(xres[:, tt, 0:D // 2], xres[:, tt, 0:D // 2], r, None, ALU.mult).then_inc(sem("out_ready"), 1)
                V_.tensor_scalar(xres[:, tt, D // 2:(KG - 1) * GW], xres[:, tt, D // 2:(KG - 1) * GW], r, None, ALU.mult)
                V_.scalar_tensor_tensor(xres[:, tt, last_group], xres[:, tt, last_group], r, gain_final[:, last_group], ALU.mult, ALU.mult)\
                    .then_inc(sem("out_ready"), 1)


NAMES = ["x", "mem", "positions", "norm_mix_g", "w_in", "conv_w", "conv_b", "lru_w_a", "lru_b_a", "lru_w_i", "lru_b_i",
         "lru_lambda", "w_rnn_proj", "w_attn_proj", "w_mix_out", "norm_xq_g", "norm_mem_g", "w_xq", "w_xkv", "w_xo",
         "norm_ffn_g", "w_ffn_gate", "w_ffn_up", "w_ffn_down", "norm_final_g"]


PARAMS = ["conv_b", "lru_b_a", "lru_b_i", "lru_lambda", "norm_mix_g", "norm_xq_g", "norm_mem_g", "norm_ffn_g"]


def constants():
    c = np.zeros((P, 3 * P + ROT), np.float32)
    c[:, 0:P] = np.eye(P)
    c[:, 2 * P:3 * P] = np.where(np.arange(P)[None, :] > np.arange(P)[:, None], -1e30, 0.0)
    c[:, 3 * P:] = np.power(np.float32(500000.0), -np.arange(ROT, dtype=np.float32) / np.float32(ROT))
    return c


def kernel(**inputs):
    import concourse.bacc as bacc
    from concourse.bass_utils import run_bass_kernel_spmd

    nc = bacc.Bacc("TRN2", target_bir_lowering=False, num_devices=1)
    arrays, tensors = {}, {}
    for name in NAMES:
        a = np.ascontiguousarray(inputs[name])
        if a.shape[0] == 1:
            a = a.reshape(a.shape[1:])
        arrays["in_" + name] = a
    arrays["in_consts"] = constants()
    for name in ("x", "mem"):
        a = arrays["in_" + name]
        arrays[f"in_{name}_T"] = np.ascontiguousarray(a.reshape(a.shape[0], KT, P).transpose(2, 1, 0))
    rows = [arrays["in_conv_w"]] + [arrays["in_" + n].reshape(1, D) for n in PARAMS]
    arrays["in_params"] = np.ascontiguousarray(np.concatenate(rows).reshape(12, KT, P).transpose(2, 0, 1))
    for name in ("conv_w", *PARAMS):
        del arrays["in_" + name]
    for name, a in arrays.items():
        tensors[name[3:]] = nc.dram_tensor(name, a.shape, mybir.dt.from_np(a.dtype), kind="ExternalInput").ap()
    tensors["out"] = nc.dram_tensor("out", (SEQ, D), F32, kind="ExternalOutput").ap()
    build(nc, tensors)
    result = run_bass_kernel_spmd(nc, [arrays], core_ids=[0])
    return result.results[0]["out"].reshape(1, SEQ, D)
```

```python
import numpy as np
import concourse.bass as bass
from concourse import mybir
from contextlib import ExitStack

F32 = mybir.dt.float32
F32R = mybir.dt.float32r
I32 = mybir.dt.int32
ALU = mybir.AluOpType
ACT = mybir.ActivationFunctionType
AX = mybir.AxisListType.X

P = 128
SEQ, D, F, MEM = 256, 2048, 5632, 256
TT = SEQ // P
GW = 512
KG = D // GW
NB = GW // P
KT = D // P
R = 4
LEAD = R
CK = 2
CG = KT // CK
WARM_UP = 8
EPS = 1e-6
ATT_SCALE = float(P) ** -0.5
FA, FB = 6, 5
ROT = 16
IN_COLS = {"xr": 0, "yr": D, "q": 2 * D, "k": 3 * D, "v": 4 * D, "g_rnn": 5 * D, "g_attn": 6 * D}
GELU_C = 0.7978845608028654
TWO_PI = 6.283185307179586
MAGIC = 12582912.0
PI_PARTS = [6.25, 0.03125, 0.0019340515136718750]
PI_PARTS.append(TWO_PI - sum(PI_PARTS))

STAGES = ["rnn_in", "rnn_out", "attn_in", "attn_out", "mix", "cross", "cross_out", "up_a", "down_a", "up_b", "down_b"]
_CH = [3 * KG * CG, KG * CG, 4 * KG * CG, KG * CG, KG * CG, 3 * CG, KG * 2, 2 * FA * CG, KG * FA * 2, 2 * FB * CG, KG * FB * 2]
_GR = [3 * KG, KG, 4 * KG, KG, KG, 3, KG, 2 * FA, KG, 2 * FB, KG]
CH0 = {s: sum(_CH[:i]) for i, s in enumerate(STAGES)}
GR0 = {s: sum(_GR[:i]) for i, s in enumerate(STAGES)}
CHUNKS = sum(_CH)
X_SIGNALS = [0, 1, 2, 3, 4, 6]
OUT_PARTS = [slice(0, GW), slice(GW, D - GW), slice(D - GW, D)]
CW, CB, BA, BI, LAM = 0, 4, 5, 6, 7


def build(nc, dram):
    ctx = ExitStack()
    with ctx:
        sems = {}

        def sem(name):
            if name not in sems:
                sems[name] = ctx.enter_context(nc.semaphore(name))
            return sems[name]

        K1 = 1024
        total = 207 * K1
        ctx.enter_context(nc.sbuf_tensor("arena", [P, total], mybir.dt.uint8))
        arena = nc.sbuf_base - total
        top = [0]

        def region(size):
            top[0] += size
            assert top[0] <= total
            return arena + top[0] - size

        def at(name, offset, shape, dt=F32):
            return nc.alloc_sbuf_tensor_at(name, [P] + shape, dt, offset=offset)

        def new(name, shape, dt=F32):
            size = 4 * int(np.prod(shape))
            return at(name, region((size + 31) // 32 * 32), shape, dt)

        raw = new("w_raw", [R, CK, GW])
        whi = new("w_hi", [R, CK, GW], F32R)
        wlo = new("w_lo", [R, CK, GW], F32R)
        xhi = new("x_hi", [KT, SEQ], F32R)
        xlo = new("x_lo", [KT, SEQ], F32R)
        U, V, G, S = region(32 * K1), region(32 * K1), region(16 * K1), region(16 * K1)
        vhi, vlo = at("v_hi", V, [KT, SEQ], F32R), at("v_lo", V + 16 * K1, [KT, SEQ], F32R)
        inner_hi = at("inner_hi", U, [FA * NB, SEQ], F32R)
        inner_lo = at("inner_lo", V, [FA * NB, SEQ], F32R)
        mhi, mlo = at("merged_hi", U, [KT, SEQ], F32R), at("merged_lo", U + 16 * K1, [KT, SEQ], F32R)
        rtok = at("rnn_tok", U, [TT, GW])
        conv = at("conv_T", U + 4 * K1, [NB, SEQ])
        ysq = at("y_squared", U, [NB, SEQ])
        rgate = at("r_gate", U + 8 * K1, [NB, SEQ])
        igate = at("i_gate", U + 12 * K1, [NB, SEQ])
        decay = at("lru_decay", U + 16 * K1, [NB, SEQ])
        yT = at("y_T", U + 20 * K1, [NB, SEQ])
        gelu = at("gelu_T", U + 24 * K1, [NB, SEQ])
        root = at("lru_root", U + 28 * K1, [NB, SEQ])
        conv_hi, conv_lo = at("conv_hi", U + 8 * K1, [NB, SEQ], F32R), at("conv_lo", U + 12 * K1, [NB, SEQ], F32R)
        lw_hi, lw_lo = at("lru_w_hi", U + 16 * K1, [2, NB, P], F32R), at("lru_w_lo", U + 28 * K1, [2, NB, P], F32R)
        ktok = at("k_tok", U, [TT, GW])
        qtok = at("q_tok", U + 4 * K1, [TT, GW])
        vtok = at("v_tok", U + 8 * K1, [TT, GW])
        kT = at("k_T", U + 12 * K1, [NB, SEQ])
        qT = at("q_T", U + 16 * K1, [NB, SEQ])
        prob = at("prob", U + 20 * K1, [NB, 3 * P])
        probT = at("prob_T", U + 26 * K1, [NB, 3 * P])
        cprob = at("cross_prob", U + 20 * K1, [TT, NB, MEM])
        gated = at("gated_rnn", G, [TT, D])
        xres = at("x_res", G, [TT, D])
        sig_attn = at("sig_attn", S, [TT, D])
        cprobT = at("cross_prob_T", S, [MEM // P, NB, SEQ])
        chi = at("cross_hi", S + 8 * K1, [NB, SEQ], F32R)
        clo = at("cross_lo", S + 12 * K1, [NB, SEQ], F32R)
        gate_tok = at("gate_tok", S, [TT, GW])
        silu = at("silu_tok", S + 4 * K1, [TT, GW])
        STAGE = [region(4 * K1), region(4 * K1)]
        stage = [at(f"stage{n}", STAGE[n], [TT, GW]) for n in range(2)]
        sq_sum, sq_next = at("square_sums_T", STAGE[0], [NB, SEQ]), at("squares_T", STAGE[1], [NB, SEQ])
        LW = region(8 * K1)
        lw = [at("lru_w0", LW, [2, NB, P]), at("lru_w1", LW + 4 * K1, [2, NB, P])]
        gain_final = at("gain_final", LW, [D])
        PAD = region(4 * NB * (4 + SEQ))
        xTp = at("conv_in_T", PAD, [NB, 4 + SEQ])
        junk = at("junk", PAD, [TT, GW])
        consts = new("consts", [P + 2 * P + ROT])
        ident, mask, inv_freq = consts[:, 0:P], consts[:, P:3 * P], consts[:, 3 * P:3 * P + ROT]
        xT_in = at("x_T_in", U + 16 * K1, [KT, SEQ])
        sq_last = at("x_last_squares_T", U + 8 * K1, [NB, SEQ])
        x_gained = at("x_gained_T", U, [NB, SEQ])
        memT_in = at("mem_T_in", S, [KT, MEM])
        table = new("params", [12, KT])
        params, gains = table[:, 0:8], table[:, 8:12]
        half_bi, neg_sp4 = new("half_b_i", [KT]), new("neg_4_softplus", [KT])
        pj = [new("block_params0", [8, NB]), new("block_params1", [8, NB])]
        pos_i, pos_f = new("pos_i", [TT], I32), new("pos_f", [TT])
        rope = new("rope_tmp", [5, TT, ROT])
        cos, sin = new("cos", [TT, NB, ROT]), new("sin", [TT, NB, ROT])
        rt = new("rope_products", [4, TT, NB, ROT])
        sp = new("softplus_tmp", [4, KT])
        pw, ones, warm = new("minus_half", [TT]), new("ones", [1]), new("unused", [1])
        ss = {n: new("ss_" + n, [TT, KG]) for n in ("x1", "x2", "x3")}
        ss.update({n: new("ss_" + n, [TT]) for n in ("x", "mem")})
        var = {n: new("var_" + n, [TT]) for n in ss}
        rstd = {n: new("rstd_" + n, [TT]) for n in ss}
        hrstd = {n: new("hrstd_" + n, [TT]) for n in ss}
        smax, nmax = new("smax", [TT, NB]), new("nmax", [TT, NB])
        psum_, rsum = new("prob_sum", [TT, NB]), new("prob_rsum", [TT, NB])

        gps = [ctx.enter_context(nc.psum_tensor(f"group{p}", [P, TT, GW], F32)) for p in range(2)]
        side = [ctx.enter_context(nc.psum_tensor(f"side{p}", [P, NB, SEQ], F32)) for p in range(2)]

        raw_full = [sem(f"raw_full{s}") for s in range(R)]
        hi_ready = [sem(f"hi_ready{s}") for s in range(R)]
        w_ready = [sem(f"w_ready{s}") for s in range(R)]
        w_used = [sem(f"w_used{s}") for s in range(R)]
        taken = [sem(f"taken{p}") for p in range(2)]

        START = 1

        def slot_of(n, i=0, per=0):
            return n % R, n // R + i * (per // R)

        def buf_of(g, i=0, per=0):
            return g % 2, g // 2 + i * (per // 2)

        def wait_product(engine, end, i=0, per=0):
            s, used = slot_of(end - 1, i, per)
            engine.wait_ge(w_used[s], START + used + 1)

        def wait_taken(engine, g, i=0, per=0):
            p, before = buf_of(g, i, per)
            engine.wait_ge(taken[p], START + before + 1)

        block = ctx.enter_context(nc.Block())

        @block.sync
        def _(sync):
            def load(n, i, per, w, row, col):
                s, before = slot_of(n, i, per)
                sync.wait_ge(w_ready[s], START + before)
                sync.dma_start(raw[:, s], w[row:row + CK * P, bass.ds(col, GW)].rearrange("(k p) n -> p k n", p=P))\
                    .then_inc(raw_full[s], 16)

            def group(n, i, per, w, col, rows_=KT, row0=0):
                for c in range(rows_ // CK):
                    load(n + c, i, per, w, row0 + c * CK * P, col)

            w_in = dram["w_in"]
            with sync.Fori(0, KG // 2) as i:
                for h in range(2):
                    n = CH0["rnn_in"] + h * 3 * CG
                    j = 2 * i + h
                    for m, name in enumerate(("xr", "yr", "g_rnn")):
                        group(n + m * CG, i, 6 * CG, w_in, IN_COLS[name] + j * GW)
                        if name == "xr":
                            sync.wait_ge(sem(f"lru_z{h}"), START + i)
                            for a, gate in enumerate(("lru_w_a", "lru_w_i")):
                                sync.dma_start(lw[h][:, a], dram[gate][bass.ds(j * NB, NB), :, :].rearrange("n k m -> k n m"))\
                                    .then_inc(sem(f"lw_full{h}"), 16)
            with sync.Fori(0, KG // 2) as i:
                for h in range(2):
                    group(CH0["rnn_out"] + h * CG, i, 2 * CG, dram["w_rnn_proj"], (2 * i + h) * GW)
            with sync.Fori(0, KG) as j:
                for m, name in enumerate(("k", "q", "v", "g_attn")):
                    group(CH0["attn_in"] + m * CG, j, 4 * CG, w_in, IN_COLS[name] + j * GW)
            for j in range(KG):
                group(CH0["attn_out"] + j * CG, 0, 0, dram["w_attn_proj"], j * GW)
            for j in range(KG):
                group(CH0["mix"] + j * CG, 0, 0, dram["w_mix_out"], j * GW)
            group(CH0["cross"], 0, 0, dram["w_xkv"], 0)
            group(CH0["cross"] + CG, 0, 0, dram["w_xq"], 0)
            group(CH0["cross"] + 2 * CG, 0, 0, dram["w_xkv"], GW)
            for j in range(KG):
                group(CH0["cross_out"] + 2 * j, 0, 0, dram["w_xo"], j * GW, rows_=NB)
            for part, f0, groups in (("a", 0, FA), ("b", FA, FB)):
                with sync.Fori(0, groups) as j:
                    for m, name in enumerate(("w_ffn_gate", "w_ffn_up")):
                        group(CH0["up_" + part] + m * CG, j, 2 * CG, dram[name], (f0 + j) * GW)
                with sync.Fori(0, KG // 2) as i:
                    for h in range(2):
                        group(CH0["down_" + part] + h * groups * 2, i, groups * 4, dram["w_ffn_down"],
                              (2 * i + h) * GW, rows_=groups * NB, row0=f0 * GW)
            for tt in range(TT):
                for part, cols in enumerate(OUT_PARTS):
                    sync.wait_ge(sem("out_ready"), tt * len(OUT_PARTS) + part + 1)
                    sync.dma_start(dram["out"][tt * P:(tt + 1) * P, cols], xres[:, tt, cols]).then_inc(sem("out_stored"), 16)
            sync.wait_ge(sem("out_stored"), 16 * TT * len(OUT_PARTS))

        @block.gpsimd
        def _(pool):
            G_ = nc.gpsimd
            G_.memset(ones[:, :], 1.0)
            G_.memset(pw[:, :], -0.5).then_inc(sem("pw_set"), 1)
            pool.wait_ge(sem("pw_set"), 1)
            chain = [0]

            def then(inst):
                chain[0] += 1
                inst.then_inc(sem("pool_chain"), 1)
                pool.wait_ge(sem("pool_chain"), chain[0])

            def root_of(name):
                pool.wait_ge(sem("var_" + name), 1)
                G_.tensor_tensor(rstd[name][:, :], var[name][:, :], pw[:, :], ALU.pow).then_inc(sem("rstd_" + name), 1)

            def square(x, j):
                then(G_.tensor_tensor((sq_sum if j == 0 else sq_next)[:, :, :], x, x, ALU.mult))
                if j > 0:
                    then(G_.tensor_tensor(sq_sum[:, :, :], sq_sum[:, :, :], sq_next[:, :, :], ALU.add))

            def add_tiles():
                for half in (NB // 2, NB // 4):
                    then(G_.tensor_tensor(sq_sum[:, 0:half, :], sq_sum[:, 0:half, :], sq_sum[:, half:2 * half, :], ALU.add))

            def rstd_of_mean(name):
                pool.wait_ge(sem(name + "_mean"), 1)
                then(G_.tensor_scalar(var[name][:, :], ss[name][:, :], EPS, None, ALU.add))
                then(G_.tensor_tensor(rstd[name][:, :], var[name][:, :], pw[:, :], ALU.pow))
                G_.tensor_scalar(hrstd[name][:, :], rstd[name][:, :], 0.5, None, ALU.mult).then_inc(sem("rstd_" + name), 1)

            def square_of(j, squares):
                pool.wait_ge(sem(f"xT_loaded{j}"), 16)
                return G_.tensor_tensor(squares[:, :, :], xT_in[:, j * NB:(j + 1) * NB, :], xT_in[:, j * NB:(j + 1) * NB, :], ALU.mult)

            def add_squares(squares):
                then(G_.tensor_tensor(sq_sum[:, :, :], sq_sum[:, :, :], squares[:, :, :], ALU.add))

            square_of(0, sq_sum)
            pool.wait_ge(sem("series_arg"), 1)
            w, w2, acc = sp[:, 0, :], sp[:, 3, :], neg_sp4[:, :]
            then(G_.tensor_scalar(acc, w2, 1.0 / 15, 1.0 / 13, ALU.mult, ALU.add))
            for k in (11, 9, 7, 5, 3, 1):
                then(G_.tensor_tensor(acc, acc, w2, ALU.mult))
                then(G_.tensor_scalar(acc, acc, 1.0 / k, None, ALU.add))
            then(G_.tensor_tensor(acc, acc, w, ALU.mult))
            then(G_.tensor_scalar(acc, acc, -8.0, None, ALU.mult))
            then(G_.tensor_tensor(acc, acc, sp[:, 2, :], ALU.add))

            square_of(1, sq_next)
            pool.wait_ge(sem(f"xT_loaded{KG - 1}"), 16)
            G_.tensor_tensor(x_gained[:, :, :], xT_in[:, KT - NB:KT, :], gains[:, 0, KT - NB:KT].unsqueeze(2).to_broadcast([P, NB, SEQ]), ALU.mult)\
                .then_inc(sem("x_gained"), 1)
            pool.wait_ge(sem("x_gained"), 1)
            add_squares(sq_next)
            then(square_of(2, sq_next))
            add_squares(sq_next)
            pool.wait_ge(sem("x_squared"), 1)
            add_squares(sq_last)
            add_tiles()
            pool.sem_inc(sem("x_squares"), 1)

            def block_params(i, h):
                pool.wait_ge(sem(f"rnn_lo{h}"), START + i)
                j4 = (2 * i + h) * NB
                G_.tensor_copy(pj[h][:, 0:BA + 1, :], params[:, 0:BA + 1, bass.ds(j4, NB)])
                for row, src in ((BI, half_bi), (LAM, neg_sp4)):
                    last = G_.tensor_copy(pj[h][:, row, :], src[:, bass.ds(j4, NB)])
                last.then_inc(sem(f"pj_ready{h}"), 1)

            for h in range(2):
                block_params(0, h)
            rstd_of_mean("x")
            for h in range(2):
                block_params(1, h)
            for j in range(KG):
                cols = slice(j * GW, (j + 1) * GW)
                pool.wait_ge(sem("merged"), j + 1)
                pool.dma_start(xres[:, :, cols], dram["x"][:, cols].rearrange("(t p) n -> p t n", p=P)).then_inc(sem("xres_loaded"), 16)
            pool.dma_start(gain_final[:, :], dram["norm_final_g"].partition_broadcast(P)).then_inc(sem("gain_final_loaded"), 16)
            pool.wait_ge(sem("merged_T"), KG)
            pool.wait_ge(sem("memT_loaded"), 16)
            for j in range(KG):
                square(memT_in[:, j * NB:(j + 1) * NB, :], j)
            add_tiles()
            pool.sem_inc(sem("mem_squares"), 1)
            root_of("x1")
            rstd_of_mean("mem")
            root_of("x2")
            for tt in range(TT):
                pool.wait_ge(sem("var_x3"), tt + 1)
                G_.tensor_tensor(rstd["x3"][:, tt:tt + 1], var["x3"][:, tt:tt + 1], pw[:, 0:1], ALU.pow).then_inc(sem("rstd_x3"), 1)

        @block.tensor
        def _(pe):
            for signal in (*w_used, *(sem(f"lru_z{h}") for h in range(2))):
                pe.sem_inc(signal, START)

            def gemm(n, g, i, per_n, per_g, xh, xl, tiles):
                p, before = buf_of(g, i, per_g)
                for c in range(tiles // CK):
                    yield c
                    if c == 0:
                        pe.wait_ge(taken[p], START + before)
                    s, used = slot_of(n + c, i, per_n)
                    pe.wait_ge(w_ready[s], START + used + 1)
                    for k in range(CK):
                        kt = c * CK + k
                        for tt in range(TT):
                            tok = slice(tt * P, (tt + 1) * P)
                            first, end = kt == 0, kt == tiles - 1
                            nc.tensor.matmul(gps[p][:, tt, :], xh[:, kt, tok], whi[:, s, k, :], start=first, stop=False)
                            nc.tensor.matmul(gps[p][:, tt, :], xh[:, kt, tok], wlo[:, s, k, :], start=False, stop=False)
                            last = nc.tensor.matmul(gps[p][:, tt, :], xl[:, kt, tok], whi[:, s, k, :], start=False, stop=end)
                    last.then_inc(w_used[s], 1)

            def transpose(src, dst, done):
                for k in range(NB):
                    for tt in range(TT):
                        last = nc.tensor.transpose(dst[:, k, tt * P:(tt + 1) * P], src[:, tt, k * P:(k + 1) * P], ident)
                last.then_inc(sem(done), 1)

            def square_sums(name, out):
                pe.wait_ge(sem(name + "_squares"), 1)
                for tt in range(TT):
                    last = nc.tensor.matmul(out[:, tt:tt + 1], sq_sum[:, 0, tt * P:(tt + 1) * P], ones[:, 0:1], start=True, stop=True)
                last.then_inc(sem(name + "_sums"), 1)

            pe.wait_ge(sem("pad_zero"), 1)
            for _ in range(WARM_UP):
                nc.tensor.matmul(side[0][:, 0, :], xTp[:, 0, 0:P], xTp[:, 0, 0:SEQ], start=True, stop=True)
            with pe.Fori(0, KG // 2) as i:
                for h in range(2):
                    j = 2 * i + h
                    n, g = CH0["rnn_in"] + h * 3 * CG, GR0["rnn_in"] + h * 3
                    for c in gemm(n, g, i, 6 * CG, 6, xhi, xlo, KT):
                        if h == 0 and c in X_SIGNALS:
                            pe.wait_ge(sem("x_lo"), X_SIGNALS.index(c) + 1)
                        if h == 0 and c == 7:
                            square_sums("x", side[1][:, 0, :])
                    for c in gemm(n + CG, g + 1, i, 6 * CG, 6, xhi, xlo, KT):
                        if c == 1:
                            pe.wait_ge(sem("consts_loaded"), 16)
                            wait_taken(pe, g, i, 6)
                            transpose(rtok, side[0], "xr_T")
                        if c == 6:
                            pe.wait_ge(sem("lw_lo"), j + 1)
                            pe.wait_ge(sem("conv_lo"), j + 1)
                            for a in range(2):
                                for b in range(NB):
                                    nc.tensor.matmul(side[a][:, b, :], lw_hi[:, a, b, :], conv_hi[:, b, :], start=True, stop=False)
                                    nc.tensor.matmul(side[a][:, b, :], lw_hi[:, a, b, :], conv_lo[:, b, :], start=False, stop=False)
                                    last = nc.tensor.matmul(side[a][:, b, :], lw_lo[:, a, b, :], conv_hi[:, b, :], start=False, stop=True)
                            last.then_inc(sem(f"lru_z{h}"), 1)
                    for c in gemm(n + 2 * CG, g + 2, i, 6 * CG, 6, xhi, xlo, KT):
                        if c == 2:
                            wait_taken(pe, g + 1, i, 6)
                            pe.wait_ge(sem("r_z"), j + 1)
                            transpose(rtok, side[0], "yr_T")
            with pe.Fori(0, KG // 2) as i:
                for h in range(2):
                    for c in gemm(CH0["rnn_out"] + h * CG, GR0["rnn_out"] + h, i, 2 * CG, 2, vhi, vlo, KT):
                        if c == 0 and h == 0:
                            pe.wait_ge(sem("rnn_lo0"), START + KG // 2)
                            pe.wait_ge(sem("rnn_lo1"), START + KG // 2 - 1)
                        if c == 6 and h == 0:
                            pe.wait_ge(sem("rnn_lo1"), START + KG // 2)
            with pe.Fori(0, KG) as j:
                n, g = CH0["attn_in"], GR0["attn_in"]
                for c in gemm(n, g, j, 4 * CG, 4, xhi, xlo, KT):
                    pass
                for c in gemm(n + CG, g + 1, j, 4 * CG, 4, xhi, xlo, KT):
                    if c == 2:
                        pe.wait_ge(sem("k_rot"), j + 1)
                        transpose(ktok, side[0], "k_T_ps")
                for c in gemm(n + 2 * CG, g + 2, j, 4 * CG, 4, xhi, xlo, KT):
                    if c == 2:
                        pe.wait_ge(sem("q_rot"), j + 1)
                        transpose(qtok, side[1], "q_T_ps")
                    if c == 3:
                        pe.wait_ge(sem("k_T"), j + 1)
                        pe.wait_ge(sem("q_T"), j + 1)
                        s0 = side[0][:, 0:2, :].rearrange("p a (b k) -> p (a b) k", b=2)
                        for b in range(NB):
                            nc.tensor.matmul(s0[:, b, :], qT[:, b, 0:P], kT[:, b, 0:P], start=True, stop=True)
                        for b in range(NB):
                            last = nc.tensor.matmul(side[1][:, b, :], qT[:, b, P:2 * P], kT[:, b, :], start=True, stop=True)
                        last.then_inc(sem("scores"), 1)
                for c in gemm(n + 3 * CG, g + 3, j, 4 * CG, 4, xhi, xlo, KT):
                    if c == 3:
                        pe.wait_ge(sem("prob"), j + 1)
                        pt1 = side[1][:, 0:2, :].rearrange("p a (b k) -> p (a b) k", b=2)
                        for b in range(NB):
                            nc.tensor.transpose(side[0][:, b, 0:P], prob[:, b, 0:P], ident)
                            nc.tensor.transpose(side[0][:, b, P:2 * P], prob[:, b, P:2 * P], ident)
                            last = nc.tensor.transpose(pt1[:, b, :], prob[:, b, 2 * P:3 * P], ident)
                        last.then_inc(sem("prob_T_ps"), 1)
                    if c == 5:
                        pe.wait_ge(sem("prob_T"), j + 1)
                        wait_taken(pe, g + 2, j, 4)
                        for b in range(NB):
                            v0, v1 = vtok[:, 0, b * P:(b + 1) * P], vtok[:, 1, b * P:(b + 1) * P]
                            nc.tensor.matmul(side[0][:, b, :], v0, probT[:, b, 0:2 * P], start=True, stop=False)
                            last = nc.tensor.matmul(side[0][:, b, P:2 * P], v1, probT[:, b, 2 * P:3 * P], start=False, stop=True)
                        last.then_inc(sem("attn_o"), 1)
            def merge_T(j):
                pe.wait_ge(sem("merged"), j + 1)
                transpose(stage[j % 2], side[j % 2], "merged_T")

            def res_T(name, g, j):
                wait_taken(pe, g)
                transpose(xres[:, :, j * GW:(j + 1) * GW], side[j % 2], name + "_T")

            for j in range(KG):
                for c in gemm(CH0["attn_out"] + j * CG, GR0["attn_out"] + j, 0, 0, 0, vhi, vlo, KT):
                    if j == 0 and c in (0, 6):
                        pe.wait_ge(sem("attn_lo"), KG - 1 if c == 0 else KG)
                    if c == 2 and j >= 1:
                        merge_T(j - 1)
            for j in range(KG):
                for c in gemm(CH0["mix"] + j * CG, GR0["mix"] + j, 0, 0, 0, mhi, mlo, KT):
                    if c == 2:
                        if j == 0:
                            merge_T(KG - 1)
                        else:
                            res_T("x1", GR0["mix"] + j - 1, j - 1)
                    if c == 6 and j == 0:
                        pe.wait_ge(sem("merged_lo"), KG)
            n, g = CH0["cross"], GR0["cross"]
            pe.wait_ge(sem("mem_lo"), KG - 1)
            for c in gemm(n, g, 0, 0, 0, vhi, vlo, KT):
                if c == 6:
                    pe.wait_ge(sem("mem_lo"), KG)
                if c == 2:
                    res_T("x1", GR0["mix"] + KG - 1, KG - 1)
                if c == 5:
                    pe.wait_ge(sem("x1_lo"), KG - 1)
                    square_sums("mem", side[0][:, 0, :])
            pe.wait_ge(sem("x1_lo"), KG)
            for c in gemm(n + CG, g + 1, 0, 0, 0, xhi, xlo, KT):
                if c == 2:
                    wait_taken(pe, g)
                    transpose(ktok, side[0], "ck_T_ps")
            for c in gemm(n + 2 * CG, g + 2, 0, 0, 0, vhi, vlo, KT):
                if c == 1:
                    wait_taken(pe, g + 1)
                    transpose(qtok, side[1], "cq_T_ps")
                if c == 2:
                    pe.wait_ge(sem("ck_T"), 1)
                    pe.wait_ge(sem("cq_T"), 1)
                    for tt in range(TT):
                        for b in range(NB):
                            last = nc.tensor.matmul(side[tt][:, b, :], qT[:, b, tt * P:(tt + 1) * P], kT[:, b, :], start=True, stop=True)
                    last.then_inc(sem("cscores"), 1)
                if c == 7:
                    pe.wait_ge(sem("cprob"), TT)
                    for m in range(MEM // P):
                        for b in range(NB):
                            for tt in range(TT):
                                last = nc.tensor.transpose(side[m][:, b, tt * P:(tt + 1) * P], cprob[:, tt, b, m * P:(m + 1) * P], ident)
                    last.then_inc(sem("cprob_T_ps"), 1)
            pe.wait_ge(sem("cprob_T0"), 1)
            pe.wait_ge(sem("cprob_T1"), 1)
            for half in range(2):
                pe.wait_ge(sem("cv0"), half + 1)
                pe.wait_ge(sem("cv1"), half + 1)
                for b in (2 * half, 2 * half + 1):
                    for m in range(MEM // P):
                        last = nc.tensor.matmul(side[half][:, b, :], vtok[:, m, b * P:(b + 1) * P], cprobT[:, m, b, :], start=m == 0, stop=m == 1)
                last.then_inc(sem("cross_o"), 1)
            for j in range(KG):
                for c in gemm(CH0["cross_out"] + 2 * j, GR0["cross_out"] + j, 0, 0, 0, chi, clo, NB):
                    if j == 0:
                        pe.wait_ge(sem("cross_lo"), c + 1)
                    if c == 1 and j >= 1:
                        res_T("x2", GR0["cross_out"] + j - 1, j - 1)

            def inner_T():
                transpose(stage[0], side[0], "inner_T")

            for part, groups in (("a", FA), ("b", FB)):
                n, g = CH0["up_" + part], GR0["up_" + part]

                def pair(j, tail, first=False):
                    for c in gemm(n, g, j, 2 * CG, 2, xhi, xlo, KT):
                        if c == 2:
                            tail()
                        if c in (4, 6) and part == "a" and first:
                            pe.wait_ge(sem("x2_lo"), KG - 1 if c == 4 else KG)
                    for c in gemm(n + CG, g + 1, j, 2 * CG, 2, xhi, xlo, KT):
                        pass

                def tail_first():
                    if part == "a":
                        res_T("x2", GR0["cross_out"] + KG - 1, KG - 1)

                done = 0 if part == "a" else FA

                def tail_inner(j):
                    wait_taken(pe, g - 1, j, 2)
                    inner_T()

                if part == "a":
                    pe.wait_ge(sem("x2_lo"), 2)
                pair(0, tail_first, first=True)
                with pe.Fori(1, groups) as j:
                    pair(j, lambda: tail_inner(j))
                nd, gd = CH0["down_" + part], GR0["down_" + part]

                def down(i, h, first):
                    for c in gemm(nd + h * groups * 2, gd + h, i, groups * 4, 2, inner_hi, inner_lo, groups * NB):
                        if first and c == 2:
                            tail_inner(groups)
                        if first and c == 6:
                            pe.wait_ge(sem("inner_lo"), done + groups)
                down(0, 0, True)
                down(0, 1, False)
                for h in range(2):
                    down(1, h, False)

        @block.scalar
        def _(act):
            def splits(n, count, i=0, per=0):
                for c in range(count):
                    yield c
                    m = n + c + LEAD
                    if m < CHUNKS:
                        s, used = slot_of(m, i, per)
                        act.wait_ge(raw_full[s], 16 * (used + 1))
                        act.wait_ge(w_used[s], START + used)
                        nc.scalar.activation(whi[:, s], raw[:, s], ACT.Copy).then_inc(hi_ready[s], 1)

            def evac(g, end, i, per_g, per_n, dst, scale, func):
                p, _ = buf_of(g)
                wait_product(act, end, i, per_n)
                for tt in range(TT):
                    last = nc.scalar.activation(dst[tt], gps[p][:, tt, :], func, scale=scale[:, tt:tt + 1])
                last.then_inc(taken[p], 1)

            def toks(x):
                return [x[:, tt, :] for tt in range(TT)]

            def copy(dst, src, ready, value, done):
                act.wait_ge(sem(ready), value)
                nc.scalar.activation(dst, src, ACT.Copy).then_inc(sem(done), 1)

            def gained_hi(src, gain, dst_hi, j, ready, value, done, signal_after=()):
                act.wait_ge(sem(ready), value)
                for b in range(NB):
                    kt = j * NB + b
                    last = nc.scalar.activation(dst_hi[:, kt, :], src[:, b, :], ACT.Copy, scale=gains[:, gain, kt:kt + 1])
                    if b == NB - 1 or b in signal_after:
                        last.then_inc(sem(done), 1)

            def mean_of(name, sums, value=1):
                act.wait_ge(sem(name + "_sums"), value)
                nc.scalar.activation(ss[name][:, :], sums, ACT.Copy, scale=1.0 / D).then_inc(sem(name + "_mean"), 1)

            squared = [0]

            def squares(src, name, j):
                if squared[0]:
                    act.wait_ge(sem("squared"), squared[0])
                for tt in range(TT):
                    last = nc.scalar.activation(junk[:, tt, :], src[:, tt, j * GW:(j + 1) * GW], ACT.Square, accum_out=ss[name][:, tt, j:j + 1])
                last.then_inc(sem("squared"), 1)
                squared[0] += 1

            def load_xT(q):
                act.dma_start(xT_in[:, q * NB:(q + 1) * NB, :], dram["x_T"][:, q * NB:(q + 1) * NB, :]).then_inc(sem(f"xT_loaded{q}"), 16)

            act.dma_start(table[:, :, :], dram["params"]).then_inc(sem("params_loaded"), 16)
            load_xT(0)
            load_xT(1)
            act.wait_ge(sem("pw_set"), 1)
            nc.scalar.activation(warm[:, :], ones[:, :], ACT.Exp)
            act.wait_ge(sem("neg_abs_lam"), 1)
            nc.scalar.activation(sp[:, 1, :], sp[:, 0, :], ACT.Exp).then_inc(sem("exp_lam"), 1)
            load_xT(2)
            load_xT(3)
            act.dma_start(pos_i[:, :], dram["positions"].rearrange("(t p) -> p t", p=P), allow_slow_non_contiguous=True)\
                .then_inc(sem("pos_loaded"), 16)

            def first_hi(s):
                act.wait_ge(raw_full[s], 16)
                nc.scalar.activation(whi[:, s], raw[:, s], ACT.Copy).then_inc(hi_ready[s], 1)

            first_hi(0)
            gained_hi(xT_in[:, 0:NB, :], 0, xhi, 0, "xT_loaded0", 16, "x_hi", signal_after=(CK - 1,))
            first_hi(1)
            act.dma_start(consts[:, :], dram["consts"]).then_inc(sem("consts_loaded"), 16)
            first_hi(2)
            gained_hi(xT_in[:, NB:2 * NB, :], 0, xhi, 1, "xT_loaded1", 16, "x_hi", signal_after=(CK - 1,))
            first_hi(3)
            gained_hi(xT_in[:, 2 * NB:3 * NB, :], 0, xhi, 2, "xT_loaded2", 16, "x_hi")
            act.wait_ge(sem("xT_loaded3"), 16)
            nc.scalar.activation(sq_last[:, :, :], xT_in[:, KT - NB:KT, :], ACT.Square).then_inc(sem("x_squared"), 1)
            copy(xhi[:, KT - NB:KT, :], x_gained[:, :, :], "x_gained", 1, "x_hi")

            with act.Fori(0, KG // 2) as i:
                for h in range(2):
                    j = 2 * i + h
                    n, g = CH0["rnn_in"] + h * 3 * CG, GR0["rnn_in"] + h * 3
                    for c in splits(n, CG, i, 6 * CG):
                        if h == 0 and c == 7:
                            mean_of("x", side[1][:, 0, 0:TT], i + 1)
                    for c in splits(n + CG, CG, i, 6 * CG):
                        if c == 0:
                            act.wait_ge(sem("rstd_x"), 1)
                            evac(g, n + CG, i, 6, 6 * CG, toks(rtok), rstd["x"], ACT.Copy)
                            act.wait_ge(sem(f"lw_full{h}"), 32 * (i + 1))
                            nc.scalar.activation(lw_hi[:, :, :, :], lw[h][:, :, :, :], ACT.Copy).then_inc(sem("lw_hi"), 1)
                        if c == 1:
                            copy(xTp[:, :, 4:], side[0][:, :, :], "xr_T", j + 1, "xr_T_sb")
                            act.wait_ge(sem("xr_T_sb"), j + 1)
                            act.wait_ge(sem(f"pj_ready{h}"), i + 1)
                            for b in range(NB):
                                last = nc.scalar.activation(conv[:, b, :], xTp[:, b, 4:], ACT.Identity, scale=pj[h][:, CW + 3, b:b + 1],
                                                            bias=pj[h][:, CB, b:b + 1])
                            last.then_inc(sem("conv_tap3"), 1)
                        if c == 3:
                            copy(conv_hi[:, :, :], conv[:, :, :], "conv_done", j + 1, "conv_hi")
                        if c == 6:
                            act.wait_ge(sem(f"lru_z{h}"), START + i + 1)
                            for b in range(NB):
                                last = nc.scalar.activation(igate[:, b, :], side[1][:, b, :], ACT.Tanh, scale=0.5, bias=pj[h][:, BI, b:b + 1])
                            last.then_inc(sem("i_tanh"), 1)
                            for b in range(NB):
                                last = nc.scalar.activation(rgate[:, b, :], side[0][:, b, :], ACT.Identity, bias=pj[h][:, BA, b:b + 1])
                            last.then_inc(sem("r_z"), 1)
                        if c == 7:
                            act.wait_ge(sem("r_min"), j + 1)
                            nc.scalar.activation(decay[:, :, :], decay[:, :, :], ACT.Exp).then_inc(sem("r_exp"), 1)
                            nc.scalar.activation(rgate[:, :, :], rgate[:, :, :], ACT.Abs).then_inc(sem("r_abs"), 1)
                            act.wait_ge(sem("r_abs"), j + 1)
                            nc.scalar.activation(rgate[:, :, :], rgate[:, :, :], ACT.Tanh, scale=0.5).then_inc(sem("r_tanh"), 1)
                    for c in splits(n + 2 * CG, CG, i, 6 * CG):
                        if c == 0:
                            evac(g + 1, n + 2 * CG, i, 6, 6 * CG, toks(rtok), rstd["x"], ACT.Copy)
                            act.wait_ge(sem("r_gate"), j + 1)
                            for b in range(NB):
                                last = nc.scalar.activation(decay[:, b, :], rgate[:, b, :], ACT.Exp, scale=pj[h][:, LAM, b:b + 1])
                            last.then_inc(sem("a"), 1)
                            act.wait_ge(sem("a"), j + 1)
                            for b in range(NB):
                                last = nc.scalar.activation(rgate[:, b, :], rgate[:, b, :], ACT.Tanh, scale=pj[h][:, LAM, b:b + 1])
                            last.then_inc(sem("a_tanh"), 1)
                        if c == 2:
                            copy(yT[:, :, :], side[0][:, :, :], "yr_T", j + 1, "y_T")
                            nc.scalar.activation(ysq[:, :, :], side[0][:, :, :], ACT.Square).then_inc(sem("y2"), 1)
                        if c == 3:
                            act.wait_ge(sem("one_less_a2"), j + 1)
                            nc.scalar.activation(root[:, :, :], root[:, :, :], ACT.Sqrt, scale=-0.25).then_inc(sem("root"), 1)
                        if c == 4:
                            act.wait_ge(sem("gelu_arg"), j + 1)
                            nc.scalar.activation(gelu[:, :, :], gelu[:, :, :], ACT.Tanh, scale=GELU_C * 0.044715).then_inc(sem("gelu_tanh"), 1)
                        if c == 6:
                            act.wait_ge(sem("rnn_val"), j + 1)
                            nc.scalar.activation(vhi[:, bass.ds(j * NB, NB), :], yT[:, :, :], ACT.Copy, scale=0.5).then_inc(sem("rnn_hi"), 1)
                        if c == CG - 1:
                            evac(g + 2, n + 3 * CG, i, 6, 6 * CG, [gated[:, tt, bass.ds(j * GW, GW)] for tt in range(TT)], hrstd["x"], ACT.Tanh)
            with act.Fori(0, KG // 2) as i:
                for h in range(2):
                    for c in splits(CH0["rnn_out"] + h * CG, CG, i, 2 * CG):
                        pass
            act.wait_ge(sem("angles"), 1)
            nc.scalar.activation(rope[:, 2], rope[:, 0], ACT.Sin)
            nc.scalar.activation(rope[:, 3], rope[:, 0], ACT.Sin, scale=0.5).then_inc(sem("sines"), 1)
            with act.Fori(0, KG) as j:
                n, g = CH0["attn_in"], GR0["attn_in"]
                for c in splits(n, CG, j, 4 * CG):
                    pass
                for c in splits(n + CG, CG, j, 4 * CG):
                    if c == 0:
                        evac(g, n + CG, j, 4, 4 * CG, toks(ktok), rstd["x"], ACT.Copy)
                    if c == 2:
                        copy(kT[:, :, :], side[0][:, :, :], "k_T_ps", j + 1, "k_T")
                for c in splits(n + 2 * CG, CG, j, 4 * CG):
                    if c == 0:
                        evac(g + 1, n + 2 * CG, j, 4, 4 * CG, toks(qtok), rstd["x"], ACT.Copy)
                    if c == 2:
                        copy(qT[:, :, :], side[1][:, :, :], "q_T_ps", j + 1, "q_T")
                    if c in (6, 7):
                        act.wait_ge(sem("neg_max"), j + 1)
                        for b in range(2 * (c - 6), 2 * (c - 6) + 2):
                            for tt, cols in ((0, slice(0, P)), (1, slice(P, 3 * P))):
                                last = nc.scalar.activation(prob[:, b, cols], prob[:, b, cols], ACT.Exp, scale=ATT_SCALE,
                                                            bias=nmax[:, tt, b:b + 1], accum_out=psum_[:, tt, b:b + 1])
                        if c == 7:
                            last.then_inc(sem("prob_exp"), 1)
                for c in splits(n + 3 * CG, CG, j, 4 * CG):
                    if c == 0:
                        evac(g + 2, n + 3 * CG, j, 4, 4 * CG, toks(vtok), rstd["x"], ACT.Copy)
                    if c == 3:
                        act.wait_ge(sem("prob_T_ps"), j + 1)
                        nc.scalar.activation(probT[:, :, 0:2 * P], side[0][:, :, :], ACT.Copy)
                        nc.scalar.activation(probT[:, :, 2 * P:3 * P], side[1][:, 0:2, :].rearrange("p a (b k) -> p (a b) k", b=2),
                                             ACT.Copy).then_inc(sem("prob_T"), 1)
                    if c == 5:
                        act.wait_ge(sem("attn_o"), j + 1)
                        nc.scalar.activation(vhi[:, bass.ds(j * NB, NB), :], side[0][:, :, :], ACT.Copy).then_inc(sem("attn_hi"), 1)
                    if c == CG - 1:
                        evac(g + 3, n + 4 * CG, j, 4, 4 * CG, [sig_attn[:, tt, bass.ds(j * GW, GW)] for tt in range(TT)], hrstd["x"], ACT.Tanh)

            def merge_hi(j):
                act.wait_ge(sem("merged_T"), j + 1)
                nc.scalar.activation(mhi[:, j * NB:(j + 1) * NB, :], side[j % 2][:, :, :], ACT.Copy, scale=0.5).then_inc(sem("merged_hi"), 1)

            for j in range(KG):
                for c in splits(CH0["attn_out"] + j * CG, CG):
                    if c == 2 and j >= 1:
                        merge_hi(j - 1)
            for j in range(KG):
                for c in splits(CH0["mix"] + j * CG, CG):
                    if c == 2:
                        if j == 0:
                            merge_hi(KG - 1)
                            act.dma_start(memT_in[:, :, :], dram["mem_T"]).then_inc(sem("memT_loaded"), 16)
                        else:
                            gained_hi(side[(j - 1) % 2], 1, xhi, j - 1, "x1_T", j, "x1_hi")
                            squares(xres, "x1", j - 1)
                    if c == 5:
                        gained_hi(memT_in[:, j * NB:(j + 1) * NB, :], 2, vhi, j, "memT_loaded", 16, "mem_hi")
            n, g = CH0["cross"], GR0["cross"]
            for c in splits(n, CG):
                if c == 2:
                    gained_hi(side[1], 1, xhi, KG - 1, "x1_T", KG, "x1_hi")
                    squares(xres, "x1", KG - 1)
                if c == 5:
                    mean_of("mem", side[0][:, 0, 0:TT])
            for c in splits(n + CG, CG):
                if c == 0:
                    act.wait_ge(sem("rstd_mem"), 1)
                    evac(g, n + CG, 0, 0, 0, toks(ktok), rstd["mem"], ACT.Copy)
                if c == 2:
                    copy(kT[:, :, :], side[0][:, :, :], "ck_T_ps", 1, "ck_T")
            for c in splits(n + 2 * CG, CG):
                if c == 0:
                    act.wait_ge(sem("rstd_x1"), 1)
                    evac(g + 1, n + 2 * CG, 0, 0, 0, toks(qtok), rstd["x1"], ACT.Copy)
                if c == 1:
                    copy(qT[:, :, :], side[1][:, :, :], "cq_T_ps", 1, "cq_T")
                if c in (3, 4):
                    tt = c - 3
                    act.wait_ge(sem("cneg_max"), tt + 1)
                    for b in range(NB):
                        last = nc.scalar.activation(cprob[:, tt, b, :], side[tt][:, b, :], ACT.Exp, scale=ATT_SCALE,
                                                    bias=nmax[:, tt, b:b + 1], accum_out=psum_[:, tt, b:b + 1])
                    last.then_inc(sem("cprob_exp"), 1)
                if c == 7:
                    act.wait_ge(sem("cprob_T_ps"), 1)
                    nc.scalar.activation(cprobT[:, 0], side[0][:, :, :], ACT.Copy).then_inc(sem("cprob_T0"), 1)
                    wait_product(act, n + 3 * CG)
                    for half in (slice(0, GW // 2), slice(GW // 2, GW)):
                        nc.scalar.activation(vtok[:, 0, half], gps[buf_of(g + 2)[0]][:, 0, half], ACT.Copy, scale=rstd["mem"][:, 0:1])\
                            .then_inc(sem("cv0"), 1)
                    for half in range(2):
                        two = slice(2 * half, 2 * half + 2)
                        act.wait_ge(sem("cross_o"), half + 1)
                        nc.scalar.activation(chi[:, two, :], side[half][:, two, :], ACT.Copy).then_inc(sem("cross_hi"), 1)
            for j in range(KG):
                for c in splits(CH0["cross_out"] + 2 * j, 2):
                    if c == 1 and j >= 1:
                        gained_hi(side[(j - 1) % 2], 3, xhi, j - 1, "x2_T", j, "x2_hi")
                        squares(xres, "x2", j - 1)
            for part, groups in (("a", FA), ("b", FB)):
                n, g = CH0["up_" + part], GR0["up_" + part]
                done = 0 if part == "a" else FA

                def inner_split(j):
                    act.wait_ge(sem("inner_T"), done + j)
                    nc.scalar.activation(inner_hi[:, bass.ds((j - 1) * NB, NB), :], side[0][:, :, :], ACT.Copy).then_inc(sem("inner_hi"), 1)

                def pair(j, tail):
                    for c in splits(n, CG, j, 2 * CG):
                        if c == 2:
                            tail()
                    for c in splits(n + CG, CG, j, 2 * CG):
                        if c == 0:
                            act.wait_ge(sem("rstd_x2"), 1)
                            p, _ = buf_of(g)
                            wait_product(act, n + CG, j, 2 * CG)
                            for tt in range(TT):
                                nc.scalar.activation(silu[:, tt, :], gps[p][:, tt, :], ACT.Tanh, scale=hrstd["x2"][:, tt:tt + 1])
                            for tt in range(TT):
                                last = nc.scalar.activation(gate_tok[:, tt, :], gps[p][:, tt, :], ACT.Copy, scale=hrstd["x2"][:, tt:tt + 1])
                            last.then_inc(taken[p], 1)

                def tail_first():
                    if part == "a":
                        gained_hi(side[1], 3, xhi, KG - 1, "x2_T", KG, "x2_hi")
                        squares(xres, "x2", KG - 1)
                pair(0, tail_first)
                with act.Fori(1, groups) as j:
                    pair(j, lambda: inner_split(j))
                nd = CH0["down_" + part]
                for q in range(KG):
                    for c in splits(nd + q * groups * 2, groups * 2):
                        if c == 2 and q == 0:
                            inner_split(groups)
                        if c == 1 and q >= 1 and part == "b":
                            wait_taken(act, GR0["down_b"] + q - 1)
                            squares(xres, "x3", q - 1)
            act.wait_ge(sem("squared"), squared[0])
            last_group = slice((KG - 1) * GW, D)
            for tt in range(TT):
                act.wait_ge(sem("last_added"), tt + 1)
                nc.scalar.activation(junk[:, tt, :], xres[:, tt, last_group], ACT.Square, accum_out=ss["x3"][:, tt, KG - 1:KG])\
                    .then_inc(sem("last_squared"), 1)

        @block.vector
        def _(dve):
            V_ = nc.vector
            for signal in (*w_ready, *taken, *(sem(f"rnn_lo{h}") for h in range(2))):
                dve.sem_inc(signal, START)

            def splits(n, count, i=0, per=0):
                for c in range(count):
                    yield c
                    m = n + c + LEAD
                    if m < CHUNKS:
                        s, used = slot_of(m, i, per)
                        dve.wait_ge(hi_ready[s], used + 1)
                        V_.tensor_tensor(wlo[:, s], raw[:, s], whi[:, s].bitcast(F32), ALU.subtract).then_inc(w_ready[s], 1)

            chain = [0]

            def then(inst):
                chain[0] += 1
                inst.then_inc(sem("vector_chain"), 1)
                dve.wait_ge(sem("vector_chain"), chain[0])

            def gained_lo(src, gain, hi, lo, j, name):
                dve.wait_ge(sem(name + "_hi"), j + 1)
                for b in range(NB):
                    kt = j * NB + b
                    last = V_.scalar_tensor_tensor(lo[:, kt, :], src[:, b, :], gains[:, gain, kt:kt + 1], hi[:, kt, :].bitcast(F32), ALU.mult, ALU.subtract)
                last.then_inc(sem(name + "_lo"), 1)

            def variance(name):
                dve.wait_ge(sem("squared"), KG * ORDER[name])
                then(V_.tensor_reduce(var[name][:, :], ss[name][:, :, :], AX, ALU.add))
                V_.tensor_scalar(var[name][:, :], var[name][:, :], 1.0 / D, EPS, ALU.mult, ALU.add).then_inc(sem("var_" + name), 1)

            ORDER = {"x1": 1, "x2": 2, "x3": 3}

            def halve(name):
                dve.wait_ge(sem("rstd_" + name), 1)
                then(V_.tensor_scalar(hrstd[name][:, :], rstd[name][:, :], 0.5, None, ALU.mult))

            def lo_prologue():
                dve.wait_ge(sem("params_loaded"), 16)
                then(V_.tensor_scalar(sp[:, 1, :], params[:, LAM, :], -1.0, None, ALU.mult))
                V_.tensor_scalar(sp[:, 2, :], sp[:, 1, :], 0.0, -4.0, ALU.max, ALU.mult)
                V_.tensor_tensor(sp[:, 0, :], params[:, LAM, :], sp[:, 1, :], ALU.min).then_inc(sem("neg_abs_lam"), 1)
                V_.tensor_scalar(half_bi[:, :], params[:, BI, :], 0.5, None, ALU.mult)
                dve.wait_ge(sem("exp_lam"), 1)
                e, w, w2 = sp[:, 1, :], sp[:, 0, :], sp[:, 3, :]
                then(V_.tensor_scalar(w, e, 2.0, None, ALU.add))
                then(V_.reciprocal(w2, w))
                then(V_.tensor_tensor(w, e, w2, ALU.mult))
                V_.tensor_tensor(w2, w, w, ALU.mult).then_inc(sem("series_arg"), 1)

                def first_lo(s):
                    dve.wait_ge(hi_ready[s], 1)
                    V_.tensor_tensor(wlo[:, s], raw[:, s], whi[:, s].bitcast(F32), ALU.subtract).then_inc(w_ready[s], 1)

                def first_x_lo(kts, count):
                    dve.wait_ge(sem("x_hi"), count)
                    for kt in kts:
                        last = V_.scalar_tensor_tensor(xlo[:, kt, :], xT_in[:, kt, :], gains[:, 0, kt:kt + 1], xhi[:, kt, :].bitcast(F32), ALU.mult, ALU.subtract)
                    last.then_inc(sem("x_lo"), 1)

                first_lo(0)
                first_x_lo(range(CK), 1)
                first_x_lo(range(CK, NB), 2)
                first_lo(1)
                first_lo(2)
                first_x_lo(range(NB, NB + CK), 3)
                first_x_lo(range(NB + CK, 2 * NB), 4)
                first_lo(3)
                first_x_lo(range(2 * NB, 3 * NB), 5)
                dve.wait_ge(sem("x_hi"), 6)
                V_.tensor_tensor(xlo[:, KT - NB:KT, :], x_gained[:, :, :], xhi[:, KT - NB:KT, :].bitcast(F32), ALU.subtract).then_inc(sem("x_lo"), 1)

            V_.memset(xTp[:, :, :], 0.0).then_inc(sem("pad_zero"), 1)
            lo_prologue()
            with dve.Fori(0, KG // 2) as i:
                for h in range(2):
                    j = 2 * i + h
                    n = CH0["rnn_in"] + h * 3 * CG
                    for c in splits(n, CG, i, 6 * CG):
                        pass
                    for c in splits(n + CG, CG, i, 6 * CG):
                        if c == 1:
                            dve.wait_ge(sem("conv_tap3"), j + 1)
                            for tap in (2, 1, 0):
                                if tap < 2:
                                    dve.wait_ge(sem(f"conv_tap{tap + 1}"), j + 1)
                                for b in range(NB):
                                    last = V_.scalar_tensor_tensor(conv[:, b, :], xTp[:, b, 1 + tap:1 + tap + SEQ], pj[h][:, CW + tap, b:b + 1],
                                                                   conv[:, b, :], ALU.mult, ALU.add)
                                last.then_inc(sem(f"conv_tap{tap}" if tap else "conv_done"), 1)
                        if c == 0:
                            dve.wait_ge(sem("lw_hi"), j + 1)
                            V_.tensor_tensor(lw_lo[:, :, :, :], lw[h][:, :, :, :], lw_hi[:, :, :, :].bitcast(F32), ALU.subtract).then_inc(sem("lw_lo"), 1)
                        if c == 3:
                            dve.wait_ge(sem("conv_hi"), j + 1)
                            V_.tensor_tensor(conv_lo[:, :, :], conv[:, :, :], conv_hi[:, :, :].bitcast(F32), ALU.subtract).then_inc(sem("conv_lo"), 1)
                        if c == 6:
                            dve.wait_ge(sem("r_z"), j + 1)
                            V_.tensor_scalar(decay[:, :, :], rgate[:, :, :], 0.0, None, ALU.min).then_inc(sem("r_min"), 1)
                        if c == 7:
                            dve.wait_ge(sem("r_tanh"), j + 1)
                            V_.scalar_tensor_tensor(rgate[:, :, :], rgate[:, :, :], 1.0, decay[:, :, :], ALU.add, ALU.mult).then_inc(sem("r_gate"), 1)
                    for c in splits(n + 2 * CG, CG, i, 6 * CG):
                        if c == 0:
                            dve.wait_ge(sem("i_tanh"), j + 1)
                            dve.wait_ge(sem("conv_done"), j + 1)
                            V_.scalar_tensor_tensor(igate[:, :, :], igate[:, :, :], 1.0, conv[:, :, :], ALU.add, ALU.mult).then_inc(sem("ix"), 1)
                        if c == 1:
                            dve.wait_ge(sem("a"), j + 1)
                            V_.tensor_tensor(root[:, :, :], decay[:, :, :], decay[:, :, :], ALU.mult).then_inc(sem("a2"), 1)
                            dve.wait_ge(sem("a2"), j + 1)
                            dve.wait_ge(sem("a_tanh"), j + 1)
                            V_.scalar_tensor_tensor(root[:, :, :], root[:, :, :], 1.0, rgate[:, :, :], ALU.add, ALU.mult).then_inc(sem("one_less_a2"), 1)
                        if c == 3:
                            dve.wait_ge(sem("y_T"), j + 1)
                            dve.wait_ge(sem("y2"), j + 1)
                            V_.scalar_tensor_tensor(gelu[:, :, :], ysq[:, :, :], 1.0 / 0.044715, yT[:, :, :], ALU.add, ALU.mult).then_inc(sem("gelu_arg"), 1)
                        if c == 4:
                            dve.wait_ge(sem("ix"), j + 1)
                            dve.wait_ge(sem("root"), j + 1)
                            V_.tensor_tensor(igate[:, :, :], igate[:, :, :], root[:, :, :], ALU.mult).then_inc(sem("u"), 1)
                            dve.wait_ge(sem("u"), j + 1)
                            for b in range(NB):
                                last = V_.tensor_tensor_scan(conv[:, b, :], decay[:, b, :], igate[:, b, :], 0.0, ALU.mult, ALU.add)
                            last.then_inc(sem("scanned"), 1)
                        if c == 5:
                            dve.wait_ge(sem("gelu_tanh"), j + 1)
                            V_.scalar_tensor_tensor(yT[:, :, :], gelu[:, :, :], 1.0, yT[:, :, :], ALU.add, ALU.mult).then_inc(sem("gelu2"), 1)
                            dve.wait_ge(sem("gelu2"), j + 1)
                            dve.wait_ge(sem("scanned"), j + 1)
                            V_.tensor_tensor(yT[:, :, :], yT[:, :, :], conv[:, :, :], ALU.mult).then_inc(sem("rnn_val"), 1)
                        if c == 7:
                            dve.wait_ge(sem("rnn_hi"), j + 1)
                            V_.scalar_tensor_tensor(vlo[:, bass.ds(j * NB, NB), :], yT[:, :, :], 0.5, vhi[:, bass.ds(j * NB, NB), :].bitcast(F32),
                                                    ALU.mult, ALU.subtract).then_inc(sem(f"rnn_lo{h}"), 1)
            dve.wait_ge(sem("pos_loaded"), 16)
            dve.wait_ge(sem("consts_loaded"), 16)
            then(V_.tensor_copy(pos_f[:, :], pos_i[:, :]))
            for tt in range(TT):
                last = V_.tensor_scalar(rope[:, 0, tt, :], inv_freq, pos_f[:, tt:tt + 1], None, ALU.mult)
            then(last)
            then(V_.tensor_scalar(rope[:, 1], rope[:, 0], 1.0 / TWO_PI, MAGIC, ALU.mult, ALU.add))
            then(V_.tensor_scalar(rope[:, 1], rope[:, 1], MAGIC, None, ALU.subtract))
            for part in PI_PARTS:
                then(V_.scalar_tensor_tensor(rope[:, 0], rope[:, 1], -part, rope[:, 0], ALU.mult, ALU.add))
            V_.tensor_scalar(rope[:, 0], rope[:, 0], 3.1415925, -3.1415925, ALU.min, ALU.max).then_inc(sem("angles"), 1)
            with dve.Fori(0, KG // 2) as i:
                for h in range(2):
                    j = 2 * i + h
                    for c in splits(CH0["rnn_out"] + h * CG, CG, i, 2 * CG):
                        if c < CG - 1:
                            continue
                        p, _ = buf_of(GR0["rnn_out"] + h)
                        wait_product(dve, CH0["rnn_out"] + (h + 1) * CG, i, 2 * CG)
                        for g in range(GR0["attn_in"] - KG - 2, GR0["attn_in"] - KG):
                            wait_taken(dve, g)
                        cols = bass.ds(j * GW, GW)
                        last = V_.scalar_tensor_tensor(gated[:, :, cols], gated[:, :, cols], 1.0, gps[p][:, :, :], ALU.add, ALU.mult)
                        last.then_inc(taken[p], 1)
            dve.wait_ge(sem("sines"), 1)
            then(V_.tensor_tensor(rope[:, 4], rope[:, 3], rope[:, 3], ALU.mult))
            for b in range(NB):
                V_.tensor_copy(sin[:, :, b, :], rope[:, 2])
                last = V_.tensor_scalar(cos[:, :, b, :], rope[:, 4], -2.0, 1.0, ALU.mult, ALU.add)
            then(last)

            def rotate(x, what, j):
                v = x[:, :, :].rearrange("p t (b d) -> p t b d", d=P)
                x1, x2 = v[:, :, :, 0:ROT], v[:, :, :, ROT:2 * ROT]
                wait_taken(dve, GR0["attn_in"] + (0 if what == "k" else 1), j, 4)
                V_.tensor_tensor(rt[:, 0], x1, cos[:, :, :, :], ALU.mult)
                V_.tensor_tensor(rt[:, 1], x2, sin[:, :, :, :], ALU.mult)
                V_.tensor_tensor(rt[:, 2], x2, cos[:, :, :, :], ALU.mult)
                V_.tensor_tensor(rt[:, 3], x1, sin[:, :, :, :], ALU.mult).then_inc(sem(what + "_rot_products"), 1)
                dve.wait_ge(sem(what + "_rot_products"), j + 1)
                V_.tensor_tensor(x1, rt[:, 0], rt[:, 1], ALU.subtract)
                V_.tensor_tensor(x2, rt[:, 2], rt[:, 3], ALU.add).then_inc(sem(what + "_rot"), 1)

            with dve.Fori(0, KG) as j:
                n = CH0["attn_in"]
                for c in splits(n, CG, j, 4 * CG):
                    pass
                for c in splits(n + CG, CG, j, 4 * CG):
                    if c == 0:
                        rotate(ktok, "k", j)
                for c in splits(n + 2 * CG, CG, j, 4 * CG):
                    if c == 0:
                        rotate(qtok, "q", j)
                    if c == 3:
                        dve.wait_ge(sem("scores"), j + 1)
                        s0 = side[0][:, 0:2, :].rearrange("p a (b k) -> p (a b) k", b=2)
                        V_.tensor_tensor(prob[:, :, 0:P], s0, mask[:, P:2 * P].unsqueeze(1).to_broadcast([P, NB, P]), ALU.add)
                        V_.tensor_tensor(prob[:, :, P:3 * P], side[1][:, :, :], mask.unsqueeze(1).to_broadcast([P, NB, 2 * P]), ALU.add)\
                            .then_inc(sem("masked"), 1)
                    if c == 5:
                        dve.wait_ge(sem("masked"), j + 1)
                        V_.tensor_reduce(smax[:, 0, :], prob[:, :, 0:P], AX, ALU.max)
                        V_.tensor_reduce(smax[:, 1, :], prob[:, :, P:3 * P], AX, ALU.max).then_inc(sem("smax"), 1)
                        dve.wait_ge(sem("smax"), j + 1)
                        V_.tensor_scalar(nmax[:, :, :], smax[:, :, :], -ATT_SCALE, None, ALU.mult).then_inc(sem("neg_max"), 1)
                for c in splits(n + 3 * CG, CG, j, 4 * CG):
                    if c == 0:
                        dve.wait_ge(sem("prob_exp"), j + 1)
                        V_.reciprocal(rsum[:, :, :], psum_[:, :, :]).then_inc(sem("rsum"), 1)
                        dve.wait_ge(sem("rsum"), j + 1)
                        V_.tensor_tensor(prob[:, :, 0:P], prob[:, :, 0:P], rsum[:, 0, :].unsqueeze(2).to_broadcast([P, NB, P]), ALU.mult)
                        V_.tensor_tensor(prob[:, :, P:3 * P], prob[:, :, P:3 * P], rsum[:, 1, :].unsqueeze(2).to_broadcast([P, NB, 2 * P]), ALU.mult)\
                            .then_inc(sem("prob"), 1)
                    if c == 6:
                        dve.wait_ge(sem("attn_hi"), j + 1)
                        V_.tensor_tensor(vlo[:, bass.ds(j * NB, NB), :], side[0][:, :, :], vhi[:, bass.ds(j * NB, NB), :].bitcast(F32), ALU.subtract)\
                            .then_inc(sem("attn_lo"), 1)

            def merge(j):
                p, before = buf_of(GR0["attn_out"] + j)
                cols = slice(j * GW, (j + 1) * GW)
                wait_product(dve, CH0["attn_out"] + (j + 1) * CG)
                wait_taken(dve, GR0["attn_out"] - 1)
                V_.scalar_tensor_tensor(stage[j % 2][:, :, :], sig_attn[:, :, cols], 1.0, gps[p][:, :, :], ALU.add, ALU.mult).then_inc(taken[p], 1)
                dve.wait_ge(taken[p], START + before + 1)
                V_.tensor_tensor(stage[j % 2][:, :, :], stage[j % 2][:, :, :], gated[:, :, cols], ALU.add).then_inc(sem("merged"), 1)

            def merge_lo(j):
                kts = slice(j * NB, (j + 1) * NB)
                dve.wait_ge(sem("merged_hi"), j + 1)
                V_.scalar_tensor_tensor(mlo[:, kts, :], side[j % 2][:, :, :], 0.5, mhi[:, kts, :].bitcast(F32), ALU.mult, ALU.subtract)\
                    .then_inc(sem("merged_lo"), 1)

            def add_group(g, end, j):
                p, _ = buf_of(g)
                cols = slice(j * GW, (j + 1) * GW)
                wait_product(dve, end)
                V_.tensor_tensor(xres[:, :, cols], xres[:, :, cols], gps[p][:, :, :], ALU.add).then_inc(taken[p], 1)

            for j in range(KG):
                for c in splits(CH0["attn_out"] + j * CG, CG):
                    if c == 3 and j >= 1:
                        merge_lo(j - 1)
                    if c == CG - 1:
                        merge(j)
            for j in range(KG):
                for c in splits(CH0["mix"] + j * CG, CG):
                    if c == 3:
                        if j == 0:
                            merge_lo(KG - 1)
                        else:
                            gained_lo(side[(j - 1) % 2], 1, xhi, xlo, j - 1, "x1")
                    if c == 6:
                        gained_lo(memT_in[:, j * NB:(j + 1) * NB, :], 2, vhi, vlo, j, "mem")
                    if c == CG - 1:
                        if j == 0:
                            dve.wait_ge(sem("xres_loaded"), 16 * KG)
                        add_group(GR0["mix"] + j, CH0["mix"] + (j + 1) * CG, j)
            n, g = CH0["cross"], GR0["cross"]
            for c in splits(n, CG):
                if c == 3:
                    gained_lo(side[1], 1, xhi, xlo, KG - 1, "x1")
                if c == 4:
                    variance("x1")
            for c in splits(n + CG, CG):
                pass
            for c in splits(n + 2 * CG, CG):
                if c == 2:
                    dve.wait_ge(sem("cscores"), 1)
                    for tt in range(TT):
                        then(V_.tensor_reduce(smax[:, tt, :], side[tt][:, :, :], AX, ALU.max))
                        V_.tensor_scalar(nmax[:, tt, :], smax[:, tt, :], -ATT_SCALE, None, ALU.mult).then_inc(sem("cneg_max"), 1)
                if c in (4, 5):
                    tt = c - 4
                    dve.wait_ge(sem("cprob_exp"), tt + 1)
                    then(V_.reciprocal(rsum[:, tt, :], psum_[:, tt, :]))
                    V_.tensor_tensor(cprob[:, tt], cprob[:, tt], rsum[:, tt, :].unsqueeze(2).to_broadcast([P, NB, MEM]), ALU.mult)\
                        .then_inc(sem("cprob"), 1)
                if c == 7:
                    dve.wait_ge(sem("cprob_T_ps"), 1)
                    V_.tensor_copy(cprobT[:, 1], side[1][:, :, :]).then_inc(sem("cprob_T1"), 1)
                    wait_product(dve, n + 3 * CG)
                    p, _ = buf_of(g + 2)
                    for half in (slice(0, GW // 2), slice(GW // 2, GW)):
                        V_.tensor_scalar(vtok[:, 1, half], gps[p][:, 1, half], rstd["mem"][:, 1:2], None, ALU.mult).then_inc(sem("cv1"), 1)
                    dve.wait_ge(sem("cv0"), 2)
                    dve.sem_inc(taken[p], 1)
                    for half in range(2):
                        two = slice(2 * half, 2 * half + 2)
                        dve.wait_ge(sem("cross_hi"), half + 1)
                        V_.tensor_tensor(clo[:, two, :], side[half][:, two, :], chi[:, two, :].bitcast(F32), ALU.subtract).then_inc(sem("cross_lo"), 1)
            for j in range(KG):
                for c in splits(CH0["cross_out"] + 2 * j, 2):
                    if c == 1 and j >= 1:
                        gained_lo(side[(j - 1) % 2], 3, xhi, xlo, j - 1, "x2")
                    if c == 1:
                        add_group(GR0["cross_out"] + j, CH0["cross_out"] + 2 * (j + 1), j)
            for part, groups in (("a", FA), ("b", FB)):
                n, g = CH0["up_" + part], GR0["up_" + part]
                done = 0 if part == "a" else FA

                def inner_rest(j):
                    kts = bass.ds((j - 1) * NB, NB)
                    dve.wait_ge(sem("inner_hi"), done + j)
                    V_.tensor_tensor(inner_lo[:, kts, :], side[0][:, :, :], inner_hi[:, kts, :].bitcast(F32), ALU.subtract)\
                        .then_inc(sem("inner_lo"), 1)

                def pair(j, tail):
                    for c in splits(n, CG, j, 2 * CG):
                        if c == 3:
                            tail()
                    for c in splits(n + CG, CG, j, 2 * CG):
                        if c == 2:
                            wait_taken(dve, g, j, 2)
                            V_.scalar_tensor_tensor(silu[:, :, :], silu[:, :, :], 1.0, gate_tok[:, :, :], ALU.add, ALU.mult).then_inc(sem("silu"), 1)
                        if c == CG - 1:
                            p, _ = buf_of(g + 1)
                            wait_product(dve, n + 2 * CG, j, 2 * CG)
                            dve.wait_ge(sem("silu"), done + j + 1)
                            for tt in range(TT):
                                last = V_.scalar_tensor_tensor(stage[0][:, tt, :], gps[p][:, tt, :], rstd["x2"][:, tt:tt + 1], silu[:, tt, :], ALU.mult, ALU.mult)
                            last.then_inc(taken[p], 1)

                def tail_first():
                    if part == "a":
                        gained_lo(side[1], 3, xhi, xlo, KG - 1, "x2")
                        variance("x2")
                        halve("x2")
                pair(0, tail_first)
                with dve.Fori(1, groups) as j:
                    pair(j, lambda: inner_rest(j))
                nd, gd = CH0["down_" + part], GR0["down_" + part]
                for q in range(KG):
                    for c in splits(nd + q * groups * 2, groups * 2):
                        if c == 3 and q == 0:
                            inner_rest(groups)
                        if c == 4 and q >= 1 and part == "b":
                            dve.wait_ge(sem("gain_final_loaded"), 16)
                            dve.wait_ge(sem("squared"), 2 * KG + q)
                            V_.tensor_tensor(xres[:, :, (q - 1) * GW:q * GW], xres[:, :, (q - 1) * GW:q * GW],
                                             gain_final[:, (q - 1) * GW:q * GW].unsqueeze(1).to_broadcast([P, TT, GW]), ALU.mult)\
                                .then_inc(sem("gained"), 1)
                        if c == groups * 2 - 1 and (part == "a" or q < KG - 1):
                            add_group(gd + q, nd + (q + 1) * groups * 2, q)
            last_group = slice((KG - 1) * GW, D)
            p, _ = buf_of(GR0["down_b"] + KG - 1)
            wait_product(dve, CHUNKS)
            for tt in range(TT):
                V_.tensor_tensor(xres[:, tt, last_group], xres[:, tt, last_group], gps[p][:, tt, :], ALU.add).then_inc(sem("last_added"), 1)
            dve.wait_ge(sem("squared"), 3 * KG - 1)
            for tt in range(TT):
                dve.wait_ge(sem("last_squared"), tt + 1)
                then(V_.tensor_reduce(var["x3"][:, tt:tt + 1], ss["x3"][:, tt, :], AX, ALU.add))
                V_.tensor_scalar(var["x3"][:, tt:tt + 1], var["x3"][:, tt:tt + 1], 1.0 / D, EPS, ALU.mult, ALU.add).then_inc(sem("var_x3"), 1)
            dve.wait_ge(sem("gained"), KG - 1)
            dve.wait_ge(sem("last_added"), TT)
            for tt in range(TT):
                dve.wait_ge(sem("rstd_x3"), tt + 1)
                r = rstd["x3"][:, tt:tt + 1]
                for cols in OUT_PARTS:
                    if cols == last_group:
                        last = V_.scalar_tensor_tensor(xres[:, tt, cols], xres[:, tt, cols], r, gain_final[:, cols], ALU.mult, ALU.mult)
                    else:
                        last = V_.tensor_scalar(xres[:, tt, cols], xres[:, tt, cols], r, None, ALU.mult)
                    last.then_inc(sem("out_ready"), 1)


NAMES = ["x", "mem", "positions", "norm_mix_g", "w_in", "conv_w", "conv_b", "lru_w_a", "lru_b_a", "lru_w_i", "lru_b_i",
         "lru_lambda", "w_rnn_proj", "w_attn_proj", "w_mix_out", "norm_xq_g", "norm_mem_g", "w_xq", "w_xkv", "w_xo",
         "norm_ffn_g", "w_ffn_gate", "w_ffn_up", "w_ffn_down", "norm_final_g"]
PARAMS = ["conv_b", "lru_b_a", "lru_b_i", "lru_lambda", "norm_mix_g", "norm_xq_g", "norm_mem_g", "norm_ffn_g"]


def constants():
    c = np.zeros((P, 3 * P + ROT), np.float32)
    c[:, 0:P] = np.eye(P)
    c[:, 2 * P:3 * P] = np.where(np.arange(P)[None, :] > np.arange(P)[:, None], -1e30, 0.0)
    c[:, 3 * P:] = np.power(np.float32(500000.0), -np.arange(ROT, dtype=np.float32) / np.float32(ROT))
    return c


def kernel(**inputs):
    import concourse.bacc as bacc
    from concourse.bass_utils import run_bass_kernel_spmd

    nc = bacc.Bacc("TRN2", target_bir_lowering=False, num_devices=1)
    arrays, tensors = {}, {}
    for name in NAMES:
        a = np.ascontiguousarray(inputs[name])
        if a.shape[0] == 1:
            a = a.reshape(a.shape[1:])
        arrays["in_" + name] = a
    arrays["in_consts"] = constants()
    for name in ("x", "mem"):
        a = arrays["in_" + name]
        arrays[f"in_{name}_T"] = np.ascontiguousarray(a.reshape(a.shape[0], KT, P).transpose(2, 1, 0))
    rows = [arrays["in_conv_w"]] + [arrays["in_" + n].reshape(1, D) for n in PARAMS]
    arrays["in_params"] = np.ascontiguousarray(np.concatenate(rows).reshape(12, KT, P).transpose(2, 0, 1))
    for name in ("conv_w", *PARAMS):
        del arrays["in_" + name]
    for name, a in arrays.items():
        tensors[name[3:]] = nc.dram_tensor(name, a.shape, mybir.dt.from_np(a.dtype), kind="ExternalInput").ap()
    tensors["out"] = nc.dram_tensor("out", (SEQ, D), F32, kind="ExternalOutput").ap()
    build(nc, tensors)
    result = run_bass_kernel_spmd(nc, [arrays], core_ids=[0])
    return result.results[0]["out"].reshape(1, SEQ, D)
```
